# Optimizing a Trainium2 kernel written in Bass

```python
import jax, jax.numpy as jnp
from jax import lax
import numpy as np

D_MODEL = 1024
BATCH = 1
SEQ = 128
DEPTH = 1
DEC_BATCH = 1
DEC_SEQ = 512
PAST_LEN = 256

GRID_W = 64
MLA_HEADS = 8
QK_NOPE = 64
QK_ROPE = 32
V_DIM = 64
Q_RANK = 768
KV_RANK = 256
CONV_CH = 512
CONV_WIDTH = 31
MIX_WIDTH = MLA_HEADS * V_DIM + CONV_CH
IN_COLS = Q_RANK + KV_RANK + QK_ROPE + 2 * CONV_CH
N_EXPERTS = 16
EXPERT_FF = 1024
EC_FACTOR = 2
Q_BLOCK = 128
ROPE_BASE = 10000.0
EPS = 1e-6
N_MOD = 6

kernel_name = "hybrid_mla_conformer_ec_diffusion_step"

def rmsnorm(x, g):
    x32 = x.astype(jnp.float32)
    y = x32 * lax.rsqrt(jnp.mean(x32 * x32, axis=-1, keepdims=True) + EPS)
    return (y * g.astype(jnp.float32)).astype(x.dtype)

def layernorm(x, g, b):
    x32 = x.astype(jnp.float32)
    mu = jnp.mean(x32, axis=-1, keepdims=True)
    var = jnp.mean(jnp.square(x32 - mu), axis=-1, keepdims=True)
    y = (x32 - mu) * lax.rsqrt(var + EPS)
    return (y * g.astype(jnp.float32) + b.astype(jnp.float32)).astype(x.dtype)

def adaln(c, w_mod, b_mod):
    m = jax.nn.silu(c) @ w_mod + b_mod
    return jnp.split(m[:, None, :], N_MOD, axis=-1)

def modulate(x, shift, scale):
    return x * (1 + scale) + shift

def axial_rope_2d(x, n_tokens):
    n_rows = n_tokens // GRID_W
    row = jnp.repeat(jnp.arange(n_rows), GRID_W)
    col = jnp.tile(jnp.arange(GRID_W), n_rows)
    half = QK_ROPE // 2
    inv_freq = 1.0 / (ROPE_BASE ** (jnp.arange(0, half, 2, dtype=jnp.float32) / half))

    def rot(xp, pos):
        ang = pos.astype(jnp.float32)[:, None] * inv_freq[None, :]
        ang = jnp.concatenate([ang, ang], axis=-1)[None, :, None, :]
        cos = jnp.cos(ang).astype(x.dtype)
        sin = jnp.sin(ang).astype(x.dtype)
        x1, x2 = jnp.split(xp, 2, axis=-1)
        return xp * cos + jnp.concatenate([-x2, x1], axis=-1) * sin

    xr, xc = jnp.split(x, 2, axis=-1)
    return jnp.concatenate([rot(xr, row), rot(xc, col)], axis=-1)

def expand_kv(ckv, krope, w_kv_up):
    B, T, _ = ckv.shape
    kv = (ckv @ w_kv_up).reshape(B, T, MLA_HEADS, QK_NOPE + V_DIM)
    k_nope, v = jnp.split(kv, [QK_NOPE], axis=-1)
    k_r = jnp.broadcast_to(krope[:, :, None, :], (B, T, MLA_HEADS, QK_ROPE))
    return jnp.concatenate([k_nope, k_r], axis=-1), v

def mha_blocks(q, k, v):
    B, S, H, Dh = q.shape
    nb = S // Q_BLOCK
    scale = (QK_NOPE + QK_ROPE) ** -0.5
    qb = q.reshape(B, nb, Q_BLOCK, H, Dh).transpose(1, 0, 2, 3, 4)

    def one_block(qi):
        s = jnp.einsum('bqhd,bkhd->bhqk', qi, k).astype(jnp.float32) * scale
        p = jax.nn.softmax(s, axis=-1).astype(v.dtype)
        return jnp.einsum('bhqk,bkhd->bqhd', p, v)

    o = lax.map(one_block, qb)
    return o.transpose(1, 0, 2, 3, 4).reshape(B, S, H * V_DIM)

def conformer_conv(u, conv_w, conv_b, ln_g, ln_b):
    a, g = jnp.split(u, 2, axis=-1)
    v = a * jax.nn.sigmoid(g)
    pad = (CONV_WIDTH - 1) // 2
    v = lax.conv_general_dilated(
        v, conv_w[:, None, :], window_strides=(1,), padding=[(pad, pad)],
        dimension_numbers=('NWC', 'WIO', 'NWC'), feature_group_count=CONV_CH) + conv_b
    return jax.nn.silu(layernorm(v, ln_g, ln_b))

def mixing_sublayer(x, shift, scale, gate, ctx_cache, attn_norm_g, w_in, q_norm_g, w_q_up,
                    kv_norm_g, w_kv_up, conv_w, conv_b, conv_ln_g, conv_ln_b, w_out):
    B, S, _ = x.shape
    h = modulate(rmsnorm(x, attn_norm_g), shift, scale)
    proj = h @ w_in
    q_lat, ckv, krope, glu_in = jnp.split(
        proj, [Q_RANK, Q_RANK + KV_RANK, Q_RANK + KV_RANK + QK_ROPE], axis=-1)
    q = (rmsnorm(q_lat, q_norm_g) @ w_q_up).reshape(B, S, MLA_HEADS, QK_NOPE + QK_ROPE)
    ckv = rmsnorm(ckv, kv_norm_g)
    if ctx_cache is None:
        k, v = expand_kv(ckv, krope, w_kv_up)
    else:
        q = jnp.concatenate([q[..., :QK_NOPE], axial_rope_2d(q[..., QK_NOPE:], S)], axis=-1)
        krope_rot = axial_rope_2d(krope[:, :, None, :], S)[:, :, 0, :]
        k_lat, v_lat = expand_kv(ckv, krope_rot, w_kv_up)
        k_ctx, v_ctx = expand_kv(ctx_cache[0], ctx_cache[1], w_kv_up)
        k = jnp.concatenate([k_ctx, k_lat], axis=1)
        v = jnp.concatenate([v_ctx, v_lat], axis=1)
    attn = mha_blocks(q, k, v)
    conv = conformer_conv(glu_in, conv_w, conv_b, conv_ln_g, conv_ln_b)
    out = jnp.concatenate([attn, conv], axis=-1) @ w_out
    return x + gate * out, ckv, krope

def expert_choice_moe(h, w_router, w_gate, w_up, w_down):
    B, S, D = h.shape
    xf = h.reshape(B * S, D)
    n_tok = B * S
    cap = EC_FACTOR * n_tok // N_EXPERTS
    aff = jax.nn.softmax((xf @ w_router).astype(jnp.float32), axis=-1)
    gates, idx = lax.top_k(aff.T, cap)
    xs = xf[idx]
    a = jnp.einsum('ecd,edf->ecf', xs, w_gate)
    u = jnp.einsum('ecd,edf->ecf', xs, w_up)
    y = jnp.einsum('ecf,efd->ecd', jax.nn.silu(a) * u, w_down) * gates[..., None].astype(h.dtype)
    out = jnp.zeros((n_tok, D), h.dtype).at[idx.reshape(-1)].add(y.reshape(-1, D))
    return out.reshape(B, S, D)

def moe_sublayer(x, shift, scale, gate, ffn_norm_g, w_router, w_gate, w_up, w_down):
    h = modulate(rmsnorm(x, ffn_norm_g), shift, scale)
    return x + gate * expert_choice_moe(h, w_router, w_gate, w_up, w_down)

def setup_inputs(seed: int = 0) -> dict:
    key = jax.random.key(seed)
    ks = iter(jax.random.split(key, 32))

    def nrm(shape, scale=1.0):
        return jax.random.normal(next(ks), shape, jnp.float32) * scale

    def gain(shape):
        return 1.0 + 0.05 * jax.random.normal(next(ks), shape, jnp.float32)

    D = D_MODEL
    return {
        "x_prompt": nrm((BATCH, SEQ, D)),
        "x_sample": nrm((DEC_BATCH, DEC_SEQ, D)),
        "cache_ckv": nrm((DEC_BATCH, DEPTH, PAST_LEN, KV_RANK)),
        "cache_krope": nrm((DEC_BATCH, DEPTH, PAST_LEN, QK_ROPE)),
        "c": nrm((DEC_BATCH, D)),
        "c_ctx": nrm((D,)),
        "w_mod": nrm((DEPTH, D, N_MOD * D), 0.5 * D ** -0.5),
        "b_mod": nrm((DEPTH, N_MOD * D), 0.01),
        "attn_norm_g": gain((DEPTH, D)),
        "w_in": nrm((DEPTH, D, IN_COLS), D ** -0.5),
        "q_norm_g": gain((DEPTH, Q_RANK)),
        "w_q_up": nrm((DEPTH, Q_RANK, MLA_HEADS * (QK_NOPE + QK_ROPE)), Q_RANK ** -0.5),
        "kv_norm_g": gain((DEPTH, KV_RANK)),
        "w_kv_up": nrm((DEPTH, KV_RANK, MLA_HEADS * (QK_NOPE + V_DIM)), KV_RANK ** -0.5),
        "conv_w": nrm((DEPTH, CONV_WIDTH, CONV_CH), CONV_WIDTH ** -0.5),
        "conv_b": nrm((DEPTH, CONV_CH), 0.01),
        "conv_ln_g": gain((DEPTH, CONV_CH)),
        "conv_ln_b": nrm((DEPTH, CONV_CH), 0.01),
        "w_out": nrm((DEPTH, MIX_WIDTH, D), MIX_WIDTH ** -0.5),
        "ffn_norm_g": gain((DEPTH, D)),
        "w_router": nrm((DEPTH, D, N_EXPERTS), D ** -0.5),
        "w_gate": nrm((DEPTH, N_EXPERTS, D, EXPERT_FF), D ** -0.5),
        "w_up": nrm((DEPTH, N_EXPERTS, D, EXPERT_FF), D ** -0.5),
        "w_down": nrm((DEPTH, N_EXPERTS, EXPERT_FF, D), EXPERT_FF ** -0.5),
        "final_norm_g": gain((D,)),
    }

def reference(x_prompt, x_sample, cache_ckv, cache_krope, c, c_ctx, w_mod, b_mod,
              attn_norm_g, w_in, q_norm_g, w_q_up, kv_norm_g, w_kv_up, conv_w, conv_b,
              conv_ln_g, conv_ln_b, w_out, ffn_norm_g, w_router, w_gate, w_up, w_down,
              final_norm_g):
    xp = x_prompt
    xs = x_sample
    ckv_states = []
    krope_states = []
    for l in range(DEPTH):
        mix_w = (attn_norm_g[l], w_in[l], q_norm_g[l], w_q_up[l], kv_norm_g[l], w_kv_up[l],
                 conv_w[l], conv_b[l], conv_ln_g[l], conv_ln_b[l], w_out[l])
        moe_w = (ffn_norm_g[l], w_router[l], w_gate[l], w_up[l], w_down[l])
        sh1c, sc1c, g1c, sh2c, sc2c, g2c = adaln(c_ctx[None, :], w_mod[l], b_mod[l])
        sh1s, sc1s, g1s, sh2s, sc2s, g2s = adaln(c, w_mod[l], b_mod[l])
        xp, ckv_p, krope_p = mixing_sublayer(xp, sh1c, sc1c, g1c, None, *mix_w)
        xp = moe_sublayer(xp, sh2c, sc2c, g2c, *moe_w)
        ckv_states.append(ckv_p)
        krope_states.append(krope_p)
        xs, _, _ = mixing_sublayer(xs, sh1s, sc1s, g1s,
                                   (cache_ckv[:, l], cache_krope[:, l]), *mix_w)
        xs = moe_sublayer(xs, sh2s, sc2s, g2s, *moe_w)
    y_prompt = rmsnorm(xp, final_norm_g)
    y_sample = rmsnorm(xs, final_norm_g)
    new_ckv = jnp.stack(ckv_states, axis=1)
    new_krope = jnp.stack(krope_states, axis=1)
    return (y_prompt, y_sample, new_ckv, new_krope)


_drawn_inputs = setup_inputs


def setup_inputs(seed=0):
    import zlib

    import numpy as np

    out = dict(_drawn_inputs(seed))
    spreads = {}
    factors = {'cache_ckv': 7.428,
     'cache_krope': 8.0,
     'b_mod': 4.298,
     'q_norm_g': 8.0,
     'conv_b': 8.0,
     'conv_ln_g': 6.263,
     'conv_ln_b': 8.0,
     'ffn_norm_g': 4.793}
    for name, (base, spread) in spreads.items():
        noise = np.random.default_rng([zlib.crc32(name.encode()), seed]).standard_normal(out[name].shape)
        drawn = base * np.exp(spread * noise) if base else spread * noise
        out[name] = __import__('jax').numpy.asarray(drawn.astype(out[name].dtype))
    for name, factor in factors.items():
        out[name] = (out[name] * factor).astype(out[name].dtype)
    return out
```

```python
from contextlib import ExitStack

import concourse.bass as bass
from concourse import mybir

F32 = mybir.dt.float32
U32 = mybir.dt.uint32
ALU = mybir.AluOpType
ACT = mybir.ActivationFunctionType
AX = mybir.AxisListType.X

P = 128
D = 1024
KD = D // P
NS, NP = 512, 128
NT = NS + NP
TT = NT // P
CTX = 256
NK = CTX + NT
KS = CTX + NS
H, DN, DR, DV = 8, 64, 32, 64
DQK = DN + DR
QR, KR, CC, W = 768, 256, 512, 31
QC, KC, CT = QR // P, KR // P, CC // P
GRID = 64
E, F = 16, 1024
CS, CP = 2 * NS // E, 2 * NP // E
C = CS + CP
EPS = 1e-6
PAD = (W - 1) // 2
GW = PAD + NS + PAD + NP + PAD
CW = NS + PAD + NP
CP0 = NS + PAD

V_C, V_CCTX, V_AG, V_FG, V_QG, V_KG, V_CB, V_LG, V_LB, V_BM = 0, 8, 16, 24, 32, 38, 40, 44, 48, 52
VR = V_BM + 48
NMOD = 6
HALF = 12

SLOT = 4 * F
SLOTS = 6


def layer(nc, x_prompt, x_sample, cache_ckv, cache_krope, c, c_ctx, w_mod, b_mod, attn_norm_g, w_in,
          q_norm_g, w_q_up, kv_norm_g, w_kv_up, conv_w, conv_b, conv_ln_g, conv_ln_b, w_out, ffn_norm_g,
          w_router, w_gate, w_up, w_down, final_norm_g, tables, y_prompt, y_sample, new_ckv, new_krope):
    ctx = ExitStack()
    with ctx:
        def sb(name, n, dt=F32):
            return ctx.enter_context(nc.sbuf_tensor(name, [P, n], dt))

        def sem(name):
            return ctx.enter_context(nc.semaphore(name))

        ring = sb("ring", SLOTS * SLOT)
        wglu = ring[:, 0:8 * 2 * CC].rearrange("p (k n) -> p k n", k=KD)
        wq = ring[:, 0:QC * 768].rearrange("p (k n) -> p k n", k=QC)
        V = ring[:, 4608:4608 + 7 * 512].rearrange("p (t n) -> p t n", t=7)
        winq = ring[:, 8192:8192 + 6144].rearrange("p (k n) -> p k n", k=KD)
        kT = ring[:, 8192:8192 + H * NK].rearrange("p (h n) -> p h n", h=H)
        sq = ring[:, 14336:14336 + 3 * NT].rearrange("p (b n) -> p b n", b=3)
        wm_c = ring[:, 16384:20480].rearrange("p (k n) -> p k n", k=KD)
        wm_a = ring[:, 20480:24576].rearrange("p (k n) -> p k n", k=KD)
        wout = ring[:, 16384:24576].rearrange("p (k n) -> p k n", k=KD)

        xr = sb("x_region", 5120)
        x = xr[:, :].rearrange("p (t n) -> p t n", t=TT)
        QT = xr[:, :].rearrange("p (h n) -> p h n", h=H)
        wm_x = xr[:, 0:4096].rearrange("p (k n) -> p k n", k=KD)
        hr = sb("h_region", 5120)
        hT = hr[:, :].rearrange("p (k n) -> p k n", k=KD)
        wm_h = hr[:, 0:4096].rearrange("p (k n) -> p k n", k=KD)
        qr = hr[:, 0:2 * NT].rearrange("p (r n) -> p r n", r=2)
        rt = hr[:, 1280:1280 + 512]
        dsq = hr[:, 1792:1792 + CT * CW].rearrange("p (c n) -> p c n", c=CT)
        rv = hr[:, 4412:4412 + CW]
        PT = hr[:, 0:1536].rearrange("p (b n) -> p b n", b=2)
        On = hr[:, 1536:4096].rearrange("p (t n) -> p t n", t=TT)
        xn2 = hr[:, 0:2048].rearrange("p (b n) -> p b n", b=2)
        gtmp = hr[:, 2048:3072].rearrange("p (b n) -> p b n", b=2)
        h2T = hr[:, 3072:5120].rearrange("p (b k n) -> p b k n", b=2, k=KD)
        mixA = sb("mix_attn", 4 * NT)[:, :].rearrange("p (k n) -> p k n", k=4)
        mixC = sb("mix_conv", CT * CW)[:, :].rearrange("p (k n) -> p k n", k=CT)
        qlr = sb("q_latent", QC * NT)
        qlat = qlr[:, :].rearrange("p (k n) -> p k n", k=QC)
        g1b = qlr[:, 0:2 * D].rearrange("p (g n) -> p g n", g=2)
        ckr = sb("ckv", KC * NK)
        ckvT = ckr[:, :].rearrange("p (k n) -> p k n", k=KC)
        kr = sb("krope", NK)
        gvr = sb("glu_value", CT * GW)
        gluv = gvr[:, :].rearrange("p (c n) -> p c n", c=CT)
        wkr = sb("w_kv", KC * 1024)
        wkv = wkr[:, :].rearrange("p (k n) -> p k n", k=KC)
        wikr = sb("w_in_kv", KD * 288)
        winkv = wikr[:, :].rearrange("p (k n) -> p k n", k=KD)
        Pb = wikr[:, 0:1536].rearrange("p (b n) -> p b n", b=2)
        cachek = Pb[:, 0, 0:512].rearrange("p (t n) -> p t n", t=2)
        cacher = Pb[:, 0, 512:576].rearrange("p (t n) -> p t n", t=2)
        vrow = Pb[:, 0, 576:704]
        cwrow = wikr[:, 768:768 + CC]
        tab = sb("tables", 384 + 1024)
        ident, ones, rotm = tab[:, 0:128], tab[:, 128:256], tab[:, 256:384]
        cos, sin = tab[:, 384:896], tab[:, 896:1408]
        vec = sb("vectors", VR)
        cw = sb("conv_taps", CT * W)[:, :].rearrange("p (c w) -> p c w", c=CT)
        cact = sb("cond_silu", 16)[:, :].rearrange("p (g k) -> p g k", g=2)
        modc = sb("modulation", 96)[:, :].rearrange("p (m g) -> p m g", g=2)
        A1 = sb("scale1", 16)[:, :].rearrange("p (k g) -> p k g", g=2)
        A2 = sb("scale2", 16)[:, :].rearrange("p (k g) -> p k g", g=2)
        ss = sb("sum_squares", 8)
        rs = sb("rstd", 8)
        rq = sb("rstd_q", 8)
        mx = sb("row_max", 2)
        nb = sb("exp_bias", 2)
        psm = sb("exp_sum", 2)
        rin = sb("exp_sum_inv", 2)
        wr = sb("w_router", KD * E)[:, :].rearrange("p (k n) -> p k n", k=KD)
        aff = sb("affinity", 2 * E)[:, :].rearrange("p (b n) -> p b n", b=2)
        affn = sb("affinity_n", 2 * E)[:, :].rearrange("p (b n) -> p b n", b=2)
        sm = sb("router_stats", 8)
        idxf = sb("choice_f", E)
        idxc = sb("choice", E, U32)
        gates = sb("gates", E)
        flag = sb("flag", 1)
        xg = wkr[:, 0:D]
        yw = wkr[:, D:2 * D]
        xsT = gvr[:, 0:KD * C].rearrange("p (k n) -> p k n", k=KD)
        eh = gvr[:, 640:640 + KD * C].rearrange("p (k n) -> p k n", k=KD)
        esil = gvr[:, 1280:1280 + KD * C].rearrange("p (k n) -> p k n", k=KD)
        A2f = gvr[:, 1920:1920 + KD * C].rearrange("p (k n) -> p k n", k=KD)
        S2f = ckr[:, 0:KD * C].rearrange("p (k n) -> p k n", k=KD)
        G2f = ckr[:, 640:640 + KD * C].rearrange("p (k n) -> p k n", k=KD)
        yT = wikr[:, 0:KD * C].rearrange("p (k n) -> p k n", k=KD)
        xmod = wikr[:, 640:640 + KD * C].rearrange("p (k n) -> p k n", k=KD)
        fgb = wikr[:, 1280:1280 + D]
        affT = kr[0:E, 0:NT]
        topv = ckr[0:E, 1280:1280 + C]
        topi = ckr[0:E, 1360:1360 + C].bitcast(U32)
        topf = ckr[0:E, 1440:1440 + C]
        diag = ckr[:, 1520:1520 + 256].rearrange("p (b n) -> p b n", b=2)
        ost = wikr[:, 1536:1536 + 288]

        ps = ctx.enter_context(nc.psum_tensor("ps", [P, 8 * 512], F32))

        def bank(b, lo=0, hi=512, p=P, p0=0):
            return ps[p0:p, b * 512 + lo:b * 512 + hi]

        acc_d = nc.dram_tensor("residual", [NT, D], F32, kind="Internal").ap()
        hn_d = nc.dram_tensor("normed", [NT, D], F32, kind="Internal").ap()

        names = """ld_small ld_cache ld_x0 ld_x1 ld_x2 ld_x3 ld_x4 ld_glu ld_winq ld_winkv ld_wkv ld_wq ld_wout
        ld_router ld_fg vecT_ps vecT_sb cact_ok sqx rstdx_s rstdx xn_ok mod_ps mod1 mod2 a1_ok hT_ps hTa hTd
        tr_ctx ctx_sb glu_pad glu_mul conv_ops conv_done pj ev sq_ok qst kvs kvs_r kvr ckv_ok rotk krt kT_rope
        rk_step wq_ok rotq rq_step rope_a ln_mean ln_d ln_sq ln_var ln_s ln_r ln_n ln_out qs_s qs_r qu_done
        nk_ps nk_sb out_kv diag_ok g1_ps g1_sb s_ps smax nb_ok exp_ok t_ps pta ptd pv_ps rin_ok o_ok at_ps ata atd
        op_ps g1m x1_ok x1sq x1s x1r x1n out_x1 out_hn0 out_hn1 out_hn2 out_hn3 out_hn4 xt_ps h2a h2d lg_ps lmax lexp lrec affn_ok aff_ps affT_ok
        topk sel sel_ps sel_sb full_ok sm_free a2_ok
        gath xt2_ps xm1 xs_ok a_ps u_ps sil h_ok y_ps yT_ok yt_ps yw_ok yw_free scat
        ld_acc0 ld_acc1 ld_acc2 ld_acc3 ld_acc4 fsq fsr frec fin_ok out_y gcol_ok""".split()
        s = {n: sem(n) for n in names}
        wmod_ld = [sem(f"wmod_ld{j}") for j in range(4)]
        slot_ld = [sem(f"slot_ld{j}") for j in range(SLOTS)]

        block = ctx.enter_context(nc.Block())

        wmod_v = w_mod[0].rearrange("(k p) n -> p k n", p=P)
        win_v = w_in[0].rearrange("(k p) n -> p k n", p=P)
        wm_buf = [wm_a, wm_c, wm_h, wm_a] + [[wm_c, wm_x, wm_a][j % 3] for j in range(8)]
        wm_sem = [0, 1, 2, 0] + [[1, 3, 0][j % 3] for j in range(8)]
        wm_cnt = [16 * (wm_sem[:j + 1].count(wm_sem[j])) for j in range(HALF)]
        wm_prev = [max([i for i in range(j) if wm_sem[i] == wm_sem[j]], default=None) for j in range(HALF)]

        def rope_units(u):
            return 4 * (u // 5) + min(u % 5, 4)

        @block.sync
        def _(sp):
            def load_mod(j):
                if wm_prev[j] is not None:
                    sp.wait_ge(s["mod_ps"], wm_prev[j] + 1)
                sp.dma_start(wm_buf[j], wmod_v[:, :, 512 * j:512 * j + 512]).then_inc(wmod_ld[wm_sem[j]], 16)

            def load_heads(dst, src, chunks, a, b, done):
                for k in range(chunks):
                    rows = src[0, k * P:(k + 1) * P, :].rearrange("p (h f) -> p h f", h=H)
                    for lo, w, col in ((0, a, 0), (a, b, H * a)):
                        sp.dma_start(dst[:, k, col:col + H * w].rearrange("p (h f) -> p h f", h=H),
                                     rows[:, :, lo:lo + w]).then_inc(done, 16)

            for j in range(3):
                load_mod(j)
            for t in range(TT):
                src = x_sample[0, t * P:(t + 1) * P, :] if t < 4 else x_prompt[0]
                sp.dma_start(x[:, t, :], src).then_inc(s[f"ld_x{t}"], 16)
            load_mod(3)
            sp.dma_start(wglu[:, :, :], win_v[:, :, 1056:2080]).then_inc(s["ld_glu"], 16)
            load_heads(wkv, w_kv_up, KC, DN, DV, s["ld_wkv"])
            load_mod(4)
            sp.dma_start(winq[:, :, :], win_v[:, :, 0:QR]).then_inc(s["ld_winq"], 16)
            sp.wait_ge(s["tr_ctx"], 1)
            sp.dma_start(winkv[:, :, :], win_v[:, :, QR:QR + 288]).then_inc(s["ld_winkv"], 16)
            sp.wait_ge(s["hT_ps"], KD)
            for j in range(5, HALF):
                load_mod(j)
                if j == 8:
                    sp.wait_ge(s["pj"], 8)
                    load_heads(wq, w_q_up, QC, DN, DR, s["ld_wq"])
            sp.wait_ge(s["mod_ps"], HALF)
            sp.dma_start(wout[:, :, :], w_out[0].rearrange("(k p) n -> p k n", p=P)).then_inc(s["ld_wout"], 16)
            sp.wait_ge(s["s_ps"], H * TT)
            for t in [4, 0, 1, 2, 3]:
                src = x_sample[0, t * P:(t + 1) * P, :] if t < 4 else x_prompt[0]
                sp.dma_start(x[:, t, :], src).then_inc(s[f"ld_x{t}"], 16)

            def slots(e, wait):
                for n in range(SLOTS):
                    w = [w_gate, w_gate, w_up, w_up, w_down, w_down][n]
                    wait(n)
                    dst = ring[:, n * SLOT:(n + 1) * SLOT].rearrange("p (k n) -> p k n", k=4)
                    src = w[0, e].rearrange("(k p) n -> p k n", p=P) if isinstance(e, int) else \
                        w[0, bass.ds(e, 1)].rearrange("o (k p) n -> p (o k) n", p=P)
                    sp.dma_start(dst, src[:, 4 * (n % 2):4 * (n % 2) + 4, :]).then_inc(slot_ld[n], 16)

            def wait_first(n):
                if n == 0:
                    sp.wait_ge(s["pv_ps"], H * TT)
                if n == 4:
                    sp.wait_ge(s["op_ps"], TT)

            slots(0, wait_first)
            with sp.Fori(1, E) as e:
                slots(e, lambda n: sp.wait_ge(s[["a_ps", "u_ps", "y_ps"][n // 2]], e))
            sp.wait_ge(s["scat"], 16 * E)
            for t in range(TT):
                sp.dma_start(x[:, t, :], acc_d[t * P:(t + 1) * P, :]).then_inc(s[f"ld_acc{t}"], 16)
            for t in range(TT):
                sp.wait_ge(s["fin_ok"], t + 1)
                dst = y_sample[0, t * P:(t + 1) * P, :] if t < 4 else y_prompt[0]
                sp.dma_start(dst, x[:, t, :]).then_inc(s["out_y"], 16)
            sp.wait_ge(s["out_y"], 16 * TT)
            sp.wait_ge(s["out_kv"], 32)

        @block.tensor
        def _(pe):
            mm, tr = nc.tensor.matmul, nc.tensor.transpose
            pe.wait_ge(s["ld_small"], 16 * 12)
            tr(bank(7, 128, 128 + VR), vrow[0:VR, :], ident[0:VR, 0:VR])
            for k in range(CT):
                last = tr(bank(6, 256 + W * k, 256 + W * (k + 1)), cwrow[0:W, k * P:(k + 1) * P], ident[0:W, 0:W])
            last.then_inc(s["vecT_ps"], 1)
            pe.wait_ge(s["ld_cache"], 32)
            for j in range(KC):
                for t in range(2):
                    tr(bank(5, j * CTX + t * P, j * CTX + (t + 1) * P), cachek[:, t, j * P:(j + 1) * P], ident)
            for t in range(2):
                last = tr(bank(4, t * P, (t + 1) * P, DR), cacher[:, t, :], ident)
            last.then_inc(s["tr_ctx"], 1)

            def mod(j):
                if j == 0:
                    pe.wait_ge(s["cact_ok"], 1)
                    pe.wait_ge(s["vecT_sb"], 2)
                if j == 4:
                    pe.wait_ge(s["mod1"], 1)
                pe.wait_ge(wmod_ld[wm_sem[j]], wm_cnt[j])
                for m in range(4):
                    o = 2 * (4 * j + m)
                    for k in range(KD):
                        last = mm(bank(7, o, o + 2), wm_buf[j][:, k, m * P:(m + 1) * P], cact[:, :, k],
                                  start=(k == 0), stop=(k == KD - 1))
                last.then_inc(s["mod_ps"], 1)

            for j in range(4):
                mod(j)
            for k in range(KD):
                if k == 0:
                    pe.wait_ge(s["xn_ok"], TT)
                if k >= 2:
                    pe.wait_ge(s["hTa"] if k % 2 == 0 else s["hTd"], k // 2)
                for t in range(TT):
                    o = bank(2 * (k % 2), t * P, (t + 1) * P) if t < 4 else bank(2 * (k % 2) + 1, 0, P)
                    last = tr(o, x[:, t, k * P:(k + 1) * P], ident)
                last.then_inc(s["hT_ps"], 1)
            pe.wait_ge(s["hTa"], KD // 2)
            pe.wait_ge(s["hTd"], KD // 2)

            def q_stat(i):
                pe.wait_ge(s["sq_ok"], i + 1)
                if i == 0:
                    pe.wait_ge(s["ctx_sb"], 1)
                for t in range(TT):
                    last = mm(bank(4, t, t + 1), sq[:, i % 3, t * P:(t + 1) * P], ones[:, 0:1],
                              start=(i == 0 and t == 0), stop=(i == QC - 1), skip_group_check=True)
                last.then_inc(s["qst"], 1)

            for i in range(17):
                if i >= 2:
                    pe.wait_ge(s["ev"], i - 1)
                if i == 0:
                    pe.wait_ge(s["ld_glu"], 16)
                if i == 8:
                    pe.wait_ge(s["ld_winq"], 16)
                if i == 14:
                    pe.wait_ge(s["ld_winkv"], 16)
                for lo, hi, b in ((0, NS, 2 * (i % 2)), (NS, NT, 2 * (i % 2) + 1)):
                    for k in range(KD):
                        if i < 8:
                            col = (CC if i % 2 == 0 else 0) + P * (i // 2)
                            w, M = wglu[:, k, col:col + P], P
                        elif i < 14:
                            w, M = winq[:, k, P * (i - 8):P * (i - 7)], P
                        else:
                            M = P if i < 16 else DR
                            w = winkv[:, k, P * (i - 14):P * (i - 14) + M]
                        last = mm(bank(b, 0, hi - lo, M), w, hT[:, k, lo:hi], start=(k == 0), stop=(k == KD - 1))
                last.then_inc(s["pj"], 1)
                if i % 2 == 1:
                    mod(4 + i // 2)
                if 10 <= i < 16:
                    q_stat(i - 10)
            for j in range(KC):
                pe.wait_ge(s["sq_ok"], QC + j + 1)
                if j == 0:
                    pe.wait_ge(s["ctx_sb"], 2)
                mm(bank(5), ones, sq[:, j, 0:NS], start=(j == 0), stop=(j == KC - 1))
                last = mm(bank(6, 0, NP), ones, sq[:, j, NS:NT], start=(j == 0), stop=(j == KC - 1))
            last.then_inc(s["kvs"], 1)

            pe.wait_ge(s["wq_ok"], 1)
            for i in range(6):
                n = 17 + i
                pe.wait_ge(s["ev"], n - 1)
                for lo, hi, b in ((0, NS, 2 * (n % 2)), (NS, NT, 2 * (n % 2) + 1)):
                    for k in range(QC):
                        w = wq[:, k, i * P:(i + 1) * P]
                        last = mm(bank(b, 0, hi - lo), w, qlat[:, k, lo:hi], start=(k == 0), stop=(k == QC - 1))
                last.then_inc(s["pj"], 1)
            pe.wait_ge(s["kvs_r"], 2)
            mm(bank(5, 0, NS, DR), rotm[0:DR, 0:DR], kr[0:DR, CTX:KS], start=True, stop=True).then_inc(s["rotk"], 1)
            pe.wait_ge(s["ev"], 22)
            mm(bank(6), rotm, qr[:, 0, 0:NS], start=True, stop=True).then_inc(s["rotq"], 1)
            pe.wait_ge(s["rk_step"], 2)
            pe.wait_ge(s["ev"], 23)
            mm(bank(5), rotm, qr[:, 1, 0:NS], start=True, stop=True).then_inc(s["rotq"], 1)
            pe.wait_ge(s["conv_done"], CT)
            pe.wait_ge(s["qs_s"], 1)
            pe.wait_ge(s["mod2"], 1)
            for k in range(CT):
                mm(bank(4), ones, mixC[:, k, 0:NS], start=(k == 0), stop=(k == CT - 1))
                last = mm(bank(7, 0, CW - NS), ones, mixC[:, k, NS:CW], start=(k == 0), stop=(k == CT - 1))
            last.then_inc(s["ln_mean"], 1)
            pe.wait_ge(s["ckv_ok"], KC)
            pe.wait_ge(s["ld_wkv"], 32 * KC)
            for i in range(4):
                n = 23 + i
                pe.wait_ge(s["ev"], n - 1)
                for lo, hi, b in ((0, 512, 2 * (n % 2)), (512, NK, 2 * (n % 2) + 1)):
                    for k in range(KC):
                        last = mm(bank(b, 0, hi - lo), wkv[:, k, i * P:(i + 1) * P], ckvT[:, k, lo:hi],
                                  start=(k == 0), stop=(k == KC - 1))
                last.then_inc(s["pj"], 1)
            pe.wait_ge(s["rq_step"], 6)
            pe.wait_ge(s["ln_sq"], CT)
            for k in range(CT):
                mm(bank(5), ones, dsq[:, k, 0:NS], start=(k == 0), stop=(k == CT - 1))
                last = mm(bank(6, 0, CW - NS), ones, dsq[:, k, NS:CW], start=(k == 0), stop=(k == CT - 1))
            last.then_inc(s["ln_var"], 1)
            for t in range(7):
                n = 27 + t
                pe.wait_ge(s["ev"], n - 1)
                for k in range(KC):
                    last = mm(bank(2 * (n % 2)), ckvT[:, k, t * P:(t + 1) * P], wkv[:, k, H * DN:],
                              start=(k == 0), stop=(k == KC - 1))
                last.then_inc(s["pj"], 1)
            pe.wait_ge(s["ln_d"], CT)
            for j in range(KC):
                tr(bank(4, j * P, (j + 1) * P), ckvT[:, j, KS:NK], ident)
            tr(bank(4, KR, KR + DR), kr[0:DR, KS:NK], ident[0:DR, 0:DR]).then_inc(s["nk_ps"], 1)
            pe.wait_ge(s["ln_s"], 2)
            for g in range(2):
                if g == 1:
                    pe.wait_ge(s["nk_sb"], 1)
                for k in range(KD):
                    n = g * KD + k
                    b = [5, 6, 4, 7][2 * g + k // 4]
                    pe.wait_ge(s["diag_ok"], n + 1)
                    mm(bank(b, (k % 4) * P, (k % 4 + 1) * P), ones, diag[:, n % 2, :],
                       start=True, stop=True).then_inc(s["g1_ps"], 1)

            def scores(u):
                h, t = divmod(u, TT)
                if u >= 2:
                    pe.wait_ge(s["exp_ok"], u - 1)
                b = 2 * (u % 2)
                q = QT[0:DQK, h, t * P:(t + 1) * P]
                if t < 4:
                    mm(bank(b), q, kT[0:DQK, h, 0:512], start=True, stop=True)
                    mm(bank(b + 1, 0, KS - 512), q, kT[0:DQK, h, 512:KS], start=True, stop=True).then_inc(s["s_ps"], 1)
                else:
                    mm(bank(b, 0, NP), q, kT[0:DQK, h, KS:NK], start=True, stop=True).then_inc(s["s_ps"], 1)

            pe.wait_ge(s["ev"], 34)
            pe.wait_ge(s["rope_a"], 8)
            pe.wait_ge(s["kT_rope"], 1)
            pe.wait_ge(s["g1_sb"], 4)
            scores(0)
            scores(1)
            for u in range(H * TT):
                h, t = divmod(u, TT)
                pe.wait_ge(s["exp_ok"], u + 1)
                if u >= 1:
                    pe.wait_ge(s["pta"], u)
                    pe.wait_ge(s["ptd"], rope_units(u))
                kts = range(6) if t < 4 else range(1)
                for kt in kts:
                    last = tr(bank(4, kt * P, (kt + 1) * P), Pb[:, u % 2, kt * P:(kt + 1) * P], ident)
                last.then_inc(s["t_ps"], 1)
                if u + 2 < H * TT:
                    scores(u + 2)
                pe.wait_ge(s["pta"], u + 1)
                pe.wait_ge(s["ptd"], rope_units(u + 1))
                if u >= 2:
                    pe.wait_ge(s["o_ok"], u - 1)
                for kt in kts:
                    vt = kt if t < 4 else 6
                    last = mm(bank(6 + u % 2, 0, DV), PT[:, u % 2, kt * P:(kt + 1) * P],
                              V[:, vt, h * DV:(h + 1) * DV], start=(kt == 0), stop=(kt == kts[-1]))
                last.then_inc(s["pv_ps"], 1)
            pe.wait_ge(s["o_ok"], H * TT)
            for k in range(4):
                if k >= 2:
                    pe.wait_ge(s["ata"] if k % 2 == 0 else s["atd"], 1)
                for t in range(TT):
                    o = bank(2 * (k % 2), t * P, (t + 1) * P) if t < 4 else bank(2 * (k % 2) + 1, 0, P)
                    last = tr(o, On[:, t, k * P:(k + 1) * P], ident)
                last.then_inc(s["at_ps"], 1)

            order = [4, 0, 1, 2, 3]

            def out_proj(i):
                t = order[i]
                if i >= 2:
                    pe.wait_ge(s["g1m"], 2 * (i - 1))
                for n in range(2):
                    for k in [4, 5, 6, 7, 0, 1, 2, 3]:
                        o = CP0 if t == 4 else t * P
                        m = mixA[:, k, t * P:(t + 1) * P] if k < 4 else mixC[:, k - 4, o:o + P]
                        last = mm(bank(2 * (i % 2) + n), m, wout[:, k, n * 512:(n + 1) * 512],
                                  start=(k == 4), stop=(k == 3))
                last.then_inc(s["op_ps"], 1)

            def x_to_features(i):
                pe.wait_ge(s["x1n"], i + 1)
                if i >= 1:
                    pe.wait_ge(s["h2a"], 4 * i)
                    pe.wait_ge(s["h2d"], 4 * i)
                for k in range(KD):
                    last = tr(bank(4 + k // 4, (k % 4) * P, (k % 4 + 1) * P), xn2[:, i % 2, k * P:(k + 1) * P], ident)
                last.then_inc(s["xt_ps"], 1)

            def router(i):
                pe.wait_ge(s["h2a"], 4 * (i + 1))
                pe.wait_ge(s["h2d"], 4 * (i + 1))
                if i >= 1:
                    pe.wait_ge(s["lexp"], i)
                for k in range(KD):
                    last = mm(bank(6, 0, E), h2T[:, i % 2, k, :], wr[:, k, :], start=(k == 0), stop=(k == KD - 1))
                last.then_inc(s["lg_ps"], 1)

            def aff_transpose(i):
                pe.wait_ge(s["affn_ok"], i + 1)
                if i >= 1:
                    pe.wait_ge(s["affT_ok"], i)
                tr(bank(7, 0, P, E), affn[:, i % 2, :], ident).then_inc(s["aff_ps"], 1)

            pe.wait_ge(s["ata"], 2)
            pe.wait_ge(s["atd"], 2)
            pe.wait_ge(s["ln_out"], 2 * CT)
            pe.wait_ge(s["ld_wout"], 16)
            pe.wait_ge(s["ld_router"], 16)
            for i in range(TT):
                out_proj(i)
                if i >= 1:
                    x_to_features(i - 1)
                if i >= 2:
                    router(i - 2)
                if i >= 3:
                    aff_transpose(i - 3)
            router(3)
            aff_transpose(2)
            x_to_features(4)
            aff_transpose(3)
            router(4)
            aff_transpose(4)
            pe.wait_ge(s["sel"], 2)
            tr(bank(5, 0, E, C), topf, ident[0:E, 0:E])
            tr(bank(5, E, 2 * E, C), topv, ident[0:E, 0:E]).then_inc(s["sel_ps"], 1)
            pe.wait_ge(s["sel_sb"], 2)

            with pe.Fori(0, E) as e:
                pe.wait_ge(s["gath"], e * 16 + 16)
                for k in range(KD):
                    last = tr(bank(6 + k // 4, (k % 4) * C, (k % 4 + 1) * C), xg[0:C, k * P:(k + 1) * P],
                              ident[0:C, 0:C])
                last.then_inc(s["xt2_ps"], 1)
                pe.wait_ge(s["xs_ok"], e + 1)
                for m, (b0, done) in enumerate(((0, s["a_ps"]), (2, s["u_ps"]), (4, s["y_ps"]))):
                    if m == 2:
                        pe.wait_ge(s["h_ok"], e + 1)
                    pe.wait_ge(slot_ld[2 * m], e * 16 + 16)
                    pe.wait_ge(slot_ld[2 * m + 1], e * 16 + 16)
                    src = xsT if m < 2 else eh
                    for f in range(KD):
                        for k in range(KD):
                            w = ring[:, 2 * m * SLOT + k * F + f * P:2 * m * SLOT + k * F + (f + 1) * P]
                            last = mm(bank(b0 + f // 4, (f % 4) * C, (f % 4 + 1) * C), w, src[:, k, :],
                                      start=(k == 0), stop=(k == KD - 1))
                    last.then_inc(done, 1)
                pe.wait_ge(s["yT_ok"], e + 1)
                for k in range(KD):
                    last = tr(bank(6 + k // 4, (k % 4) * P, (k % 4 + 1) * P, C), yT[:, k, :], ident)
                last.then_inc(s["yt_ps"], 1)
                pe.wait_ge(s["yw_ok"], e + 1)

        @block.scalar
        def _(act):
            A = nc.scalar.activation
            act.dma_start(tab[:, :], tables).then_inc(s["ld_small"], 16)
            rows = [(V_C, c[0], 8), (V_CCTX, c_ctx, 8), (V_AG, attn_norm_g[0], 8), (V_FG, ffn_norm_g[0], 8),
                    (V_QG, q_norm_g[0], 6), (V_KG, kv_norm_g[0], 2), (V_CB, conv_b[0], 4), (V_LG, conv_ln_g[0], 4),
                    (V_LB, conv_ln_b[0], 4), (V_BM, b_mod[0], 48)]
            for r, v, n in rows:
                act.dma_start(vrow[r:r + n, :], v.rearrange("(r n) -> r n", n=P)).then_inc(s["ld_small"], 16)
            act.dma_start(cwrow[0:W, :], conv_w[0]).then_inc(s["ld_small"], 16)
            act.dma_start(cachek, cache_ckv[0, 0].rearrange("(t p) n -> p t n", p=P)).then_inc(s["ld_cache"], 16)
            act.dma_start(cacher, cache_krope[0, 0].rearrange("(t p) n -> p t n", p=P)).then_inc(s["ld_cache"], 16)
            act.dma_start(wr, w_router[0].rearrange("(k p) n -> p k n", p=P)).then_inc(s["ld_router"], 16)
            act.wait_ge(s["vecT_sb"], 1)
            A(cact, vec[:, V_C:V_C + 16].rearrange("p (g k) -> p g k", g=2), ACT.Silu).then_inc(s["cact_ok"], 1)
            for t in range(TT):
                act.wait_ge(s[f"ld_x{t}"], 16)
                A(mixC[:, 0:2, 0:512], x[:, t, :].rearrange("p (a n) -> p a n", a=2), ACT.Square,
                  accum_out=ss[:, t:t + 1]).then_inc(s["sqx"], 1)
                act.wait_ge(s["sqx"], t + 1)
            act.wait_ge(s["gcol_ok"], 1)
            A(rs[:, 0:TT], ss[:, 0:TT], ACT.Sqrt, scale=1.0 / D, bias=ss[:, 5:6]).then_inc(s["rstdx_s"], 1)
            act.wait_ge(s["a1_ok"], 1)
            for k in range(0, KD, 2):
                act.wait_ge(s["hT_ps"], k + 1)
                A(hT[:, k, 0:NS], bank(0), ACT.Identity, scale=A1[:, k, 0:1], bias=modc[:, k, 0:1])
                A(hT[:, k, NS:NT], bank(1, 0, NP), ACT.Identity, scale=A1[:, k, 1:2],
                  bias=modc[:, k, 1:2]).then_inc(s["hTa"], 1)
            for i in range(17):
                b = 2 * (i % 2)
                act.wait_ge(s["pj"], i + 1)
                if i < 8 and i % 2 == 0:
                    cc = i // 2
                    if cc >= 2:
                        act.wait_ge(s["glu_mul"], cc - 1)
                    A(sq[:, cc % 2, 0:NS], bank(b), ACT.Sigmoid)
                    A(sq[:, cc % 2, NS:NT], bank(b + 1, 0, NP), ACT.Sigmoid).then_inc(s["ev"], 1)
                elif i < 8:
                    if i == 1:
                        act.wait_ge(s["glu_pad"], 1)
                    cc = i // 2
                    A(gluv[:, cc, PAD:PAD + NS], bank(b), ACT.Copy)
                    A(gluv[:, cc, 2 * PAD + NS:2 * PAD + NT], bank(b + 1, 0, NP), ACT.Copy).then_inc(s["ev"], 1)
                elif i < 14:
                    A(qlat[:, i - 8, 0:NS], bank(b), ACT.Copy)
                    A(qlat[:, i - 8, NS:NT], bank(b + 1, 0, NP), ACT.Copy).then_inc(s["ev"], 1)
                elif i < 16:
                    A(ckvT[:, i - 14, CTX:KS], bank(b), ACT.Copy)
                    A(ckvT[:, i - 14, KS:NK], bank(b + 1, 0, NP), ACT.Copy).then_inc(s["ev"], 1)
                else:
                    A(kr[0:DR, CTX:KS], bank(b, 0, 512, DR), ACT.Copy)
                    A(kr[0:DR, KS:NK], bank(b + 1, 0, NP, DR), ACT.Copy).then_inc(s["ev"], 1)
            act.wait_ge(s["qst"], QC)
            A(rq[:, 0:TT], bank(4, 0, TT), ACT.Sqrt, scale=1.0 / QR, bias=ss[:, 5:6]).then_inc(s["qs_s"], 1)
            act.wait_ge(s["kvs"], 1)
            A(sq[:, 2, 0:NS], bank(5), ACT.Sqrt, scale=1.0 / KR, bias=ss[:, 5:6]).then_inc(s["kvs_r"], 1)
            A(sq[:, 2, NS:NT], bank(6, 0, NP), ACT.Sqrt, scale=1.0 / KR, bias=ss[:, 5:6]).then_inc(s["kvs_r"], 1)
            for i in range(6):
                b = 2 * ((17 + i) % 2)
                act.wait_ge(s["pj"], 18 + i)
                if i < 4:
                    for a in range(2):
                        A(QT[0:DN, 2 * i + a, 0:NS], bank(b, 0, 512, DN * (a + 1), DN * a), ACT.Copy)
                        last = A(QT[0:DN, 2 * i + a, NS:NT], bank(b + 1, 0, NP, DN * (a + 1), DN * a), ACT.Copy)
                else:
                    A(qr[:, i - 4, 0:NS], bank(b), ACT.Copy)
                    last = A(qr[:, i - 4, NS:NT], bank(b + 1, 0, NP), ACT.Copy)
                last.then_inc(s["ev"], 1)
            act.wait_ge(s["kvr"], 1)
            act.wait_ge(s["ckv_ok"], KC)
            for i in range(4):
                b = 2 * ((23 + i) % 2)
                act.wait_ge(s["pj"], 24 + i)
                for a in range(2):
                    A(kT[0:DN, 2 * i + a, 0:512], bank(b, 0, 512, DN * (a + 1), DN * a), ACT.Copy)
                    last = A(kT[0:DN, 2 * i + a, 512:NK], bank(b + 1, 0, NK - 512, DN * (a + 1), DN * a), ACT.Copy)
                last.then_inc(s["ev"], 1)
            act.wait_ge(s["ln_var"], 1)
            A(rv[:, 0:NS], bank(5), ACT.Sqrt, scale=1.0 / CC, bias=ss[:, 5:6]).then_inc(s["ln_s"], 1)
            A(rv[:, NS:CW], bank(6, 0, CW - NS), ACT.Sqrt, scale=1.0 / CC, bias=ss[:, 5:6]).then_inc(s["ln_s"], 1)
            for r in range(2):
                act.wait_ge(s["rq_step"], 3 * (r + 1))
                for j in range(4):
                    A(QT[DN:DQK, 4 * r + j, :], qr[DR * j:DR * (j + 1), r, :], ACT.Copy).then_inc(s["rope_a"], 1)
            for t in range(7):
                act.wait_ge(s["pj"], 28 + t)
                A(V[:, t, :], bank(2 * ((27 + t) % 2)), ACT.Copy).then_inc(s["ev"], 1)
            for k in range(CT):
                act.wait_ge(s["ln_n"], k + 1)
                for lo, hi in ((0, NS), (CP0, CW)):
                    A(mixC[:, k, lo:hi], mixC[:, k, lo:hi], ACT.Silu, scale=vec[:, V_LG + k:V_LG + k + 1],
                      bias=vec[:, V_LB + k:V_LB + k + 1]).then_inc(s["ln_out"], 1)
            for n in range(4):
                b = [5, 6, 4, 7][n]
                act.wait_ge(s["g1_ps"], 4 * (n + 1))
                A(g1b[:, n // 2, (n % 2) * 512:(n % 2 + 1) * 512], bank(b), ACT.Copy).then_inc(s["g1_sb"], 1)
            def exps(u):
                h, t = divmod(u, TT)
                n = KS if t < 4 else NP
                act.wait_ge(s["nb_ok"], u + 1)
                if u >= 2:
                    act.wait_ge(s["t_ps"], u - 1)
                    act.wait_ge(s["rin_ok"], u - 1)
                b = 2 * (u % 2)
                A(Pb[:, u % 2, 0:n], bank(b, 0, n), ACT.Exp, scale=rq[:, t:t + 1], bias=nb[:, u % 2:u % 2 + 1],
                  accum_out=psm[:, u % 2:u % 2 + 1]).then_inc(s["exp_ok"], 1)

            exps(0)
            for u in range(H * TT):
                if u + 1 < H * TT:
                    exps(u + 1)
                act.wait_ge(s["t_ps"], u + 1)
                if u >= 2:
                    act.wait_ge(s["pv_ps"], u - 1)
                n = 512 if u % TT < 4 else NP
                A(PT[:, u % 2, 0:n], bank(4, 0, n), ACT.Copy).then_inc(s["pta"], 1)
            for k in (0, 2):
                act.wait_ge(s["at_ps"], k + 1)
                A(mixA[:, k, 0:NS], bank(0), ACT.Copy)
                A(mixA[:, k, NS:NT], bank(1, 0, NP), ACT.Copy).then_inc(s["ata"], 1)

            order = [4, 0, 1, 2, 3]

            def norm(i):
                t = order[i]
                act.wait_ge(s["x1_ok"], 2 * (i + 1))
                A(g1b_junk, x[:, t, :], ACT.Square, accum_out=ss[:, t:t + 1]).then_inc(s["x1sq"], 1)
                act.wait_ge(s["x1sq"], i + 1)
                A(rs[:, t:t + 1], ss[:, t:t + 1], ACT.Sqrt, scale=1.0 / D, bias=ss[:, 5:6]).then_inc(s["x1s"], 1)
                act.dma_start(acc_d[t * P:(t + 1) * P, :], x[:, t, :]).then_inc(s["out_x1"], 16)
                act.wait_ge(s["x1n"], i + 1)
                act.dma_start(hn_d[t * P:(t + 1) * P, :], xn2[:, i % 2, :]).then_inc(s[f"out_hn{i}"], 16)

            def h2(i):
                g = 1 if order[i] == 4 else 0
                act.wait_ge(s["xt_ps"], i + 1)
                if i >= 2:
                    act.wait_ge(s["lg_ps"], i - 1)
                for k in range(4):
                    A(h2T[:, i % 2, k, :], bank(4, k * P, (k + 1) * P), ACT.Identity, scale=A2[:, k, g:g + 1],
                      bias=modc[:, 24 + k, g:g + 1]).then_inc(s["h2a"], 1)

            def rexp(i):
                act.wait_ge(s["lmax"], i + 1)
                if i >= 2:
                    act.wait_ge(s["affn_ok"], i - 1)
                A(aff[:, i % 2, :], bank(6, 0, E), ACT.Exp, bias=sm[:, i % 2:i % 2 + 1],
                  accum_out=sm[:, 2 + i % 2:3 + i % 2]).then_inc(s["lexp"], 1)

            g1b_junk = qlr[:, 2 * D:2 * D + D]
            for i in range(TT):
                norm(i)
                if i >= 1:
                    h2(i - 1)
                if i >= 2:
                    rexp(i - 2)
            rexp(3)
            h2(4)
            rexp(4)

            act.wait_ge(s["sel_sb"], 2)
            with act.Fori(0, E) as e:
                act.wait_ge(s["a_ps"], e + 1)
                A(esil.rearrange("p (b f) n -> p b (f n)", b=2), ps[:, 0:1024].rearrange("p (b n) -> p b n", b=2)[:, :, 0:4 * C],
                  ACT.Silu).then_inc(s["sil"], 1)
                act.wait_ge(s["yt_ps"], e + 1)
                act.wait_ge(s["yw_free"], e + 1)
                A(yw[0:C, :], ps[0:C, 6 * 512:8 * 512], ACT.Copy, scale=gates[0:C, bass.ds(e, 1)]).then_inc(s["yw_ok"], 1)
            for t in range(TT):
                act.wait_ge(s[f"ld_acc{t}"], 16)
                A(g1b_junk, x[:, t, :], ACT.Square, accum_out=ss[:, t:t + 1]).then_inc(s["fsq"], 1)
                act.wait_ge(s["fsq"], t + 1)
                A(rs[:, t:t + 1], ss[:, t:t + 1], ACT.Sqrt, scale=1.0 / D, bias=ss[:, 5:6]).then_inc(s["fsr"], 1)

        @block.vector
        def _(dve):
            v = nc.vector
            v.memset(ss[:, 5:6], EPS).then_inc(s["gcol_ok"], 1)
            dve.wait_ge(s["vecT_ps"], 1)
            v.tensor_copy(vec[:, :], bank(7, 128, 128 + VR)).then_inc(s["vecT_sb"], 1)
            v.tensor_copy(cw, bank(6, 256, 256 + CT * W).rearrange("p (c w) -> p c w", c=CT)).then_inc(s["vecT_sb"], 1)
            dve.wait_ge(s["tr_ctx"], 1)
            v.tensor_copy(kr[0:DR, 0:CTX], bank(4, 0, CTX, DR)).then_inc(s["ctx_sb"], 1)
            v.tensor_copy(ckvT[:, :, 0:CTX], bank(5).rearrange("p (k n) -> p k n", k=KC)).then_inc(s["ctx_sb"], 1)
            dve.wait_ge(s["rstdx_s"], 1)
            v.reciprocal(rs[:, 0:TT], rs[:, 0:TT]).then_inc(s["rstdx"], 1)
            dve.wait_ge(s["rstdx"], 1)
            for t in range(TT):
                v.tensor_scalar(x[:, t, :], x[:, t, :], rs[:, t:t + 1], None, ALU.mult).then_inc(s["xn_ok"], 1)
            dve.wait_ge(s["mod_ps"], 4)
            v.tensor_tensor(modc[:, 0:16, :], bank(7, 0, 32).rearrange("p (m g) -> p m g", g=2),
                            vec[:, V_BM:V_BM + 16].unsqueeze(2).broadcast_to([P, 16, 2]), ALU.add).then_inc(s["mod1"], 1)
            dve.wait_ge(s["mod1"], 1)
            v.scalar_tensor_tensor(out=A1, in0=modc[:, 8:16, :], scalar=1.0,
                                   in1=vec[:, V_AG:V_AG + 8].unsqueeze(2).broadcast_to([P, 8, 2]),
                                   op0=ALU.add, op1=ALU.mult).then_inc(s["a1_ok"], 1)
            dve.wait_ge(s["a1_ok"], 1)
            for k in range(1, KD, 2):
                dve.wait_ge(s["hT_ps"], k + 1)
                v.tensor_scalar(hT[:, k, 0:NS], bank(2), A1[:, k, 0:1], modc[:, k, 0:1], ALU.mult, ALU.add)
                v.tensor_scalar(hT[:, k, NS:NT], bank(3, 0, NP), A1[:, k, 1:2], modc[:, k, 1:2],
                                ALU.mult, ALU.add).then_inc(s["hTd"], 1)
            n = 0
            for cc in range(CT):
                dve.wait_ge(s["glu_mul"], cc + 1)
                if cc == 0:
                    dve.wait_ge(s["sqx"], TT)
                for w in range(W):
                    src = gluv[:, cc, w:w + CW]
                    if w == 0:
                        o = v.tensor_scalar(mixC[:, cc, :], src, cw[:, cc, 0:1], vec[:, V_CB + cc:V_CB + cc + 1],
                                            ALU.mult, ALU.add)
                    else:
                        dve.wait_ge(s["conv_ops"], n)
                        o = v.scalar_tensor_tensor(out=mixC[:, cc, :], in0=src, scalar=cw[:, cc, w:w + 1],
                                                   in1=mixC[:, cc, :], op0=ALU.mult, op1=ALU.add)
                    if w < W - 1:
                        o.then_inc(s["conv_ops"], 1)
                        n += 1
                    else:
                        o.then_inc(s["conv_done"], 1)
            dve.wait_ge(s["qs_s"], 1)
            v.reciprocal(rq[:, 0:TT], rq[:, 0:TT]).then_inc(s["qs_r"], 1)
            dve.wait_ge(s["qs_r"], 1)
            v.tensor_scalar(rq[:, 0:TT], rq[:, 0:TT], float(DQK) ** -0.5, None, ALU.mult).then_inc(s["qs_r"], 1)
            dve.wait_ge(s["kvs_r"], 2)
            v.reciprocal(sq[:, 2, :], sq[:, 2, :]).then_inc(s["kvr"], 1)
            dve.wait_ge(s["kvr"], 1)
            for j in range(KC):
                v.scalar_tensor_tensor(out=ckvT[:, j, CTX:NK], in0=ckvT[:, j, CTX:NK], scalar=vec[:, V_KG + j:V_KG + j + 1],
                                       in1=sq[:, 2, :], op0=ALU.mult, op1=ALU.mult).then_inc(s["ckv_ok"], 1)
            dve.wait_ge(s["rotk"], 1)
            v.tensor_tensor(kr[0:DR, CTX:KS], kr[0:DR, CTX:KS], cos[0:DR, :], ALU.mult).then_inc(s["rk_step"], 1)
            v.tensor_tensor(rt[0:DR, :], bank(5, 0, NS, DR), sin[0:DR, :], ALU.mult).then_inc(s["rk_step"], 1)
            dve.wait_ge(s["rk_step"], 2)
            v.tensor_tensor(kr[0:DR, CTX:KS], kr[0:DR, CTX:KS], rt[0:DR, :], ALU.add).then_inc(s["krt"], 1)
            dve.wait_ge(s["krt"], 1)
            dve.wait_ge(s["ckv_ok"], KC)
            v.tensor_copy(kT[DN:DQK, :, :], kr[0:DR, :].unsqueeze(1).broadcast_to([DR, H, NK])).then_inc(s["kT_rope"], 1)
            dve.wait_ge(s["mod_ps"], HALF)
            v.tensor_tensor(modc[:, 16:48, :], bank(7, 32, 96).rearrange("p (m g) -> p m g", g=2),
                            vec[:, V_BM + 16:V_BM + 48].unsqueeze(2).broadcast_to([P, 32, 2]), ALU.add).then_inc(s["mod2"], 1)
            dve.wait_ge(s["mod2"], 1)
            v.scalar_tensor_tensor(out=A2, in0=modc[:, 32:40, :], scalar=1.0,
                                   in1=vec[:, V_FG:V_FG + 8].unsqueeze(2).broadcast_to([P, 8, 2]),
                                   op0=ALU.add, op1=ALU.mult).then_inc(s["a2_ok"], 1)
            for r in range(2):
                dve.wait_ge(s["rotq"], r + 1)
                v.tensor_tensor(qr[:, r, 0:NS], qr[:, r, 0:NS], cos, ALU.mult).then_inc(s["rq_step"], 1)
                v.tensor_tensor(rt, bank(6 - r), sin, ALU.mult).then_inc(s["rq_step"], 1)
                dve.wait_ge(s["rq_step"], 3 * r + 2)
                v.tensor_tensor(qr[:, r, 0:NS], qr[:, r, 0:NS], rt, ALU.add).then_inc(s["rq_step"], 1)
                dve.wait_ge(s["rq_step"], 3 * r + 3)
            dve.wait_ge(s["ln_mean"], 1)
            for k in range(CT):
                v.scalar_tensor_tensor(out=mixC[:, k, 0:NS], in0=bank(4), scalar=-1.0 / CC, in1=mixC[:, k, 0:NS],
                                       op0=ALU.mult, op1=ALU.add)
                v.scalar_tensor_tensor(out=mixC[:, k, NS:CW], in0=bank(7, 0, CW - NS), scalar=-1.0 / CC,
                                       in1=mixC[:, k, NS:CW], op0=ALU.mult, op1=ALU.add).then_inc(s["ln_d"], 1)
            dve.wait_ge(s["ln_s"], 2)
            v.reciprocal(rv, rv).then_inc(s["ln_r"], 1)
            dve.wait_ge(s["ln_r"], 1)
            dve.wait_ge(s["ln_sq"], CT)
            for k in range(CT):
                v.tensor_tensor(mixC[:, k, :], mixC[:, k, :], rv, ALU.mult).then_inc(s["ln_n"], 1)
            dve.wait_ge(s["nk_ps"], 1)
            v.tensor_copy(ost, bank(4, 0, 288)).then_inc(s["nk_sb"], 1)

            def maxima(u):
                t = u % TT
                n = KS if t < 4 else NP
                dve.wait_ge(s["s_ps"], u + 1)
                if u >= 2:
                    dve.wait_ge(s["exp_ok"], u - 1)
                v.reduce_max(mx[:, u % 2:u % 2 + 1], bank(2 * (u % 2), 0, n), AX).then_inc(s["smax"], 1)
                dve.wait_ge(s["smax"], u + 1)
                v.tensor_scalar(nb[:, u % 2:u % 2 + 1], mx[:, u % 2:u % 2 + 1], rq[:, t:t + 1], -1.0,
                                ALU.mult, ALU.mult).then_inc(s["nb_ok"], 1)

            def output(u):
                h, t = divmod(u, TT)
                dve.wait_ge(s["pv_ps"], u + 1)
                dve.wait_ge(s["rin_ok"], u + 1)
                v.tensor_scalar(On[:, t, h * DV:(h + 1) * DV], bank(6 + u % 2, 0, DV), rin[:, u % 2:u % 2 + 1], None,
                                ALU.mult).then_inc(s["o_ok"], 1)

            dve.wait_ge(s["qs_r"], 2)
            maxima(0)
            for u in range(H * TT):
                if u + 1 < H * TT:
                    maxima(u + 1)
                dve.wait_ge(s["exp_ok"], u + 1)
                if u >= 2:
                    dve.wait_ge(s["o_ok"], u - 1)
                v.reciprocal(rin[:, u % 2:u % 2 + 1], psm[:, u % 2:u % 2 + 1]).then_inc(s["rin_ok"], 1)
                if u % TT < 4:
                    dve.wait_ge(s["t_ps"], u + 1)
                    if u >= 2:
                        dve.wait_ge(s["pv_ps"], u - 1)
                    v.tensor_copy(PT[:, u % 2, 512:KS], bank(5, 0, KS - 512)).then_inc(s["ptd"], 1)
                if u >= 1:
                    output(u - 1)
            output(H * TT - 1)
            for k in (1, 3):
                dve.wait_ge(s["at_ps"], k + 1)
                v.tensor_copy(mixA[:, k, 0:NS], bank(2))
                v.tensor_copy(mixA[:, k, NS:NT], bank(3, 0, NP)).then_inc(s["atd"], 1)

            order = [4, 0, 1, 2, 3]
            dve.wait_ge(s["g1_sb"], 4)

            def residual(i):
                t = order[i]
                g = 1 if t == 4 else 0
                dve.wait_ge(s["op_ps"], i + 1)
                dve.wait_ge(s[f"ld_x{t}"], 32)
                for n in range(2):
                    c = slice(n * 512, (n + 1) * 512)
                    if i >= 1:
                        dve.wait_ge(s["x1_ok"], 2 * i)
                    v.tensor_tensor(gtmp[:, n, :], bank(2 * (i % 2) + n), g1b[:, g, c], ALU.mult).then_inc(s["g1m"], 1)
                for n in range(2):
                    c = slice(n * 512, (n + 1) * 512)
                    dve.wait_ge(s["g1m"], 2 * i + n + 1)
                    v.tensor_tensor(x[:, t, c], x[:, t, c], gtmp[:, n, :], ALU.add).then_inc(s["x1_ok"], 1)
                dve.wait_ge(s["x1s"], i + 1)
                v.reciprocal(rs[:, t:t + 1], rs[:, t:t + 1]).then_inc(s["x1r"], 1)
                dve.wait_ge(s["x1r"], i + 1)
                if i >= 2:
                    dve.wait_ge(s["xt_ps"], i - 1)
                    dve.wait_ge(s[f"out_hn{i - 2}"], 16)
                dve.wait_ge(s["x1_ok"], 2 * (i + 1))
                v.tensor_scalar(xn2[:, i % 2, :], x[:, t, :], rs[:, t:t + 1], None, ALU.mult).then_inc(s["x1n"], 1)

            def h2(i):
                g = 1 if order[i] == 4 else 0
                dve.wait_ge(s["xt_ps"], i + 1)
                if i >= 2:
                    dve.wait_ge(s["lg_ps"], i - 1)
                for k in range(4, KD):
                    v.tensor_scalar(h2T[:, i % 2, k, :], bank(5, (k - 4) * P, (k - 3) * P), A2[:, k, g:g + 1],
                                    modc[:, 24 + k, g:g + 1], ALU.mult, ALU.add).then_inc(s["h2d"], 1)

            def softmax_in(i):
                dve.wait_ge(s["lg_ps"], i + 1)
                if i >= 2:
                    dve.wait_ge(s["lexp"], i - 1)
                v.tensor_reduce(sm[:, i % 2:i % 2 + 1], bank(6, 0, E), AX, ALU.max, negate=True).then_inc(s["lmax"], 1)

            def softmax_out(i):
                dve.wait_ge(s["lexp"], i + 1)
                v.reciprocal(sm[:, 4 + i % 2:5 + i % 2], sm[:, 2 + i % 2:3 + i % 2]).then_inc(s["lrec"], 1)
                dve.wait_ge(s["lrec"], i + 1)
                if i >= 2:
                    dve.wait_ge(s["aff_ps"], i - 1)
                v.tensor_scalar(affn[:, i % 2, :], aff[:, i % 2, :], sm[:, 4 + i % 2:5 + i % 2], None,
                                ALU.mult).then_inc(s["affn_ok"], 1)

            def aff_out(i):
                t = order[i]
                dve.wait_ge(s["aff_ps"], i + 1)
                v.tensor_copy(affT[:, t * P:(t + 1) * P], bank(7, 0, P, E)).then_inc(s["affT_ok"], 1)

            top = [0]

            def choose(src, o, rounds):
                for r in range(rounds):
                    best = topv[:, o + 8 * r:o + 8 * r + 8]
                    v.max(best, src).then_inc(s["topk"], 1)
                    dve.wait_ge(s["topk"], top[0] + 1)
                    v.max_index(topi[:, o + 8 * r:o + 8 * r + 8], best, src).then_inc(s["topk"], 1)
                    dve.wait_ge(s["topk"], top[0] + 2)
                    v.match_replace(src, best, src, -1.0).then_inc(s["topk"], 1)
                    dve.wait_ge(s["topk"], top[0] + 3)
                    top[0] += 3

            dve.wait_ge(s["a2_ok"], 1)
            for i in range(TT):
                residual(i)
                if i >= 1:
                    h2(i - 1)
                if i >= 2:
                    softmax_in(i - 2)
                    softmax_out(i - 2)
                if i >= 3:
                    aff_out(i - 3)
                if i == 3:
                    dve.wait_ge(s["affT_ok"], 1)
                    choose(affT[:, NS:NT], CS, CP // 8)
            softmax_in(3)
            softmax_out(3)
            aff_out(2)
            h2(4)
            aff_out(3)
            softmax_in(4)
            softmax_out(4)
            aff_out(4)
            dve.wait_ge(s["affT_ok"], TT)
            choose(affT[:, 0:NS], 0, CS // 8)
            v.tensor_copy(topf[:, 0:CS], topi[:, 0:CS]).then_inc(s["sel"], 1)
            v.tensor_scalar(topf[:, CS:C], topi[:, CS:C], float(NS), None, ALU.add).then_inc(s["sel"], 1)
            dve.wait_ge(s["sel_ps"], 1)
            v.tensor_copy(idxc[0:C, :], bank(5, 0, E, C)).then_inc(s["sel_sb"], 1)
            v.tensor_copy(gates[0:C, :], bank(5, E, 2 * E, C)).then_inc(s["sel_sb"], 1)

            def two(b):
                return ps[:, b * 512:(b + 2) * 512].rearrange("p (b n) -> p b n", b=2)[:, :, 0:4 * C]

            def half(t):
                return t.rearrange("p (b f) n -> p b (f n)", b=2)

            dve.wait_ge(s["full_ok"], 6)
            with dve.Fori(0, E) as e:
                dve.wait_ge(s["xt2_ps"], e + 1)
                v.tensor_tensor(half(xmod), two(6), half(A2f), ALU.mult).then_inc(s["xm1"], 1)
                dve.wait_ge(s["xm1"], e + 1)
                v.tensor_tensor(xsT, xmod, S2f, ALU.add).then_inc(s["xs_ok"], 1)
                dve.wait_ge(s["sil"], e + 1)
                dve.wait_ge(s["u_ps"], e + 1)
                v.tensor_tensor(half(eh), two(2), half(esil), ALU.mult).then_inc(s["h_ok"], 1)
                dve.wait_ge(s["y_ps"], e + 1)
                v.tensor_tensor(half(yT), two(4), half(G2f), ALU.mult).then_inc(s["yT_ok"], 1)
            dve.wait_ge(s["ld_fg"], 16)
            for t in range(TT):
                dve.wait_ge(s["fsr"], t + 1)
                v.reciprocal(rs[:, t:t + 1], rs[:, t:t + 1]).then_inc(s["frec"], 1)
                dve.wait_ge(s["frec"], t + 1)
                v.scalar_tensor_tensor(out=x[:, t, :], in0=x[:, t, :], scalar=rs[:, t:t + 1], in1=fgb, op0=ALU.mult,
                                       op1=ALU.mult).then_inc(s["fin_ok"], 1)

        @block.gpsimd
        def _(pool):
            g_ = nc.gpsimd
            for o, n in ((0, PAD), (PAD + NS, PAD), (2 * PAD + NT, PAD)):
                last = g_.memset(gluv[:, :, o:o + n], 0.0)
            last.then_inc(s["glu_pad"], 1)
            for cc in range(CT):
                pool.wait_ge(s["ev"], 2 * cc + 2)
                g_.tensor_tensor(gluv[:, cc, PAD:PAD + NS], gluv[:, cc, PAD:PAD + NS], sq[:, cc % 2, 0:NS], ALU.mult)
                o = 2 * PAD + NS
                g_.tensor_tensor(gluv[:, cc, o:o + NP], gluv[:, cc, o:o + NP], sq[:, cc % 2, NS:NT],
                                 ALU.mult).then_inc(s["glu_mul"], 1)
            pool.wait_ge(s["glu_mul"], CT)
            for i in range(QC + KC):
                pool.wait_ge(s["ev"], 9 + i)
                if 3 <= i < QC:
                    pool.wait_ge(s["qst"], i - 2)
                if i >= QC:
                    pool.wait_ge(s["qst"], QC)
                src = qlat[:, i, :] if i < QC else ckvT[:, i - QC, CTX:NK]
                g_.tensor_tensor(sq[:, i % 3, :], src, src, ALU.mult).then_inc(s["sq_ok"], 1)
                if i == 2:
                    pool.wait_ge(s["ld_wq"], 32 * QC)
                    for k in range(QC):
                        last = g_.tensor_scalar(wq[:, k, :], wq[:, k, :], vec[:, V_QG + k:V_QG + k + 1], None,
                                                ALU.mult)
                    last.then_inc(s["wq_ok"], 1)
            for k in range(CT):
                pool.wait_ge(s["ln_d"], k + 1)
                g_.tensor_tensor(dsq[:, k, :], mixC[:, k, :], mixC[:, k, :], ALU.mult).then_inc(s["ln_sq"], 1)
            pool.wait_ge(s["nk_sb"], 1)
            pool.dma_start(new_ckv[0, 0], ost[:, 0:KR]).then_inc(s["out_kv"], 16)
            pool.dma_start(new_krope[0, 0], ost[:, KR:KR + DR]).then_inc(s["out_kv"], 16)
            for n in range(16):
                if n >= 2:
                    pool.wait_ge(s["g1_ps"], n - 1)
                g, k = divmod(n, KD)
                g_.tensor_scalar(diag[:, n % 2, :], ident, modc[:, 16 + k, g:g + 1], None, ALU.mult).then_inc(s["diag_ok"], 1)
            pool.wait_ge(s["at_ps"], 4)
            pool.wait_ge(s["a2_ok"], 1)
            for dst, src in ((A2f, A2), (S2f, modc[:, 24:32, :]), (G2f, modc[:, 40:48, :])):
                for g, lo, hi in ((0, 0, CS), (1, CS, C)):
                    g_.tensor_copy(dst[:, :, lo:hi], src[:, :, g:g + 1].broadcast_to([P, KD, hi - lo])).then_inc(s["full_ok"], 1)
            pool.wait_ge(s["out_kv"], 32)
            pool.dma_start(fgb, final_norm_g.rearrange("(o n) -> o n", o=1).broadcast_to([P, D])).then_inc(s["ld_fg"], 16)
            def scatter(e):
                pool.wait_ge(s["yw_ok"], e + 1)
                g_.indirect_dma_start(acc_d, bass.IndirectOffsetOnAxis(ap=idxc[0:C, e:e + 1], axis=0), yw[0:C, :], None,
                                      compute_op=ALU.add).then_inc(s["scat"], 16)
                pool.wait_ge(s["scat"], 16 * (e + 1))
                g_.memset(flag[:, :], 0.0).then_inc(s["yw_free"], 1)

            pool.wait_ge(s["sel_sb"], 2)
            for i in range(TT):
                pool.wait_ge(s[f"out_hn{i}"], 16)
            pool.wait_ge(s["out_x1"], 16 * TT)
            g_.memset(flag[:, :], 0.0).then_inc(s["yw_free"], 1)
            for e in range(E):
                if e >= 1:
                    pool.wait_ge(s["xt2_ps"], e)
                g_.indirect_dma_start(xg[0:C, :], None, hn_d, bass.IndirectOffsetOnAxis(ap=idxc[0:C, e:e + 1], axis=0)).then_inc(s["gath"], 16)
                if e >= 1:
                    scatter(e - 1)
            scatter(E - 1)


_INS = ["x_prompt", "x_sample", "cache_ckv", "cache_krope", "c", "c_ctx", "w_mod", "b_mod", "attn_norm_g", "w_in",
        "q_norm_g", "w_q_up", "kv_norm_g", "w_kv_up", "conv_w", "conv_b", "conv_ln_g", "conv_ln_b", "w_out",
        "ffn_norm_g", "w_router", "w_gate", "w_up", "w_down", "final_norm_g"]
_OUTS = [(1, 128, 1024), (1, 512, 1024), (1, 1, 128, 256), (1, 1, 128, 32)]


def _tables():
    import numpy as _np
    t = _np.zeros((128, 1408), _np.float32)
    t[:, 0:128] = _np.eye(128)
    t[:, 128:256] = 1.0
    for m in range(128):
        if m % 16 < 8:
            t[m + 8, 256 + m] = -1.0
        else:
            t[m - 8, 256 + m] = 1.0
    inv = (1.0 / (_np.float32(10000.0) ** (_np.arange(0, 16, 2, dtype=_np.float32) / _np.float32(16)))).astype(_np.float32)
    pos = _np.arange(512)
    f = _np.arange(128) % 32
    where = _np.where(f[:, None] < 16, pos[None, :] // 64, pos[None, :] % 64).astype(_np.float32)
    ang = (where * inv[f % 8][:, None]).astype(_np.float32)
    t[:, 384:896] = _np.cos(ang)
    t[:, 896:1408] = _np.sin(ang)
    return t


def kernel(**inputs):
    import numpy as _np
    import concourse.bacc as _bacc
    from concourse import mybir as _mybir
    from concourse.bass_utils import run_bass_kernel_spmd as _run

    nc = _bacc.Bacc("TRN2", target_bir_lowering=False, num_devices=1, dynamic_dma_scratch_size=4096)
    arrays, args = {}, []
    for name in _INS:
        a = _np.ascontiguousarray(inputs[name])
        arrays[f"in_{name}_dram"] = a
        args.append(nc.dram_tensor(f"in_{name}_dram", a.shape, _mybir.dt.from_np(a.dtype), kind="ExternalInput").ap())
    arrays["in_tables_dram"] = _tables()
    args.append(nc.dram_tensor("in_tables_dram", (128, 1408), _mybir.dt.float32, kind="ExternalInput").ap())
    for i, shape in enumerate(_OUTS):
        args.append(nc.dram_tensor(f"out_{i}_dram", shape, _mybir.dt.float32, kind="ExternalOutput").ap())
    layer(nc, *args)
    r = _run(nc, [arrays], core_ids=[0])
    return tuple(r.results[0][f"out_{i}_dram"] for i in range(len(_OUTS)))
```

```python
from contextlib import ExitStack

import concourse.bass as bass
from concourse import mybir

F32 = mybir.dt.float32
U32 = mybir.dt.uint32
ALU = mybir.AluOpType
ACT = mybir.ActivationFunctionType
AX = mybir.AxisListType.X

P = 128
D = 1024
KD = D // P
NS, NP = 512, 128
NT = NS + NP
TT = NT // P
CTX = 256
NK = CTX + NT
KS = CTX + NS
H, DN, DR, DV = 8, 64, 32, 64
DQK = DN + DR
QR, KR, CC, W = 768, 256, 512, 31
QC, KC, CT = QR // P, KR // P, CC // P
GRID = 64
E, F = 16, 1024
CS, CP = 2 * NS // E, 2 * NP // E
C = CS + CP
EPS = 1e-6
PAD = (W - 1) // 2
GW = PAD + NS + PAD + NP + PAD
CW = NS + PAD + NP
CP0 = NS + PAD

V_C, V_CCTX, V_AG, V_FG, V_QG, V_KG, V_CB, V_LG, V_LB, V_BM = 0, 8, 16, 24, 32, 38, 40, 44, 48, 52
VR = V_BM + 48
NMOD = 6
HALF = 12

SLOT = 4 * F
SLOTS = 6


def layer(nc, x_prompt, x_sample, cache_ckv, cache_krope, c, c_ctx, w_mod, b_mod, attn_norm_g, w_in,
          q_norm_g, w_q_up, kv_norm_g, w_kv_up, conv_w, conv_b, conv_ln_g, conv_ln_b, w_out, ffn_norm_g,
          w_router, w_gate, w_up, w_down, final_norm_g, tables, y_prompt, y_sample, new_ckv, new_krope):
    ctx = ExitStack()
    with ctx:
        def sb(name, n, dt=F32):
            return ctx.enter_context(nc.sbuf_tensor(name, [P, n], dt))

        def sem(name):
            return ctx.enter_context(nc.semaphore(name))

        ring = sb("ring", SLOTS * SLOT)
        wglu = ring[:, 0:8 * 2 * CC].rearrange("p (k n) -> p k n", k=KD)
        wq = ring[:, 0:QC * 768].rearrange("p (k n) -> p k n", k=QC)
        V = ring[:, 4608:4608 + 7 * 512].rearrange("p (t n) -> p t n", t=7)
        winq = ring[:, 8192:8192 + 6144].rearrange("p (k n) -> p k n", k=KD)
        kT = ring[:, 8192:8192 + H * NK].rearrange("p (h n) -> p h n", h=H)
        sq = ring[:, 14336:14336 + 3 * NT].rearrange("p (b n) -> p b n", b=3)
        wm_c = ring[:, 16384:20480].rearrange("p (k n) -> p k n", k=KD)
        wm_a = ring[:, 20480:24576].rearrange("p (k n) -> p k n", k=KD)
        wout = ring[:, 16384:24576].rearrange("p (k n) -> p k n", k=KD)

        xr = sb("x_region", 5120)
        x = xr[:, :].rearrange("p (t n) -> p t n", t=TT)
        QT = xr[:, :].rearrange("p (h n) -> p h n", h=H)
        wm_x = xr[:, 0:4096].rearrange("p (k n) -> p k n", k=KD)
        hr = sb("h_region", 5120)
        hT = hr[:, :].rearrange("p (k n) -> p k n", k=KD)
        wm_h = hr[:, 0:4096].rearrange("p (k n) -> p k n", k=KD)
        qr = hr[:, 0:2 * NT].rearrange("p (r n) -> p r n", r=2)
        rt = hr[:, 1280:1280 + NS]
        dsq = hr[:, 1792:1792 + CT * CW].rearrange("p (c n) -> p c n", c=CT)
        rv = hr[:, 4412:4412 + CW]
        xn2 = hr[:, 0:2048].rearrange("p (b n) -> p b n", b=2)
        gtmp = hr[:, 2048:3072].rearrange("p (b n) -> p b n", b=2)
        h2T = hr[:, 3072:5120].rearrange("p (b k n) -> p b k n", b=2, k=KD)
        mar = sb("mix_attn", 4 * NT)
        mixA = mar[:, :].rearrange("p (k n) -> p k n", k=4)
        modr = mar[:, 0:1024].rearrange("p (b n) -> p b n", b=2)
        diag = mar[:, 1024:2048].rearrange("p (b k n) -> p b k n", b=2, k=4)
        q_rows = mar[:, 0:NT]
        mixC = sb("mix_conv", CT * CW)[:, :].rearrange("p (k n) -> p k n", k=CT)
        qlr = sb("q_latent", QC * NT)
        qlat = qlr[:, :].rearrange("p (k n) -> p k n", k=QC)
        PT = [r[:, 0:3072].rearrange("p (k a n) -> p k a n", k=6, a=2) for r in (hr, qlr)]
        ckr = sb("ckv", KC * NK)
        ckvT = ckr[:, :].rearrange("p (k n) -> p k n", k=KC)
        kr = sb("krope", NK)
        gvr = sb("glu_value", CT * GW)
        gluv = gvr[:, :].rearrange("p (c n) -> p c n", c=CT)
        g1b = gvr[:, 0:2 * D].rearrange("p (g n) -> p g n", g=2)
        wkr = sb("w_kv", KC * 1024)
        wkv = wkr[:, :].rearrange("p (k n) -> p k n", k=KC)
        wikr = sb("w_in_kv", KD * 288)
        winkv = wikr[:, :].rearrange("p (k n) -> p k n", k=KD)
        Pb = wikr[:, 0:1536].rearrange("p (b n) -> p b n", b=2)
        cachek = Pb[:, 0, 0:512].rearrange("p (t n) -> p t n", t=2)
        cacher = Pb[:, 0, 512:576].rearrange("p (t n) -> p t n", t=2)
        vrow = Pb[:, 0, 576:704]
        cwrow = wikr[:, 768:768 + CC]
        tab = sb("tables", 384 + 1024)
        ident, ones, rotm = tab[:, 0:128], tab[:, 128:256], tab[:, 256:384]
        cos, sin = tab[:, 384:896], tab[:, 896:1408]
        vec = sb("vectors", VR)
        cw = sb("conv_taps", CT * W)[:, :].rearrange("p (c w) -> p c w", c=CT)
        cact = sb("cond_silu", KD * 32)[:, :].rearrange("p (k n) -> p k n", k=KD)
        modt = sb("mod_parts", 48 * 8)[:, :].rearrange("p (m n) -> p m n", m=48)
        modc = sb("modulation", 96)[:, :].rearrange("p (m g) -> p m g", g=2)
        A1 = sb("scale1", 16)[:, :].rearrange("p (k g) -> p k g", g=2)
        A2 = sb("scale2", 16)[:, :].rearrange("p (k g) -> p k g", g=2)
        ss = sb("sum_squares", 8)
        rs = sb("rstd", 8)
        rq = sb("rstd_q", 8)
        mx = sb("row_max", 2)
        nb = sb("exp_bias", 2)
        psm = sb("exp_sum", 2)
        rin = sb("exp_sum_inv", 2)
        wr = sb("w_router", KD * E)[:, :].rearrange("p (k n) -> p k n", k=KD)
        aff = sb("affinity", 2 * E)[:, :].rearrange("p (b n) -> p b n", b=2)
        affn = sb("affinity_n", 2 * E)[:, :].rearrange("p (b n) -> p b n", b=2)
        sm = sb("router_stats", 8)
        idxf = sb("choice_f", E)
        idxc = sb("choice", E, U32)
        gates = sb("gates", E)
        flag = sb("flag", 1)
        xg = wkr[:, 0:D]
        G2r = wkr[:, D:2 * D]
        yw = xr[:, 3968:3968 + D]
        A2f = ckr[:, 0:KD * C].rearrange("p (k n) -> p k n", k=KD)
        S2f = ckr[:, 640:640 + KD * C].rearrange("p (k n) -> p k n", k=KD)
        fgb = qlr[:, D:2 * D]
        esil = xr[:, 0:D]
        eh = xr[:, D:2 * D]
        xsT = xr[:, 2048:2048 + KD * C].rearrange("p (k n) -> p k n", k=KD)
        ehT = xr[:, 2688:2688 + KD * C].rearrange("p (k n) -> p k n", k=KD)
        xmod = xr[:, 3328:3328 + KD * C].rearrange("p (k n) -> p k n", k=KD)
        grp = wikr[:, 1824:1824 + 2 * C].rearrange("p (g n) -> p g n", g=2)
        affT = kr[0:E, 0:NT]
        topv = ckr[0:E, 1280:1280 + C]
        topi = ckr[0:E, 1360:1360 + C].bitcast(U32)
        topf = ckr[0:E, 1440:1440 + C]
        ost = wikr[:, 1536:1536 + 288]

        ps = ctx.enter_context(nc.psum_tensor("ps", [P, 8 * 512], F32))

        def bank(b, lo=0, hi=512, p=P, p0=0):
            return ps[p0:p, b * 512 + lo:b * 512 + hi]

        def two_banks(b, n):
            return ps[:, b * 512:(b + 2) * 512].rearrange("p (b n) -> p b n", b=2)[:, :, 0:n]

        def halves(t):
            return t.rearrange("p (b f) n -> p b (f n)", b=2)

        acc_d = nc.dram_tensor("residual", [NT, D], F32, kind="Internal").ap()
        hn_d = nc.dram_tensor("normed", [NT, D], F32, kind="Internal").ap()

        names = """ld_small ld_cache ld_x0 ld_x1 ld_x2 ld_x3 ld_x4 ld_glu ld_winq ld_winkv ld_wkv ld_wq ld_wout
        ld_router ld_fg vecT_ps vecT_sb cact_ok sqx rstdx_s rstdx xn_ok mod_ps mod1 mod2 a1_ok hT_ps hTa hTd
        tr_ctx ctx_sb glu_pad glu_mul conv_ops conv_done pj ev sq_ok qst kvs kvs_r kvr qrow_ok qcol ckv_ok rotk krt kT_rope
        rk_step wq_ok rotq rq_step rope_a ln_mean ln_d ln_sq ln_var ln_s ln_r ln_n ln_out qs_s qs_r qu_done
        nk_ps nk_sb out_kv diag_ok g1_ps g1_sb s_ps smax nb_ok exp_ok t_ps pta ptd pv_ps rin_ok pn_ok ata cact_z mraw_sb mT_ps mT_sb red1 red2 g2_ps g2_sb grp_ok
        op_ps g1m x1_ok x1sq x1s x1r x1n out_x1 out_hn0 out_hn1 out_hn2 out_hn3 out_hn4 xt_ps h2a h2d lg_ps lmax lexp lrec affn_ok aff_ps affT_ok
        topk sel sel_ps sel_sb full_ok sm_free a2_ok
        gath xt2_ps xm1 xs_ok a_ps u_ps sil h_ok hT_tr hT_ok y_ps yw_ok yw_free scat
        ld_acc0 ld_acc1 ld_acc2 ld_acc3 ld_acc4 fsq fsr frec fin_ok out_y gcol_ok""".split()
        s = {n: sem(n) for n in names}
        wmod_ld = [sem(f"wmod_ld{j}") for j in range(4)]
        slot_ld = [sem(f"slot_ld{j}") for j in range(SLOTS)]

        block = ctx.enter_context(nc.Block())

        wmod_v = w_mod[0].rearrange("(k p) n -> p k n", p=P)
        win_v = w_in[0].rearrange("(k p) n -> p k n", p=P)
        wm_buf = [wm_a, wm_c, wm_h, wm_a] + [[wm_c, wm_x, wm_a][j % 3] for j in range(8)]
        wm_sem = [0, 1, 2, 0] + [[1, 3, 0][j % 3] for j in range(8)]
        wm_cnt = [16 * (wm_sem[:j + 1].count(wm_sem[j])) for j in range(HALF)]
        wm_prev = [max([i for i in range(j) if wm_sem[i] == wm_sem[j]], default=None) for j in range(HALF)]

        HN = NT // 2
        HK = NK // 2
        CH = (CW + 1) // 2

        groups = [(hp, ts) for hp in range(H // 2) for ts in ((0, 1), (2, 3), (4,))]
        steps = [(2 * hp + a, t, n) for n, (hp, ts) in enumerate(groups) for a in range(2) for t in ts]
        U = len(steps)

        def sample_steps(u):
            return sum(t < 4 for _, t, _ in steps[:u])

        def steps_before(n):
            return sum(m < n for _, _, m in steps)

        @block.sync
        def _(sp):
            def load_mod(j):
                if wm_prev[j] is not None:
                    sp.wait_ge(s["mod_ps"], wm_prev[j] + 1)
                sp.dma_start(wm_buf[j], wmod_v[:, :, 512 * j:512 * j + 512]).then_inc(wmod_ld[wm_sem[j]], 16)

            def load_heads(dst, src, chunks, a, b, done):
                for k in range(chunks):
                    rows = src[0, k * P:(k + 1) * P, :].rearrange("p (h f) -> p h f", h=H)
                    for lo, w, col in ((0, a, 0), (a, b, H * a)):
                        sp.dma_start(dst[:, k, col:col + H * w].rearrange("p (h f) -> p h f", h=H),
                                     rows[:, :, lo:lo + w]).then_inc(done, 16)

            for j in range(3):
                load_mod(j)
            for t in range(TT):
                src = x_sample[0, t * P:(t + 1) * P, :] if t < 4 else x_prompt[0]
                sp.dma_start(x[:, t, :], src).then_inc(s[f"ld_x{t}"], 16)
            load_mod(3)
            sp.dma_start(wglu[:, :, :], win_v[:, :, 1056:2080]).then_inc(s["ld_glu"], 16)
            load_heads(wkv, w_kv_up, KC, DN, DV, s["ld_wkv"])
            load_mod(4)
            sp.dma_start(winq[:, :, :], win_v[:, :, 0:QR]).then_inc(s["ld_winq"], 16)
            sp.wait_ge(s["tr_ctx"], 1)
            sp.dma_start(winkv[:, :, :], win_v[:, :, QR:QR + 288]).then_inc(s["ld_winkv"], 16)
            sp.wait_ge(s["hT_ps"], KD)
            for j in range(5, HALF):
                load_mod(j)
                if j == 8:
                    sp.wait_ge(s["pj"], 8)
                    load_heads(wq, w_q_up, QC, DN, DR, s["ld_wq"])
            sp.wait_ge(s["mod_ps"], HALF)
            sp.dma_start(wout[:, :, :], w_out[0].rearrange("(k p) n -> p k n", p=P)).then_inc(s["ld_wout"], 16)
            sp.wait_ge(s["s_ps"], U)
            for t in [4, 0, 1, 2, 3]:
                src = x_sample[0, t * P:(t + 1) * P, :] if t < 4 else x_prompt[0]
                sp.dma_start(x[:, t, :], src).then_inc(s[f"ld_x{t}"], 16)

            def slots(e, wait):
                for n in range(SLOTS):
                    w = [w_gate, w_gate, w_up, w_up, w_down, w_down][n]
                    wait(n)
                    dst = ring[:, n * SLOT:(n + 1) * SLOT].rearrange("p (k n) -> p k n", k=4)
                    src = w[0, e].rearrange("(k p) n -> p k n", p=P) if isinstance(e, int) else \
                        w[0, bass.ds(e, 1)].rearrange("o (k p) n -> p (o k) n", p=P)
                    sp.dma_start(dst, src[:, 4 * (n % 2):4 * (n % 2) + 4, :]).then_inc(slot_ld[n], 16)

            def wait_first(n):
                if n == 0:
                    sp.wait_ge(s["pv_ps"], len(groups))
                if n == 4:
                    sp.wait_ge(s["op_ps"], TT)

            slots(0, wait_first)
            with sp.Fori(1, E) as e:
                slots(e, lambda n: sp.wait_ge(s[["a_ps", "u_ps", "y_ps"][n // 2]], e))
            sp.wait_ge(s["scat"], 16 * E)
            for t in range(TT):
                sp.dma_start(x[:, t, :], acc_d[t * P:(t + 1) * P, :]).then_inc(s[f"ld_acc{t}"], 16)
            for t in range(TT):
                sp.wait_ge(s["fin_ok"], t + 1)
                dst = y_sample[0, t * P:(t + 1) * P, :] if t < 4 else y_prompt[0]
                sp.dma_start(dst, x[:, t, :]).then_inc(s["out_y"], 16)
            sp.wait_ge(s["out_y"], 16 * TT)
            sp.wait_ge(s["out_kv"], 32)

        @block.tensor
        def _(pe):
            mm, tr = nc.tensor.matmul, nc.tensor.transpose
            pe.wait_ge(s["ld_small"], 16 * 12)
            tr(bank(7, 128, 128 + VR), vrow[0:VR, :], ident[0:VR, 0:VR])
            for k in range(CT):
                last = tr(bank(6, 256 + W * k, 256 + W * (k + 1)), cwrow[0:W, k * P:(k + 1) * P], ident[0:W, 0:W])
            last.then_inc(s["vecT_ps"], 1)
            pe.wait_ge(s["ld_cache"], 32)
            for j in range(KC):
                for t in range(2):
                    tr(bank(5, j * CTX + t * P, j * CTX + (t + 1) * P), cachek[:, t, j * P:(j + 1) * P], ident)
            for t in range(2):
                last = tr(bank(4, t * P, (t + 1) * P, DR), cacher[:, t, :], ident)
            last.then_inc(s["tr_ctx"], 1)

            def mod_bank(j):
                return j if j < 4 else 7

            def mod(j):
                if j == 0:
                    pe.wait_ge(s["cact_ok"], 1)
                if j == 4:
                    pe.wait_ge(s["vecT_sb"], 2)
                if j > 4:
                    pe.wait_ge(s["mraw_sb"], j)
                pe.wait_ge(wmod_ld[wm_sem[j]], wm_cnt[j])
                for k in range(KD):
                    q = k % 4
                    last = mm(bank(mod_bank(j), 0, 512, 32 * q + 32, 32 * q), cact[:, k, :], wm_buf[j][:, k, :],
                              start=(k < 4), stop=(k >= 4))
                last.then_inc(s["mod_ps"], 1)

            def mod_turn(j):
                pe.wait_ge(s["mraw_sb"], j + 1)
                if j == 0:
                    pe.wait_ge(s["vecT_sb"], 2)
                if j >= 1:
                    pe.wait_ge(s["mT_sb"], j)
                for m in range(4):
                    last = tr(bank(6, m * P, (m + 1) * P), modr[:, j % 2, m * P:(m + 1) * P], ident)
                last.then_inc(s["mT_ps"], 1)

            for j in range(4):
                mod(j)
                if j >= 1:
                    mod_turn(j - 1)
            mod_turn(3)
            for k in range(KD):
                if k == 0:
                    pe.wait_ge(s["xn_ok"], TT)
                    pe.wait_ge(s["mraw_sb"], 4)
                if k >= 2:
                    pe.wait_ge(s["hTa"] if k % 2 == 0 else s["hTd"], k // 2)
                for t in range(TT):
                    o = bank(2 * (k % 2), t * P, (t + 1) * P) if t < 4 else bank(2 * (k % 2) + 1, 0, P)
                    last = tr(o, x[:, t, k * P:(k + 1) * P], ident)
                last.then_inc(s["hT_ps"], 1)
            pe.wait_ge(s["hTa"], KD // 2)
            pe.wait_ge(s["hTd"], KD // 2)

            def q_stat(i):
                pe.wait_ge(s["sq_ok"], i + 1)
                if i == 0:
                    pe.wait_ge(s["ctx_sb"], 2)
                q = i % 4
                for n in range(2):
                    last = mm(bank(4 + n, 0, HN, 32 * q + 32, 32 * q), ones[:, 0:32], sq[:, i % 3, n * HN:(n + 1) * HN],
                              start=(i < 4), stop=(i + 4 >= QC))
                last.then_inc(s["qst"], 1)

            for i in range(17):
                if i >= 2:
                    pe.wait_ge(s["ev"], i - 1)
                if i == 0:
                    pe.wait_ge(s["ld_glu"], 16)
                if i == 8:
                    pe.wait_ge(s["ld_winq"], 16)
                if i == 14:
                    pe.wait_ge(s["ld_winkv"], 16)
                for lo, hi, b in ((0, HN, 2 * (i % 2)), (HN, NT, 2 * (i % 2) + 1)):
                    for k in range(KD):
                        if i < 8:
                            col = (CC if i % 2 == 0 else 0) + P * (i // 2)
                            w, M = wglu[:, k, col:col + P], P
                        elif i < 14:
                            w, M = winq[:, k, P * (i - 8):P * (i - 7)], P
                        else:
                            M = P if i < 16 else DR
                            w = winkv[:, k, P * (i - 14):P * (i - 14) + M]
                        last = mm(bank(b, 0, hi - lo, M), w, hT[:, k, lo:hi], start=(k == 0), stop=(k == KD - 1))
                last.then_inc(s["pj"], 1)
                if i % 2 == 1:
                    mod(4 + i // 2)
                elif i >= 2:
                    mod_turn(3 + i // 2)
                if 10 <= i < 16:
                    q_stat(i - 10)
            for j in range(KC):
                pe.wait_ge(s["sq_ok"], QC + j + 1)
                if j == 0:
                    pe.wait_ge(s["mT_sb"], HALF)
                    pe.wait_ge(s["mraw_sb"], HALF)
                mm(bank(6, 0, HN), ones, sq[:, j, 0:HN], start=(j == 0), stop=(j == KC - 1))
                last = mm(bank(7, 0, HN), ones, sq[:, j, HN:NT], start=(j == 0), stop=(j == KC - 1))
            last.then_inc(s["kvs"], 1)
            pe.wait_ge(s["qrow_ok"], 2)
            for t in range(TT):
                last = mm(bank(4, t, t + 1), q_rows[:, t * P:(t + 1) * P], ones[:, 0:1], start=True, stop=True)
            last.then_inc(s["qcol"], 1)

            pe.wait_ge(s["wq_ok"], 1)
            for i in range(6):
                n = 17 + i
                pe.wait_ge(s["ev"], n - 1)
                for lo, hi, b in ((0, HN, 2 * (n % 2)), (HN, NT, 2 * (n % 2) + 1)):
                    for k in range(QC):
                        w = wq[:, k, i * P:(i + 1) * P]
                        last = mm(bank(b, 0, hi - lo), w, qlat[:, k, lo:hi], start=(k == 0), stop=(k == QC - 1))
                last.then_inc(s["pj"], 1)
            pe.wait_ge(s["qrow_ok"], 2)
            pe.wait_ge(s["kvs_r"], 2)
            mm(bank(5, 0, NS, DR), rotm[0:DR, 0:DR], kr[0:DR, CTX:KS], start=True, stop=True).then_inc(s["rotk"], 1)
            pe.wait_ge(s["ev"], 22)
            mm(bank(6), rotm, qr[:, 0, 0:NS], start=True, stop=True).then_inc(s["rotq"], 1)
            pe.wait_ge(s["rk_step"], 2)
            pe.wait_ge(s["ev"], 23)
            mm(bank(5), rotm, qr[:, 1, 0:NS], start=True, stop=True).then_inc(s["rotq"], 1)
            pe.wait_ge(s["conv_done"], CT)
            pe.wait_ge(s["qs_s"], 1)
            for k in range(CT):
                mm(bank(4, 0, CH), ones, mixC[:, k, 0:CH], start=(k == 0), stop=(k == CT - 1))
                last = mm(bank(7, 0, CW - CH), ones, mixC[:, k, CH:CW], start=(k == 0), stop=(k == CT - 1))
            last.then_inc(s["ln_mean"], 1)
            pe.wait_ge(s["ckv_ok"], KC)
            pe.wait_ge(s["ld_wkv"], 32 * KC)
            for i in range(4):
                n = 23 + i
                pe.wait_ge(s["ev"], n - 1)
                for lo, hi, b in ((0, HK, 2 * (n % 2)), (HK, NK, 2 * (n % 2) + 1)):
                    for k in range(KC):
                        last = mm(bank(b, 0, hi - lo), wkv[:, k, i * P:(i + 1) * P], ckvT[:, k, lo:hi],
                                  start=(k == 0), stop=(k == KC - 1))
                last.then_inc(s["pj"], 1)
            pe.wait_ge(s["rq_step"], 6)
            pe.wait_ge(s["ln_sq"], CT)
            for k in range(CT):
                mm(bank(5, 0, CH), ones, dsq[:, k, 0:CH], start=(k == 0), stop=(k == CT - 1))
                last = mm(bank(6, 0, CW - CH), ones, dsq[:, k, CH:CW], start=(k == 0), stop=(k == CT - 1))
            last.then_inc(s["ln_var"], 1)
            for t in range(7):
                n = 27 + t
                pe.wait_ge(s["ev"], n - 1)
                for k in range(KC):
                    last = mm(bank(2 * (n % 2)), ckvT[:, k, t * P:(t + 1) * P], wkv[:, k, H * DN:],
                              start=(k == 0), stop=(k == KC - 1))
                last.then_inc(s["pj"], 1)
            pe.wait_ge(s["ln_d"], CT)
            for j in range(KC):
                tr(bank(4, j * P, (j + 1) * P), ckvT[:, j, KS:NK], ident)
            tr(bank(4, KR, KR + DR), kr[0:DR, KS:NK], ident[0:DR, 0:DR]).then_inc(s["nk_ps"], 1)
            pe.wait_ge(s["ln_s"], 2)
            for n in range(4):
                if n == 2:
                    pe.wait_ge(s["nk_sb"], 1)
                pe.wait_ge(s["diag_ok"], n + 1)
                mm(bank([5, 6, 4, 7][n]), ones, diag[:, n % 2, :, :].rearrange("p k n -> p (k n)"),
                   start=True, stop=True).then_inc(s["g1_ps"], 1)
            pe.wait_ge(s["grp_ok"], 1)
            pe.wait_ge(s["g1_sb"], 2)
            for g in range(2):
                for n in range(2):
                    pe.wait_ge(s["diag_ok"], 5 + 2 * g + n)
                    mm(bank(5 + n, 0, 512, C), grp[:, g, :], diag[:, n, :, :].rearrange("p k n -> p (k n)"),
                       start=(g == 0), stop=(g == 1)).then_inc(s["g2_ps"], 1)

            def scores(u):
                h, t, _ = steps[u]
                if u >= 2:
                    pe.wait_ge(s["exp_ok"], u - 1)
                b = 2 * (u % 2)
                q = QT[0:DQK, h, t * P:(t + 1) * P]
                if t < 4:
                    mm(bank(b, 0, KS // 2), q, kT[0:DQK, h, 0:KS // 2], start=True, stop=True)
                    mm(bank(b + 1, 0, KS // 2), q, kT[0:DQK, h, KS // 2:KS], start=True, stop=True).then_inc(s["s_ps"], 1)
                else:
                    mm(bank(b, 0, NP), q, kT[0:DQK, h, KS:NK], start=True, stop=True).then_inc(s["s_ps"], 1)

            def weighted_values(n):
                hp, ts = groups[n]
                w = P * len(ts)
                pe.wait_ge(s["pta"], steps_before(n + 1))
                pe.wait_ge(s["ptd"], sample_steps(steps_before(n + 1)))
                if n >= 2:
                    pe.wait_ge(s["ata"], n - 1)
                kts = range(6) if ts[0] < 4 else [6]
                for kt in kts:
                    for a in range(2):
                        h = 2 * hp + a
                        last = mm(bank(6 + n % 2, 0, w, 64 * a + 64, 64 * a), V[:, kt, h * DV:(h + 1) * DV],
                                  PT[n % 2][:, kt % 6, a, 0:w], start=(kt == kts[0]), stop=(kt == kts[-1]),
                                  skip_group_check=True)
                last.then_inc(s["pv_ps"], 1)

            pe.wait_ge(s["ev"], 34)
            pe.wait_ge(s["rope_a"], 8)
            pe.wait_ge(s["kT_rope"], 1)
            pe.wait_ge(s["g1_sb"], 4)
            pe.wait_ge(s["g2_sb"], 2)
            scores(0)
            scores(1)
            for u in range(U):
                h, t, n = steps[u]
                pe.wait_ge(s["pn_ok"], u + 1)
                if u >= 1:
                    pe.wait_ge(s["pta"], u)
                    pe.wait_ge(s["ptd"], sample_steps(u))
                for kt in range(6) if t < 4 else range(1):
                    last = tr(bank(4 + kt // 3, kt % 3 * P, (kt % 3 + 1) * P), Pb[:, u % 2, kt * P:(kt + 1) * P], ident)
                last.then_inc(s["t_ps"], 1)
                if u + 2 < U:
                    scores(u + 2)
                if u >= 1 and steps[u - 1][2] != n:
                    weighted_values(n - 1)
            weighted_values(len(groups) - 1)

            order = [4, 0, 1, 2, 3]

            def out_proj(i):
                t = order[i]
                if i >= 2:
                    pe.wait_ge(s["g1m"], 2 * (i - 1))
                for n in range(2):
                    for k in [4, 5, 6, 7, 0, 1, 2, 3]:
                        o = CP0 if t == 4 else t * P
                        m = mixA[:, k, t * P:(t + 1) * P] if k < 4 else mixC[:, k - 4, o:o + P]
                        last = mm(bank(2 * (i % 2) + n), m, wout[:, k, n * 512:(n + 1) * 512],
                                  start=(k == 4), stop=(k == 3))
                last.then_inc(s["op_ps"], 1)

            def x_to_features(i):
                pe.wait_ge(s["x1n"], i + 1)
                if i >= 1:
                    pe.wait_ge(s["h2a"], 4 * i)
                    pe.wait_ge(s["h2d"], 4 * i)
                for k in range(KD):
                    last = tr(bank(4 + k // 4, (k % 4) * P, (k % 4 + 1) * P), xn2[:, i % 2, k * P:(k + 1) * P], ident)
                last.then_inc(s["xt_ps"], 1)

            def router(i):
                pe.wait_ge(s["h2a"], 4 * (i + 1))
                pe.wait_ge(s["h2d"], 4 * (i + 1))
                if i >= 1:
                    pe.wait_ge(s["lexp"], i)
                for k in range(KD):
                    last = mm(bank(6, 0, E), h2T[:, i % 2, k, :], wr[:, k, :], start=(k == 0), stop=(k == KD - 1))
                last.then_inc(s["lg_ps"], 1)

            def aff_transpose(i):
                pe.wait_ge(s["affn_ok"], i + 1)
                if i >= 1:
                    pe.wait_ge(s["affT_ok"], i)
                tr(bank(7, 0, P, E), affn[:, i % 2, :], ident).then_inc(s["aff_ps"], 1)

            pe.wait_ge(s["ata"], len(groups))
            pe.wait_ge(s["ln_out"], 2 * CT)
            pe.wait_ge(s["ld_wout"], 16)
            pe.wait_ge(s["ld_router"], 16)
            for i in range(TT):
                out_proj(i)
                if i >= 1:
                    x_to_features(i - 1)
                if i >= 2:
                    router(i - 2)
                if i >= 3:
                    aff_transpose(i - 3)
            router(3)
            aff_transpose(2)
            x_to_features(4)
            aff_transpose(3)
            router(4)
            aff_transpose(4)
            pe.wait_ge(s["sel"], 2)
            tr(bank(5, 0, E, C), topf, ident[0:E, 0:E])
            tr(bank(5, E, 2 * E, C), topv, ident[0:E, 0:E]).then_inc(s["sel_ps"], 1)
            pe.wait_ge(s["sel_sb"], 2)

            def rows_to_features(e):
                pe.wait_ge(s["gath"], e * 16 + 16)
                for k in range(KD):
                    last = tr(bank(6 + k // 4, (k % 4) * C, (k % 4 + 1) * C), xg[0:C, k * P:(k + 1) * P],
                              ident[0:C, 0:C])
                last.then_inc(s["xt2_ps"], 1)

            def matrix(e, m, src, done):
                for k in range(KD):
                    if k % 4 == 0:
                        pe.wait_ge(slot_ld[2 * m + k // 4], e * 16 + 16)
                    for n in range(2):
                        o = 2 * m * SLOT + k * F + n * 512
                        last = mm(bank([0, 2, 6][m] + n, 0, 512, C), src[:, k, :], ring[:, o:o + 512],
                                  start=(k == 0), stop=(k == KD - 1))
                last.then_inc(done, 1)

            def expert(e, last_one):
                pe.wait_ge(s["xs_ok"], e + 1)
                matrix(e, 0, xsT, s["a_ps"])
                matrix(e, 1, xsT, s["u_ps"])
                if not last_one:
                    rows_to_features(e + 1)
                pe.wait_ge(s["h_ok"], e + 1)
                for k in range(KD):
                    last = tr(bank(4 + k // 4, (k % 4) * C, (k % 4 + 1) * C), eh[0:C, k * P:(k + 1) * P],
                              ident[0:C, 0:C])
                last.then_inc(s["hT_tr"], 1)
                pe.wait_ge(s["hT_ok"], e + 1)
                if not last_one:
                    pe.wait_ge(s["xs_ok"], e + 2)
                matrix(e, 2, ehT, s["y_ps"])
                pe.wait_ge(s["yw_ok"], e + 1)

            rows_to_features(0)
            with pe.Fori(0, E - 1) as e:
                expert(e, False)
            expert(E - 1, True)

        @block.scalar
        def _(act):
            A = nc.scalar.activation
            act.dma_start(tab[:, :], tables).then_inc(s["ld_small"], 16)
            rows = [(V_C, c[0], 8), (V_CCTX, c_ctx, 8), (V_AG, attn_norm_g[0], 8), (V_FG, ffn_norm_g[0], 8),
                    (V_QG, q_norm_g[0], 6), (V_KG, kv_norm_g[0], 2), (V_CB, conv_b[0], 4), (V_LG, conv_ln_g[0], 4),
                    (V_LB, conv_ln_b[0], 4), (V_BM, b_mod[0], 48)]
            for r, v, n in rows:
                act.dma_start(vrow[r:r + n, :], v.rearrange("(r n) -> r n", n=P)).then_inc(s["ld_small"], 16)
            act.dma_start(cwrow[0:W, :], conv_w[0]).then_inc(s["ld_small"], 16)
            act.dma_start(cachek, cache_ckv[0, 0].rearrange("(t p) n -> p t n", p=P)).then_inc(s["ld_cache"], 16)
            act.dma_start(cacher, cache_krope[0, 0].rearrange("(t p) n -> p t n", p=P)).then_inc(s["ld_cache"], 16)
            act.dma_start(wr, w_router[0].rearrange("(k p) n -> p k n", p=P)).then_inc(s["ld_router"], 16)
            act.wait_ge(s["vecT_sb"], 1)
            act.wait_ge(s["cact_z"], 1)
            A(cact[:, :, 0:2], vec[:, V_C:V_C + 16].rearrange("p (g k) -> p k g", g=2), ACT.Silu).then_inc(s["cact_ok"], 1)

            def mod_out(j):
                act.wait_ge(s["mod_ps"], j + 1)
                if j >= 2:
                    act.wait_ge(s["mT_ps"], j - 1)
                A(modr[:, j % 2, :], bank(j if j < 4 else 7), ACT.Copy).then_inc(s["mraw_sb"], 1)

            def mod_cols(j):
                act.wait_ge(s["mT_ps"], j + 1)
                A(modt[:, 4 * j:4 * j + 4, :].rearrange("p m (q g) -> p m q g", q=4),
                  bank(6).rearrange("p (m q r) -> p m q r", m=4, q=4)[:, :, :, 0:2], ACT.Copy).then_inc(s["mT_sb"], 1)

            for t in range(TT):
                act.wait_ge(s[f"ld_x{t}"], 16)
                A(mixC[:, 0:2, 0:512], x[:, t, :].rearrange("p (a n) -> p a n", a=2), ACT.Square,
                  accum_out=ss[:, t:t + 1]).then_inc(s["sqx"], 1)
                act.wait_ge(s["sqx"], t + 1)
            act.wait_ge(s["gcol_ok"], 1)
            A(rs[:, 0:TT], ss[:, 0:TT], ACT.Sqrt, scale=1.0 / D, bias=ss[:, 5:6]).then_inc(s["rstdx_s"], 1)
            for j in range(4):
                mod_out(j)
                if j >= 1:
                    mod_cols(j - 1)
            mod_cols(3)
            act.wait_ge(s["a1_ok"], 1)
            for k in range(0, KD, 2):
                act.wait_ge(s["hT_ps"], k + 1)
                A(hT[:, k, 0:NS], bank(0), ACT.Identity, scale=A1[:, k, 0:1], bias=modc[:, k, 0:1])
                A(hT[:, k, NS:NT], bank(1, 0, NP), ACT.Identity, scale=A1[:, k, 1:2],
                  bias=modc[:, k, 1:2]).then_inc(s["hTa"], 1)
            for i in range(17):
                b = 2 * (i % 2)
                act.wait_ge(s["pj"], i + 1)
                if i < 8 and i % 2 == 0:
                    cc = i // 2
                    if cc >= 2:
                        act.wait_ge(s["glu_mul"], cc - 1)
                    A(sq[:, cc % 2, 0:HN], bank(b, 0, HN), ACT.Sigmoid)
                    A(sq[:, cc % 2, HN:NT], bank(b + 1, 0, HN), ACT.Sigmoid).then_inc(s["ev"], 1)
                elif i < 8:
                    if i == 1:
                        act.wait_ge(s["glu_pad"], 1)
                    cc = i // 2
                    A(gluv[:, cc, PAD:PAD + HN], bank(b, 0, HN), ACT.Copy)
                    A(gluv[:, cc, PAD + HN:PAD + NS], bank(b + 1, 0, NS - HN), ACT.Copy)
                    A(gluv[:, cc, 2 * PAD + NS:2 * PAD + NT], bank(b + 1, NS - HN, HN), ACT.Copy).then_inc(s["ev"], 1)
                else:
                    M = P if i < 16 else DR
                    dst = qlat[:, i - 8, :] if i < 14 else ckvT[:, i - 14, CTX:NK] if i < 16 else kr[0:DR, CTX:NK]
                    A(dst[:, 0:HN], bank(b, 0, HN, M), ACT.Copy)
                    A(dst[:, HN:NT], bank(b + 1, 0, HN, M), ACT.Copy).then_inc(s["ev"], 1)
                if i % 2 == 1:
                    mod_out(4 + i // 2)
                elif i >= 2:
                    mod_cols(3 + i // 2)
            act.wait_ge(s["qst"], QC)
            act.wait_ge(s["mT_ps"], HALF)
            for n in range(2):
                A(q_rows[:, n * HN:(n + 1) * HN], bank(4 + n, 0, HN), ACT.Copy).then_inc(s["qrow_ok"], 1)
            act.wait_ge(s["kvs"], 1)
            for n in range(2):
                A(sq[:, 2, n * HN:(n + 1) * HN], bank(6 + n, 0, HN), ACT.Sqrt, scale=1.0 / KR,
                  bias=ss[:, 5:6]).then_inc(s["kvs_r"], 1)
            act.wait_ge(s["qcol"], 1)
            A(rq[:, 0:TT], bank(4, 0, TT), ACT.Sqrt, scale=1.0 / (32 * QR), bias=ss[:, 5:6]).then_inc(s["qs_s"], 1)
            for i in range(6):
                b = 2 * ((17 + i) % 2)
                act.wait_ge(s["pj"], 18 + i)
                for n in range(2):
                    cols = slice(n * HN, (n + 1) * HN)
                    if i < 4:
                        for a in range(2):
                            last = A(QT[0:DN, 2 * i + a, cols], bank(b + n, 0, HN, DN * (a + 1), DN * a), ACT.Copy)
                    else:
                        last = A(qr[:, i - 4, cols], bank(b + n, 0, HN), ACT.Copy)
                last.then_inc(s["ev"], 1)
            act.wait_ge(s["kvr"], 1)
            act.wait_ge(s["ckv_ok"], KC)
            for i in range(4):
                b = 2 * ((23 + i) % 2)
                act.wait_ge(s["pj"], 24 + i)
                for a in range(2):
                    A(kT[0:DN, 2 * i + a, 0:HK], bank(b, 0, HK, DN * (a + 1), DN * a), ACT.Copy)
                    last = A(kT[0:DN, 2 * i + a, HK:NK], bank(b + 1, 0, HK, DN * (a + 1), DN * a), ACT.Copy)
                last.then_inc(s["ev"], 1)
            act.wait_ge(s["ln_var"], 1)
            A(rv[:, 0:CH], bank(5, 0, CH), ACT.Sqrt, scale=1.0 / CC, bias=ss[:, 5:6]).then_inc(s["ln_s"], 1)
            A(rv[:, CH:CW], bank(6, 0, CW - CH), ACT.Sqrt, scale=1.0 / CC, bias=ss[:, 5:6]).then_inc(s["ln_s"], 1)
            for r in range(2):
                act.wait_ge(s["rq_step"], 3 * (r + 1))
                for j in range(4):
                    A(QT[DN:DQK, 4 * r + j, :], qr[DR * j:DR * (j + 1), r, :], ACT.Copy).then_inc(s["rope_a"], 1)
            for t in range(7):
                act.wait_ge(s["pj"], 28 + t)
                A(V[:, t, :], bank(2 * ((27 + t) % 2)), ACT.Copy).then_inc(s["ev"], 1)
            for k in range(CT):
                act.wait_ge(s["ln_n"], k + 1)
                for lo, hi in ((0, NS), (CP0, CW)):
                    A(mixC[:, k, lo:hi], mixC[:, k, lo:hi], ACT.Silu, scale=vec[:, V_LG + k:V_LG + k + 1],
                      bias=vec[:, V_LB + k:V_LB + k + 1]).then_inc(s["ln_out"], 1)
            for n in range(4):
                b = [5, 6, 4, 7][n]
                act.wait_ge(s["g1_ps"], n + 1)
                A(g1b[:, n // 2, (n % 2) * 512:(n % 2 + 1) * 512], bank(b), ACT.Copy).then_inc(s["g1_sb"], 1)
            act.wait_ge(s["g2_ps"], 4)
            for n in range(2):
                A(G2r[0:C, n * 512:(n + 1) * 512], bank(5 + n, 0, 512, C), ACT.Copy).then_inc(s["g2_sb"], 1)
            def exps(u):
                h, t, _ = steps[u]
                act.wait_ge(s["nb_ok"], u + 1)
                if u >= 2:
                    act.wait_ge(s["t_ps"], u - 1)
                b = 2 * (u % 2)
                if t < 4:
                    out, src = Pb[:, u % 2, :].rearrange("p (a n) -> p a n", a=2), two_banks(b, KS // 2)
                else:
                    out, src = Pb[:, u % 2, 0:NP], bank(b, 0, NP)
                A(out, src, ACT.Exp, scale=rq[:, t:t + 1], bias=nb[:, u % 2:u % 2 + 1],
                  accum_out=psm[:, u % 2:u % 2 + 1]).then_inc(s["exp_ok"], 1)

            def attn_out(n):
                hp, ts = groups[n]
                act.wait_ge(s["pv_ps"], n + 1)
                w = P * len(ts)
                A(mixA[:, hp, ts[0] * P:ts[0] * P + w], bank(6 + n % 2, 0, w), ACT.Copy).then_inc(s["ata"], 1)

            exps(0)
            for u in range(U):
                h, t, n = steps[u]
                if u + 1 < U:
                    exps(u + 1)
                act.wait_ge(s["t_ps"], u + 1)
                if n >= 2:
                    act.wait_ge(s["pv_ps"], n - 1)
                w = 3 if t < 4 else 1
                A(PT[n % 2][:, 0:w, h % 2, t % 2 * P:(t % 2 + 1) * P], bank(4, 0, w * P).rearrange("p (k n) -> p k n", k=w),
                  ACT.Copy).then_inc(s["pta"], 1)
                if u >= 2 and steps[u - 1][2] != steps[u - 2][2]:
                    attn_out(steps[u - 2][2])
            attn_out(len(groups) - 1)

            order = [4, 0, 1, 2, 3]

            def norm(i):
                t = order[i]
                act.wait_ge(s["x1_ok"], 2 * (i + 1))
                if i == 0:
                    act.wait_ge(s["t_ps"], U)
                A(g1b_junk, x[:, t, :], ACT.Square, accum_out=ss[:, t:t + 1]).then_inc(s["x1sq"], 1)
                act.wait_ge(s["x1sq"], i + 1)
                A(rs[:, t:t + 1], ss[:, t:t + 1], ACT.Sqrt, scale=1.0 / D, bias=ss[:, 5:6]).then_inc(s["x1s"], 1)
                act.dma_start(acc_d[t * P:(t + 1) * P, :], x[:, t, :]).then_inc(s["out_x1"], 16)
                act.wait_ge(s["x1n"], i + 1)
                act.dma_start(hn_d[t * P:(t + 1) * P, :], xn2[:, i % 2, :]).then_inc(s[f"out_hn{i}"], 16)

            def h2(i):
                g = 1 if order[i] == 4 else 0
                act.wait_ge(s["xt_ps"], i + 1)
                if i >= 2:
                    act.wait_ge(s["lg_ps"], i - 1)
                for k in range(4):
                    A(h2T[:, i % 2, k, :], bank(4, k * P, (k + 1) * P), ACT.Identity, scale=A2[:, k, g:g + 1],
                      bias=modc[:, 24 + k, g:g + 1]).then_inc(s["h2a"], 1)

            def rexp(i):
                act.wait_ge(s["lmax"], i + 1)
                if i >= 2:
                    act.wait_ge(s["affn_ok"], i - 1)
                A(aff[:, i % 2, :], bank(6, 0, E), ACT.Exp, bias=sm[:, i % 2:i % 2 + 1],
                  accum_out=sm[:, 2 + i % 2:3 + i % 2]).then_inc(s["lexp"], 1)

            g1b_junk = wikr[:, 0:D]
            for i in range(TT):
                norm(i)
                if i >= 1:
                    h2(i - 1)
                if i >= 2:
                    rexp(i - 2)
            rexp(3)
            h2(4)
            rexp(4)

            def expert(e, last_one):
                act.wait_ge(s["a_ps"], e + 1)
                A(esil[0:C, :], ps[0:C, 0:1024], ACT.Silu).then_inc(s["sil"], 1)
                act.wait_ge(s["hT_tr"], e + 1)
                A(halves(ehT), two_banks(4, 4 * C), ACT.Copy).then_inc(s["hT_ok"], 1)

            with act.Fori(0, E - 1) as e:
                expert(e, False)
            expert(E - 1, True)
            for t in range(TT):
                act.wait_ge(s[f"ld_acc{t}"], 16)
                A(g1b_junk, x[:, t, :], ACT.Square, accum_out=ss[:, t:t + 1]).then_inc(s["fsq"], 1)
                act.wait_ge(s["fsq"], t + 1)
                A(rs[:, t:t + 1], ss[:, t:t + 1], ACT.Sqrt, scale=1.0 / D, bias=ss[:, 5:6]).then_inc(s["fsr"], 1)

        @block.vector
        def _(dve):
            v = nc.vector
            v.memset(ss[:, 5:6], EPS).then_inc(s["gcol_ok"], 1)
            dve.wait_ge(s["vecT_ps"], 1)
            v.tensor_copy(vec[:, :], bank(7, 128, 128 + VR)).then_inc(s["vecT_sb"], 1)
            v.tensor_copy(cw, bank(6, 256, 256 + CT * W).rearrange("p (c w) -> p c w", c=CT)).then_inc(s["vecT_sb"], 1)
            dve.wait_ge(s["tr_ctx"], 1)
            v.tensor_copy(kr[0:DR, 0:CTX], bank(4, 0, CTX, DR)).then_inc(s["ctx_sb"], 1)
            v.tensor_copy(ckvT[:, :, 0:CTX], bank(5).rearrange("p (k n) -> p k n", k=KC)).then_inc(s["ctx_sb"], 1)
            dve.wait_ge(s["rstdx_s"], 1)
            v.reciprocal(rs[:, 0:TT], rs[:, 0:TT]).then_inc(s["rstdx"], 1)
            dve.wait_ge(s["rstdx"], 1)
            for t in range(TT):
                v.tensor_scalar(x[:, t, :], x[:, t, :], rs[:, t:t + 1], None, ALU.mult).then_inc(s["xn_ok"], 1)
            dve.wait_ge(s["mT_sb"], 4)
            v.tensor_reduce(modc[:, 0:16, :], modt[:, 0:16, :].rearrange("p m (q g) -> p m g q", q=4), AX,
                            ALU.add).then_inc(s["red1"], 1)
            dve.wait_ge(s["red1"], 1)
            v.tensor_tensor(modc[:, 0:16, :], modc[:, 0:16, :],
                            vec[:, V_BM:V_BM + 16].unsqueeze(2).broadcast_to([P, 16, 2]), ALU.add).then_inc(s["mod1"], 1)
            dve.wait_ge(s["mod1"], 1)
            v.scalar_tensor_tensor(out=A1, in0=modc[:, 8:16, :], scalar=1.0,
                                   in1=vec[:, V_AG:V_AG + 8].unsqueeze(2).broadcast_to([P, 8, 2]),
                                   op0=ALU.add, op1=ALU.mult).then_inc(s["a1_ok"], 1)
            dve.wait_ge(s["a1_ok"], 1)
            for k in range(1, KD, 2):
                dve.wait_ge(s["hT_ps"], k + 1)
                v.tensor_scalar(hT[:, k, 0:NS], bank(2), A1[:, k, 0:1], modc[:, k, 0:1], ALU.mult, ALU.add)
                v.tensor_scalar(hT[:, k, NS:NT], bank(3, 0, NP), A1[:, k, 1:2], modc[:, k, 1:2],
                                ALU.mult, ALU.add).then_inc(s["hTd"], 1)
            n = 0
            for cc in range(CT):
                dve.wait_ge(s["glu_mul"], cc + 1)
                if cc == 0:
                    dve.wait_ge(s["sqx"], TT)
                for w in range(W):
                    src = gluv[:, cc, w:w + CW]
                    if w == 0:
                        o = v.tensor_scalar(mixC[:, cc, :], src, cw[:, cc, 0:1], vec[:, V_CB + cc:V_CB + cc + 1],
                                            ALU.mult, ALU.add)
                    else:
                        dve.wait_ge(s["conv_ops"], n)
                        o = v.scalar_tensor_tensor(out=mixC[:, cc, :], in0=src, scalar=cw[:, cc, w:w + 1],
                                                   in1=mixC[:, cc, :], op0=ALU.mult, op1=ALU.add)
                    if w < W - 1:
                        o.then_inc(s["conv_ops"], 1)
                        n += 1
                    else:
                        o.then_inc(s["conv_done"], 1)
            dve.wait_ge(s["qs_s"], 1)
            v.reciprocal(rq[:, 0:TT], rq[:, 0:TT]).then_inc(s["qs_r"], 1)
            dve.wait_ge(s["qs_r"], 1)
            v.tensor_scalar(rq[:, 0:TT], rq[:, 0:TT], float(DQK) ** -0.5, None, ALU.mult).then_inc(s["qs_r"], 1)
            dve.wait_ge(s["kvs_r"], 2)
            v.reciprocal(sq[:, 2, :], sq[:, 2, :]).then_inc(s["kvr"], 1)
            dve.wait_ge(s["kvr"], 1)
            for j in range(KC):
                v.scalar_tensor_tensor(out=ckvT[:, j, CTX:NK], in0=ckvT[:, j, CTX:NK], scalar=vec[:, V_KG + j:V_KG + j + 1],
                                       in1=sq[:, 2, :], op0=ALU.mult, op1=ALU.mult).then_inc(s["ckv_ok"], 1)
            dve.wait_ge(s["rotk"], 1)
            v.tensor_tensor(kr[0:DR, CTX:KS], kr[0:DR, CTX:KS], cos[0:DR, :], ALU.mult).then_inc(s["rk_step"], 1)
            v.tensor_tensor(rt[0:DR, :], bank(5, 0, NS, DR), sin[0:DR, :], ALU.mult).then_inc(s["rk_step"], 1)
            dve.wait_ge(s["rk_step"], 2)
            v.tensor_tensor(kr[0:DR, CTX:KS], kr[0:DR, CTX:KS], rt[0:DR, :], ALU.add).then_inc(s["krt"], 1)
            dve.wait_ge(s["krt"], 1)
            dve.wait_ge(s["ckv_ok"], KC)
            v.tensor_copy(kT[DN:DQK, :, :], kr[0:DR, :].unsqueeze(1).broadcast_to([DR, H, NK])).then_inc(s["kT_rope"], 1)
            dve.wait_ge(s["mT_sb"], HALF)
            v.tensor_reduce(modc[:, 16:48, :], modt[:, 16:48, :].rearrange("p m (q g) -> p m g q", q=4), AX,
                            ALU.add).then_inc(s["red2"], 1)
            dve.wait_ge(s["red2"], 1)
            v.tensor_tensor(modc[:, 16:48, :], modc[:, 16:48, :],
                            vec[:, V_BM + 16:V_BM + 48].unsqueeze(2).broadcast_to([P, 32, 2]), ALU.add).then_inc(s["mod2"], 1)
            dve.wait_ge(s["mod2"], 1)
            v.scalar_tensor_tensor(out=A2, in0=modc[:, 32:40, :], scalar=1.0,
                                   in1=vec[:, V_FG:V_FG + 8].unsqueeze(2).broadcast_to([P, 8, 2]),
                                   op0=ALU.add, op1=ALU.mult).then_inc(s["a2_ok"], 1)
            for r in range(2):
                dve.wait_ge(s["rotq"], r + 1)
                v.tensor_tensor(qr[:, r, 0:NS], qr[:, r, 0:NS], cos, ALU.mult).then_inc(s["rq_step"], 1)
                v.tensor_tensor(rt, bank(6 - r), sin, ALU.mult).then_inc(s["rq_step"], 1)
                dve.wait_ge(s["rq_step"], 3 * r + 2)
                v.tensor_tensor(qr[:, r, 0:NS], qr[:, r, 0:NS], rt, ALU.add).then_inc(s["rq_step"], 1)
                dve.wait_ge(s["rq_step"], 3 * r + 3)
            dve.wait_ge(s["ln_mean"], 1)
            for k in range(CT):
                v.scalar_tensor_tensor(out=mixC[:, k, 0:CH], in0=bank(4, 0, CH), scalar=-1.0 / CC,
                                       in1=mixC[:, k, 0:CH], op0=ALU.mult, op1=ALU.add)
                v.scalar_tensor_tensor(out=mixC[:, k, CH:CW], in0=bank(7, 0, CW - CH), scalar=-1.0 / CC,
                                       in1=mixC[:, k, CH:CW], op0=ALU.mult, op1=ALU.add).then_inc(s["ln_d"], 1)
            dve.wait_ge(s["ln_s"], 2)
            v.reciprocal(rv, rv).then_inc(s["ln_r"], 1)
            dve.wait_ge(s["ln_r"], 1)
            dve.wait_ge(s["ln_sq"], CT)
            for k in range(CT):
                v.tensor_tensor(mixC[:, k, :], mixC[:, k, :], rv, ALU.mult).then_inc(s["ln_n"], 1)
            dve.wait_ge(s["nk_ps"], 1)
            v.tensor_copy(ost, bank(4, 0, 288)).then_inc(s["nk_sb"], 1)

            def maxima(u):
                h, t, _ = steps[u]
                dve.wait_ge(s["s_ps"], u + 1)
                if u >= 2:
                    dve.wait_ge(s["exp_ok"], u - 1)
                b = 2 * (u % 2)
                if t < 4:
                    m = v.tensor_reduce(mx[:, u % 2:u % 2 + 1], two_banks(b, KS // 2), mybir.AxisListType.XY, ALU.max)
                else:
                    m = v.reduce_max(mx[:, u % 2:u % 2 + 1], bank(b, 0, NP), AX)
                m.then_inc(s["smax"], 1)
                dve.wait_ge(s["smax"], u + 1)
                v.tensor_scalar(nb[:, u % 2:u % 2 + 1], mx[:, u % 2:u % 2 + 1], rq[:, t:t + 1], -1.0,
                                ALU.mult, ALU.mult).then_inc(s["nb_ok"], 1)

            dve.wait_ge(s["qs_r"], 2)
            maxima(0)
            for u in range(U):
                h, t, n = steps[u]
                if u + 1 < U:
                    maxima(u + 1)
                dve.wait_ge(s["exp_ok"], u + 1)
                v.reciprocal(rin[:, u % 2:u % 2 + 1], psm[:, u % 2:u % 2 + 1]).then_inc(s["rin_ok"], 1)
                dve.wait_ge(s["rin_ok"], u + 1)
                w = KS if t < 4 else NP
                v.tensor_scalar(Pb[:, u % 2, 0:w], Pb[:, u % 2, 0:w], rin[:, u % 2:u % 2 + 1], None,
                                ALU.mult).then_inc(s["pn_ok"], 1)
                if t < 4:
                    dve.wait_ge(s["t_ps"], u + 1)
                    if n >= 2:
                        dve.wait_ge(s["pv_ps"], n - 1)
                    v.tensor_copy(PT[n % 2][:, 3:6, h % 2, t % 2 * P:(t % 2 + 1) * P],
                                  bank(5, 0, 3 * P).rearrange("p (k n) -> p k n", k=3)).then_inc(s["ptd"], 1)

            order = [4, 0, 1, 2, 3]
            dve.wait_ge(s["g1_sb"], 4)

            def residual(i):
                t = order[i]
                g = 1 if t == 4 else 0
                dve.wait_ge(s["op_ps"], i + 1)
                dve.wait_ge(s[f"ld_x{t}"], 32)
                for n in range(2):
                    c = slice(n * 512, (n + 1) * 512)
                    if i >= 1:
                        dve.wait_ge(s["x1_ok"], 2 * i)
                    v.tensor_tensor(gtmp[:, n, :], bank(2 * (i % 2) + n), g1b[:, g, c], ALU.mult).then_inc(s["g1m"], 1)
                for n in range(2):
                    c = slice(n * 512, (n + 1) * 512)
                    dve.wait_ge(s["g1m"], 2 * i + n + 1)
                    v.tensor_tensor(x[:, t, c], x[:, t, c], gtmp[:, n, :], ALU.add).then_inc(s["x1_ok"], 1)
                dve.wait_ge(s["x1s"], i + 1)
                v.reciprocal(rs[:, t:t + 1], rs[:, t:t + 1]).then_inc(s["x1r"], 1)
                dve.wait_ge(s["x1r"], i + 1)
                if i >= 2:
                    dve.wait_ge(s["xt_ps"], i - 1)
                    dve.wait_ge(s[f"out_hn{i - 2}"], 16)
                dve.wait_ge(s["x1_ok"], 2 * (i + 1))
                v.tensor_scalar(xn2[:, i % 2, :], x[:, t, :], rs[:, t:t + 1], None, ALU.mult).then_inc(s["x1n"], 1)

            def h2(i):
                g = 1 if order[i] == 4 else 0
                dve.wait_ge(s["xt_ps"], i + 1)
                if i >= 2:
                    dve.wait_ge(s["lg_ps"], i - 1)
                for k in range(4, KD):
                    v.tensor_scalar(h2T[:, i % 2, k, :], bank(5, (k - 4) * P, (k - 3) * P), A2[:, k, g:g + 1],
                                    modc[:, 24 + k, g:g + 1], ALU.mult, ALU.add).then_inc(s["h2d"], 1)

            def softmax_in(i):
                dve.wait_ge(s["lg_ps"], i + 1)
                if i >= 2:
                    dve.wait_ge(s["lexp"], i - 1)
                v.tensor_reduce(sm[:, i % 2:i % 2 + 1], bank(6, 0, E), AX, ALU.max, negate=True).then_inc(s["lmax"], 1)

            def softmax_out(i):
                dve.wait_ge(s["lexp"], i + 1)
                v.reciprocal(sm[:, 4 + i % 2:5 + i % 2], sm[:, 2 + i % 2:3 + i % 2]).then_inc(s["lrec"], 1)
                dve.wait_ge(s["lrec"], i + 1)
                if i >= 2:
                    dve.wait_ge(s["aff_ps"], i - 1)
                v.tensor_scalar(affn[:, i % 2, :], aff[:, i % 2, :], sm[:, 4 + i % 2:5 + i % 2], None,
                                ALU.mult).then_inc(s["affn_ok"], 1)

            def aff_out(i):
                t = order[i]
                dve.wait_ge(s["aff_ps"], i + 1)
                v.tensor_copy(affT[:, t * P:(t + 1) * P], bank(7, 0, P, E)).then_inc(s["affT_ok"], 1)

            top = [0]

            def choose(src, o, rounds):
                for r in range(rounds):
                    best = topv[:, o + 8 * r:o + 8 * r + 8]
                    v.max(best, src).then_inc(s["topk"], 1)
                    dve.wait_ge(s["topk"], top[0] + 1)
                    v.max_index(topi[:, o + 8 * r:o + 8 * r + 8], best, src).then_inc(s["topk"], 1)
                    dve.wait_ge(s["topk"], top[0] + 2)
                    v.match_replace(src, best, src, -1.0).then_inc(s["topk"], 1)
                    dve.wait_ge(s["topk"], top[0] + 3)
                    top[0] += 3

            dve.wait_ge(s["a2_ok"], 1)
            for i in range(TT):
                residual(i)
                if i >= 1:
                    h2(i - 1)
                if i >= 2:
                    softmax_in(i - 2)
                    softmax_out(i - 2)
                if i >= 3:
                    aff_out(i - 3)
                if i == 3:
                    dve.wait_ge(s["affT_ok"], 1)
                    choose(affT[:, NS:NT], CS, CP // 8)
            softmax_in(3)
            softmax_out(3)
            aff_out(2)
            h2(4)
            aff_out(3)
            softmax_in(4)
            softmax_out(4)
            aff_out(4)
            dve.wait_ge(s["affT_ok"], TT)
            choose(affT[:, 0:NS], 0, CS // 8)
            v.tensor_copy(topf[:, 0:CS], topi[:, 0:CS]).then_inc(s["sel"], 1)
            v.tensor_scalar(topf[:, CS:C], topi[:, CS:C], float(NS), None, ALU.add).then_inc(s["sel"], 1)
            dve.wait_ge(s["sel_ps"], 1)
            v.tensor_copy(idxc[0:C, :], bank(5, 0, E, C)).then_inc(s["sel_sb"], 1)
            v.tensor_copy(gates[0:C, :], bank(5, E, 2 * E, C)).then_inc(s["sel_sb"], 1)

            def modulate(e):
                dve.wait_ge(s["xt2_ps"], e + 1)
                v.tensor_tensor(halves(xmod), two_banks(6, 4 * C), halves(A2f), ALU.mult).then_inc(s["xm1"], 1)
                dve.wait_ge(s["xm1"], e + 1)
                v.tensor_tensor(xsT, xmod, S2f, ALU.add).then_inc(s["xs_ok"], 1)

            def expert(e, last_one):
                dve.wait_ge(s["sil"], e + 1)
                dve.wait_ge(s["u_ps"], e + 1)
                v.tensor_tensor(eh[0:C, :], ps[0:C, 1024:2048], esil[0:C, :], ALU.mult).then_inc(s["h_ok"], 1)
                if not last_one:
                    modulate(e + 1)
                dve.wait_ge(s["y_ps"], e + 1)
                dve.wait_ge(s["yw_free"], e + 1)
                v.scalar_tensor_tensor(out=yw[0:C, :], in0=ps[0:C, 3072:4096], scalar=gates[0:C, bass.ds(e, 1)],
                                       in1=G2r[0:C, :], op0=ALU.mult, op1=ALU.mult).then_inc(s["yw_ok"], 1)

            dve.wait_ge(s["full_ok"], 4)
            dve.wait_ge(s["out_x1"], 16 * TT)
            modulate(0)
            with dve.Fori(0, E - 1) as e:
                expert(e, False)
            expert(E - 1, True)
            dve.wait_ge(s["ld_fg"], 16)
            for t in range(TT):
                dve.wait_ge(s["fsr"], t + 1)
                v.reciprocal(rs[:, t:t + 1], rs[:, t:t + 1]).then_inc(s["frec"], 1)
                dve.wait_ge(s["frec"], t + 1)
                v.scalar_tensor_tensor(out=x[:, t, :], in0=x[:, t, :], scalar=rs[:, t:t + 1], in1=fgb, op0=ALU.mult,
                                       op1=ALU.mult).then_inc(s["fin_ok"], 1)

        @block.gpsimd
        def _(pool):
            g_ = nc.gpsimd
            g_.memset(cact[:, :, :], 0.0).then_inc(s["cact_z"], 1)
            for o, n in ((0, PAD), (PAD + NS, PAD), (2 * PAD + NT, PAD)):
                last = g_.memset(gluv[:, :, o:o + n], 0.0)
            last.then_inc(s["glu_pad"], 1)
            for cc in range(CT):
                pool.wait_ge(s["ev"], 2 * cc + 2)
                g_.tensor_tensor(gluv[:, cc, PAD:PAD + NS], gluv[:, cc, PAD:PAD + NS], sq[:, cc % 2, 0:NS], ALU.mult)
                o = 2 * PAD + NS
                g_.tensor_tensor(gluv[:, cc, o:o + NP], gluv[:, cc, o:o + NP], sq[:, cc % 2, NS:NT],
                                 ALU.mult).then_inc(s["glu_mul"], 1)
            pool.wait_ge(s["glu_mul"], CT)
            for i in range(QC + KC):
                pool.wait_ge(s["ev"], 9 + i)
                if 3 <= i < QC:
                    pool.wait_ge(s["qst"], i - 2)
                if i >= QC:
                    pool.wait_ge(s["qst"], QC)
                src = qlat[:, i, :] if i < QC else ckvT[:, i - QC, CTX:NK]
                g_.tensor_tensor(sq[:, i % 3, :], src, src, ALU.mult).then_inc(s["sq_ok"], 1)
                if i == 2:
                    pool.wait_ge(s["ld_wq"], 32 * QC)
                    for k in range(QC):
                        last = g_.tensor_scalar(wq[:, k, :], wq[:, k, :], vec[:, V_QG + k:V_QG + k + 1], None,
                                                ALU.mult)
                    last.then_inc(s["wq_ok"], 1)
            for k in range(CT):
                pool.wait_ge(s["ln_d"], k + 1)
                g_.tensor_tensor(dsq[:, k, :], mixC[:, k, :], mixC[:, k, :], ALU.mult).then_inc(s["ln_sq"], 1)
            pool.wait_ge(s["nk_sb"], 1)
            pool.dma_start(new_ckv[0, 0], ost[:, 0:KR]).then_inc(s["out_kv"], 16)
            pool.dma_start(new_krope[0, 0], ost[:, KR:KR + DR]).then_inc(s["out_kv"], 16)
            pool.wait_ge(s["mod2"], 1)
            pool.wait_ge(s["ev"], 17)
            pool.wait_ge(s["a2_ok"], 1)
            for n in range(8):
                if n in (2, 3, 4, 5):
                    pool.wait_ge(s["g1_ps"], n - 1)
                if n >= 6:
                    pool.wait_ge(s["g2_ps"], n - 5)
                which, g, half = n // 4, n // 2 % 2, n % 2
                for k in range(4):
                    m = [16, 40][which] + 4 * half + k
                    last = g_.tensor_scalar(diag[:, n % 2, k, :], ident, modc[:, m, g:g + 1], None, ALU.mult)
                last.then_inc(s["diag_ok"], 1)
                if n == 0:
                    for g in range(2):
                        g_.memset(grp[:, g, 0:CS], 1.0 - g)
                        last = g_.memset(grp[:, g, CS:C], float(g))
                    last.then_inc(s["grp_ok"], 1)
            pool.wait_ge(s["nk_ps"], 1)
            for dst, src in ((A2f, A2), (S2f, modc[:, 24:32, :])):
                for g, lo, hi in ((0, 0, CS), (1, CS, C)):
                    g_.tensor_copy(dst[:, :, lo:hi], src[:, :, g:g + 1].broadcast_to([P, KD, hi - lo])).then_inc(s["full_ok"], 1)
            pool.wait_ge(s["t_ps"], U)
            pool.wait_ge(s["pv_ps"], len(groups))
            pool.wait_ge(s["out_kv"], 32)
            pool.dma_start(fgb, final_norm_g.rearrange("(o n) -> o n", o=1).broadcast_to([P, D])).then_inc(s["ld_fg"], 16)
            def scatter(e):
                pool.wait_ge(s["yw_ok"], e + 1)
                g_.indirect_dma_start(acc_d, bass.IndirectOffsetOnAxis(ap=idxc[0:C, e:e + 1], axis=0), yw[0:C, :], None,
                                      compute_op=ALU.add).then_inc(s["scat"], 16)
                pool.wait_ge(s["scat"], 16 * (e + 1))
                g_.memset(flag[:, :], 0.0).then_inc(s["yw_free"], 1)

            pool.wait_ge(s["sel_sb"], 2)
            for i in range(TT):
                pool.wait_ge(s[f"out_hn{i}"], 16)
            pool.wait_ge(s["out_x1"], 16 * TT)
            g_.memset(flag[:, :], 0.0).then_inc(s["yw_free"], 1)
            for e in range(E):
                if e >= 1:
                    pool.wait_ge(s["xt2_ps"], e)
                g_.indirect_dma_start(xg[0:C, :], None, hn_d, bass.IndirectOffsetOnAxis(ap=idxc[0:C, e:e + 1], axis=0)).then_inc(s["gath"], 16)
                if e >= 1:
                    scatter(e - 1)
            scatter(E - 1)


_INS = ["x_prompt", "x_sample", "cache_ckv", "cache_krope", "c", "c_ctx", "w_mod", "b_mod", "attn_norm_g", "w_in",
        "q_norm_g", "w_q_up", "kv_norm_g", "w_kv_up", "conv_w", "conv_b", "conv_ln_g", "conv_ln_b", "w_out",
        "ffn_norm_g", "w_router", "w_gate", "w_up", "w_down", "final_norm_g"]
_OUTS = [(1, 128, 1024), (1, 512, 1024), (1, 1, 128, 256), (1, 1, 128, 32)]


def _tables():
    import numpy as _np
    t = _np.zeros((128, 1408), _np.float32)
    t[:, 0:128] = _np.eye(128)
    t[:, 128:256] = 1.0
    for m in range(128):
        if m % 16 < 8:
            t[m + 8, 256 + m] = -1.0
        else:
            t[m - 8, 256 + m] = 1.0
    inv = (1.0 / (_np.float32(10000.0) ** (_np.arange(0, 16, 2, dtype=_np.float32) / _np.float32(16)))).astype(_np.float32)
    pos = _np.arange(512)
    f = _np.arange(128) % 32
    where = _np.where(f[:, None] < 16, pos[None, :] // 64, pos[None, :] % 64).astype(_np.float32)
    ang = (where * inv[f % 8][:, None]).astype(_np.float32)
    t[:, 384:896] = _np.cos(ang)
    t[:, 896:1408] = _np.sin(ang)
    return t


def kernel(**inputs):
    import numpy as _np
    import concourse.bacc as _bacc
    from concourse import mybir as _mybir
    from concourse.bass_utils import run_bass_kernel_spmd as _run

    nc = _bacc.Bacc("TRN2", target_bir_lowering=False, num_devices=1, dynamic_dma_scratch_size=2048)
    arrays, args = {}, []
    for name in _INS:
        a = _np.ascontiguousarray(inputs[name])
        arrays[f"in_{name}_dram"] = a
        args.append(nc.dram_tensor(f"in_{name}_dram", a.shape, _mybir.dt.from_np(a.dtype), kind="ExternalInput").ap())
    arrays["in_tables_dram"] = _tables()
    args.append(nc.dram_tensor("in_tables_dram", (128, 1408), _mybir.dt.float32, kind="ExternalInput").ap())
    for i, shape in enumerate(_OUTS):
        args.append(nc.dram_tensor(f"out_{i}_dram", shape, _mybir.dt.float32, kind="ExternalOutput").ap())
    layer(nc, *args)
    r = _run(nc, [arrays], core_ids=[0])
    return tuple(r.results[0][f"out_{i}_dram"] for i in range(len(_OUTS)))
```

```python
from contextlib import ExitStack

import concourse.bass as bass
from concourse import mybir

F32 = mybir.dt.float32
F32R = mybir.dt.float32r
U32 = mybir.dt.uint32
ALU = mybir.AluOpType
ACT = mybir.ActivationFunctionType
AX = mybir.AxisListType.X

P = 128
D = 1024
KD = D // P
NS, NP = 512, 128
NT = NS + NP
TT = NT // P
CTX = 256
NK = CTX + NT
KS = CTX + NS
H, DN, DR, DV = 8, 64, 32, 64
DQK = DN + DR
QR, KR, CC, W = 768, 256, 512, 31
QC, KC, CT = QR // P, KR // P, CC // P
GRID = 64
E, F = 16, 1024
CS, CP = 2 * NS // E, 2 * NP // E
SH, PQ, CPT = P // CS, 4, 32
SW, PW = D // SH, D // PQ
SJ, PJ = SW // P, PW // P
XR = SW + PW
SPARE = PQ * (CPT - CP) // PQ
EPS = 1e-6
PAD = (W - 1) // 2
GW = PAD + NS + PAD + NP + PAD
CW = NS + PAD + NP
CP0 = NS + PAD

V_C, V_CCTX, V_AG, V_FG, V_QG, V_KG, V_CB, V_LG, V_LB, V_BM = 0, 8, 16, 24, 32, 38, 40, 44, 48, 52
VR = V_BM + 48
NMOD = 6
HALF = 12

SLOT = 4 * F
SLOTS = 6


def layer(nc, x_prompt, x_sample, cache_ckv, cache_krope, c, c_ctx, w_mod, b_mod, attn_norm_g, w_in,
          q_norm_g, w_q_up, kv_norm_g, w_kv_up, conv_w, conv_b, conv_ln_g, conv_ln_b, w_out, ffn_norm_g,
          w_router, w_gate, w_up, w_down, final_norm_g, tables, y_prompt, y_sample, new_ckv, new_krope):
    ctx = ExitStack()
    with ctx:
        starts = {}

        def sb(name, n, dt=F32):
            starts[name] = -(-nc.sbuf_base // 32) * 32
            return ctx.enter_context(nc.sbuf_tensor(name, [P, n], dt))

        def rounded(name, where, first, n):
            return nc.alloc_sbuf_tensor_at(name, [P, n], F32R, offset=starts[where] + 4 * first)

        def sem(name):
            return ctx.enter_context(nc.semaphore(name))

        ring = sb("ring", SLOTS * SLOT)
        wglu = ring[:, 0:8 * 2 * CC].rearrange("p (k n) -> p k n", k=KD)
        wq = ring[:, 0:QC * 768].rearrange("p (k n) -> p k n", k=QC)
        V = ring[:, 4608:4608 + 7 * 512].rearrange("p (t n) -> p t n", t=7)
        winq = ring[:, 8192:8192 + 6144].rearrange("p (k n) -> p k n", k=KD)
        kT = ring[:, 8192:8192 + H * NK].rearrange("p (h n) -> p h n", h=H)
        sq = ring[:, 14336:14336 + 3 * NT].rearrange("p (b n) -> p b n", b=3)
        wm_c = ring[:, 16384:20480].rearrange("p (k n) -> p k n", k=KD)
        wm_a = ring[:, 20480:24576].rearrange("p (k n) -> p k n", k=KD)
        wout = ring[:, 16384:24576].rearrange("p (k n) -> p k n", k=KD)

        xr = sb("x_region", 5120)
        x = xr[:, :].rearrange("p (t n) -> p t n", t=TT)
        QT = xr[:, :].rearrange("p (h n) -> p h n", h=H)
        hr = sb("h_region", 5120)
        h_hi = rounded("h_high", "h_region", 0, KD * NT)[:, :].rearrange("p (k n) -> p k n", k=KD)
        h_lo = rounded("h_low", "x_region", 0, KD * NT)[:, :].rearrange("p (k n) -> p k n", k=KD)
        wm_h = hr[:, 0:4096].rearrange("p (k n) -> p k n", k=KD)
        qr = hr[:, 0:2 * NT].rearrange("p (r n) -> p r n", r=2)
        rt = hr[:, 1280:1280 + NS]
        dsq = hr[:, 1792:1792 + CT * CW].rearrange("p (c n) -> p c n", c=CT)
        rv = hr[:, 4412:4412 + CW]
        xn2 = hr[:, 0:2048].rearrange("p (b n) -> p b n", b=2)
        gtmp = hr[:, 2048:3072].rearrange("p (b n) -> p b n", b=2)
        h2T = hr[:, 3072:5120].rearrange("p (b k n) -> p b k n", b=2, k=KD)
        mar = sb("mix_attn", 4 * NT)
        mixA = mar[:, :].rearrange("p (k n) -> p k n", k=4)
        modr = mar[:, 0:1024].rearrange("p (b n) -> p b n", b=2)
        diag = mar[:, 1024:2048].rearrange("p (b k n) -> p b k n", b=2, k=4)
        q_rows = mar[:, 0:NT]
        mcr = sb("mix_conv", CT * CW)
        mixC = mcr[:, :].rearrange("p (k n) -> p k n", k=CT)
        qlr = sb("q_latent", QC * NT)
        qlat = qlr[:, :].rearrange("p (k n) -> p k n", k=QC)
        PT = [r[:, 0:3072].rearrange("p (k a n) -> p k a n", k=6, a=2) for r in (hr, qlr)]
        ckr = sb("ckv", KC * NK)
        ckvT = ckr[:, :].rearrange("p (k n) -> p k n", k=KC)
        kr = sb("krope", NK)
        gvr = sb("glu_value", CT * GW)
        gluv = gvr[:, :].rearrange("p (c n) -> p c n", c=CT)
        g1b = gvr[:, 0:2 * D].rearrange("p (g n) -> p g n", g=2)
        wkr = sb("w_kv", KC * 1024)
        wkv = wkr[:, :].rearrange("p (k n) -> p k n", k=KC)
        wikr = sb("w_in_kv", KD * 288)
        winkv = wikr[:, :].rearrange("p (k n) -> p k n", k=KD)
        Pb = wikr[:, 0:1536].rearrange("p (b n) -> p b n", b=2)
        cachek = Pb[:, 0, 0:512].rearrange("p (t n) -> p t n", t=2)
        cacher = Pb[:, 0, 512:576].rearrange("p (t n) -> p t n", t=2)
        vrow = Pb[:, 0, 576:704]
        cwrow = wikr[:, 768:768 + CC]
        tab = sb("tables", 384 + 1024)
        ident, ones, rotm = tab[:, 0:128], tab[:, 128:256], tab[:, 256:384]
        cos, sin = tab[:, 384:896], tab[:, 896:1408]
        vec = sb("vectors", VR)
        cw = sb("conv_taps", CT * W)[:, :].rearrange("p (c w) -> p c w", c=CT)
        cact = sb("cond_silu", KD * 32)[:, :].rearrange("p (k n) -> p k n", k=KD)
        modt = sb("mod_parts", 48 * 8)[:, :].rearrange("p (m n) -> p m n", m=48)
        modc = sb("modulation", 96)[:, :].rearrange("p (m g) -> p m g", g=2)
        A1 = sb("scale1", 16)[:, :].rearrange("p (k g) -> p k g", g=2)
        A2 = sb("scale2", 16)[:, :].rearrange("p (k g) -> p k g", g=2)
        ss = sb("sum_squares", 8)
        rs = sb("rstd", 8)
        ss2 = tab[:, 384:400].rearrange("p (n t) -> p n t", n=2)
        sse = tab[:, 400:408]
        rq = sb("rstd_q", 8)
        mx = sb("row_max", 2)
        nb = sb("exp_bias", 2)
        psm = sb("exp_sum", 2)
        rin = sb("exp_sum_inv", 2)
        wr = sb("w_router", KD * E)[:, :].rearrange("p (k n) -> p k n", k=KD)
        aff = sb("affinity", 2 * E)[:, :].rearrange("p (b n) -> p b n", b=2)
        affn = sb("affinity_n", 2 * E)[:, :].rearrange("p (b n) -> p b n", b=2)
        sm = sb("router_stats", 8)
        idxc = sb("choice", 2 * E, U32)[:, :].rearrange("p (g n) -> p g n", g=2)
        gates = sb("gates", 2 * E)[:, :].rearrange("p (g n) -> p g n", g=2)
        flag = sb("flag", 1)
        h_full = [mcr[:, k * NT:(k + 1) * NT] for k in range(4)] + [gvr[:, k * NT:(k + 1) * NT] for k in range(4)]
        w_parts = [[rounded(f"w_{part}_{where}", where, first, D) for part, first in (("high", 0), ("low", D))]
                   for where in ("w_kv", "q_latent", "w_in_kv")]
        xg = wkr[:, 0:XR]
        G2r = wkr[:, D:D + XR]
        A2f = ckr[:, 0:XR]
        S2f = ckr[:, XR:2 * XR]
        fgb = qlr[:, D:2 * D]
        esil, eh, xsT, ehT, xmod, yw = [xr[:, i * XR:(i + 1) * XR] for i in range(6)]
        affT = kr[0:E, 0:NT]
        topv = ckr[0:E, 1536:1536 + CS + CP]
        topi = ckr[0:E, 1616:1616 + CS + CP].bitcast(U32)
        topv2, topi2 = kr[0:E, 768:768 + CS], kr[0:E, 832:832 + CS].bitcast(U32)
        from_a, b_place, change = [tab[0:E, 512 + CS * i:512 + CS * (i + 1)] for i in range(3)]
        rows = wikr[0:E, 1824:1824 + 2 * P].rearrange("p (g n) -> p g n", g=2)
        gs_row = wikr[0:E, 2080:2080 + P]
        gp_row = kr[0:E, 640:640 + P]
        ost = wikr[:, 1536:1536 + 288]

        ps = ctx.enter_context(nc.psum_tensor("ps", [P, 8 * 512], F32))

        def bank(b, lo=0, hi=512, p=P, p0=0):
            return ps[p0:p, b * 512 + lo:b * 512 + hi]

        def two_banks(b, n):
            return ps[:, b * 512:(b + 2) * 512].rearrange("p (b n) -> p b n", b=2)[:, :, 0:n]

        cuts = ((slice(0, SW), SH, CS, SW), (slice(SW, XR), PQ, CPT, PW))

        acc_d = nc.dram_tensor("residual", [NT + SPARE, D], F32, kind="Internal").ap()
        hn_d = nc.dram_tensor("normed", [NT + SPARE, D], F32, kind="Internal").ap()
        acc_cut = [acc_d.rearrange("r (h n) -> (r h) n", h=h) for h in (SH, PQ)]
        hn_cut = [hn_d.rearrange("r (h n) -> (r h) n", h=h) for h in (SH, PQ)]

        names = """ld_rows ld_angles spare_ok xs_s xs_p u_s a_s sil_s sil_p h_s h_p hTs_tr hTp_tr hTs hTp ld_small ld_cache ld_x0
        ld_x1 ld_x2 ld_x3 ld_x4 ld_glu ld_winq ld_winkv ld_wkv ld_wq ld_wout ld_router ld_fg vecT_ps vecT_sb cact_ok
        sqx rstdx_s rstdx xn_ok mod_ps a1_ok hT_ps hTa hTd tr_ctx ctx_sb glu_pad glu_mul conv_ops conv_done pj ev
        sq_ok qst kvs kvs_r kvr qrow_ok qcol ckv_ok kT_rope rk_step wq_ok rq_step rope_a ln_mean ln_d ln_sq ln_var
        ln_s ln_r ln_n ln_out qs_s qs_r nk_ps nk_sb out_kv diag_ok g1_ps g1_sb s_ps smax nb_ok exp_ok t_ps pta ptd
        pv_ps rin_ok pn_ok ata cact_z mraw_sb mT_ps mT_sb g2_ps g2_sb op_ps g1m x1_ok whi_ok wlo_ok hlo_p hlo_d rot
        kv_sq mod_sum red merge x1h x1sq x1s x1r x1n out_x1 out_hn0 out_hn1 out_hn2 out_hn3 out_hn4 xt_ps h2a h2d
        lg_ps lmax lexp lrec affn_ok aff_ps affT_ok topk sel sel_ps sel_sb full_ok a2_ok gath xt2_ps xm1 a_ps u_ps
        y_ps yw_ok yw_free scat fin_ok out_y gcol_ok""".split()
        s = {n: sem(n) for n in names}
        wmod_ld = [sem(f"wmod_ld{j}") for j in range(4)]
        slot_ld = [sem(f"slot_ld{j}") for j in range(SLOTS)]

        tiles_in = [("kv", 0), ("gate", 0), ("value", 0), ("kv", 1), ("kr", 0)]
        tiles_in += [(kind, j) for j in range(1, CT) for kind in ("gate", "value")]
        tiles_in += [("q", j) for j in range(QC)]

        def tile_in(i):
            kind, j = tiles_in[i]
            M = DR if kind == "kr" else P
            src, col, done = {"kv": (winkv, P * j, "ld_winkv"), "kr": (winkv, KR, "ld_winkv"),
                              "gate": (wglu, CC + P * j, "ld_glu"), "value": (wglu, P * j, "ld_glu"),
                              "q": (winq, P * j, "ld_winq")}[kind]
            parts = w_parts[0 if i % 2 == 0 else 2 if kind == "q" else 1]
            view = [part[:, 0:KD * M].rearrange("p (k n) -> p k n", k=KD) for part in parts]
            return src[:, :, col:col + M], M, done, view

        def after(kind, j):
            return tiles_in.index((kind, j)) + 1

        block = ctx.enter_context(nc.Block())

        wmod_v = w_mod[0].rearrange("(k p) n -> p k n", p=P)
        win_v = w_in[0].rearrange("(k p) n -> p k n", p=P)
        wm_buf = [wm_a, wm_c, wm_h, wm_a] + [[wm_c, wm_a][j % 2] for j in range(8)]
        wm_sem = [0, 1, 2, 0] + [[1, 0][j % 2] for j in range(8)]
        wm_cnt = [16 * (wm_sem[:j + 1].count(wm_sem[j])) for j in range(HALF)]
        wm_prev = [max([i for i in range(j) if wm_sem[i] == wm_sem[j]], default=None) for j in range(HALF)]

        hT_bank = [4, 0, 2, 6, 4, 6, 2, 4]

        HN = NT // 2
        HK = NK // 2
        CH = (CW + 1) // 2

        groups = [(hp, ts) for hp in range(H // 2) for ts in ((0, 1), (2, 3), (4,))]
        steps = [(2 * hp + a, t, n) for n, (hp, ts) in enumerate(groups) for a in range(2) for t in ts]
        U = len(steps)

        def sample_steps(u):
            return sum(t < 4 for _, t, _ in steps[:u])

        def steps_before(n):
            return sum(m < n for _, _, m in steps)

        @block.sync
        def _(sp):
            def load_mod(j):
                if wm_prev[j] is not None:
                    sp.wait_ge(s["mod_ps"], wm_prev[j] + 1)
                sp.dma_start(wm_buf[j], wmod_v[:, :, 512 * j:512 * j + 512]).then_inc(wmod_ld[wm_sem[j]], 16)

            def load_heads(dst, src, chunks, a, b, done):
                for k in range(chunks):
                    rows = src[0, k * P:(k + 1) * P, :].rearrange("p (h f) -> p h f", h=H)
                    for lo, w, col in ((0, a, 0), (a, b, H * a)):
                        sp.dma_start(dst[:, k, col:col + H * w].rearrange("p (h f) -> p h f", h=H),
                                     rows[:, :, lo:lo + w]).then_inc(done, 16)

            load_mod(0)
            sp.wait_ge(s["ld_small"], 16 * 12)
            load_mod(1)
            load_mod(2)
            for dst in (acc_d, hn_d):
                sp.dma_start(dst[NT:NT + SPARE, :], x_prompt[0, 0:SPARE, :]).then_inc(s["spare_ok"], 16)
            for t in range(TT):
                src = x_sample[0, t * P:(t + 1) * P, :] if t < 4 else x_prompt[0]
                sp.dma_start(x[:, t, :], src).then_inc(s[f"ld_x{t}"], 16)
            sp.wait_ge(s["tr_ctx"], 1)
            sp.dma_start(winkv[:, :, :], win_v[:, :, QR:QR + 288]).then_inc(s["ld_winkv"], 16)
            load_mod(3)
            load_mod(4)
            sp.dma_start(wglu[:, :, :], win_v[:, :, 1056:2080]).then_inc(s["ld_glu"], 16)
            for j in range(5, HALF):
                load_mod(j)
                if j == 6:
                    sp.dma_start(winq[:, :, :], win_v[:, :, 0:QR]).then_inc(s["ld_winq"], 16)
            sp.wait_ge(s["wlo_ok"], after("value", CT - 1))
            load_heads(wq, w_q_up, QC, DN, DR, s["ld_wq"])
            sp.wait_ge(s["pj"], len(tiles_in))
            load_heads(wkv, w_kv_up, KC, DN, DV, s["ld_wkv"])
            sp.wait_ge(s["mod_ps"], HALF)
            sp.dma_start(wout[:, :, :], w_out[0].rearrange("(k p) n -> p k n", p=P)).then_inc(s["ld_wout"], 16)
            sp.dma_start(rows, tables[0:E, 1408:1408 + 2 * P].rearrange("p (g n) -> p g n", g=2)).then_inc(s["ld_rows"], 16)
            sp.wait_ge(s["s_ps"], U)
            for t in [4, 0, 1, 2, 3]:
                src = x_sample[0, t * P:(t + 1) * P, :] if t < 4 else x_prompt[0]
                sp.dma_start(x[:, t, :], src).then_inc(s[f"ld_x{t}"], 16)

            def slots(e, wait):
                for n in range(SLOTS):
                    w = [w_gate, w_gate, w_up, w_up, w_down, w_down][n]
                    wait(n)
                    dst = ring[:, n * SLOT:(n + 1) * SLOT].rearrange("p (k n) -> p k n", k=4)
                    src = w[0, e].rearrange("(k p) n -> p k n", p=P) if isinstance(e, int) else \
                        w[0, bass.ds(e, 1)].rearrange("o (k p) n -> p (o k) n", p=P)
                    sp.dma_start(dst, src[:, 4 * (n % 2):4 * (n % 2) + 4, :]).then_inc(slot_ld[n], 16)

            def wait_first(n):
                if n == 0:
                    sp.wait_ge(s["pv_ps"], len(groups))
                if n == 4:
                    sp.wait_ge(s["op_ps"], 2 * TT)

            slots(0, wait_first)
            with sp.Fori(1, E) as e:
                slots(e, lambda n: sp.wait_ge(s[["a_ps", "u_ps", "y_ps"][n // 2]], 2 * e - 1 + n % 2))
            sp.wait_ge(s["scat"], 32 * E)
            for t in range(TT):
                sp.dma_start(x[:, t, :], acc_d[t * P:(t + 1) * P, :]).then_inc(s[f"ld_x{t}"], 16)
            for t in range(TT):
                sp.wait_ge(s["fin_ok"], t + 1)
                dst = y_sample[0, t * P:(t + 1) * P, :] if t < 4 else y_prompt[0]
                sp.dma_start(dst, x[:, t, :]).then_inc(s["out_y"], 16)
            sp.wait_ge(s["out_y"], 16 * TT)
            sp.wait_ge(s["out_kv"], 32)

        @block.tensor
        def _(pe):
            mm, tr = nc.tensor.matmul, nc.tensor.transpose
            pe.wait_ge(s["ld_small"], 16 * 12)
            tr(bank(7, 128, 128 + VR), vrow[0:VR, :], ident[0:VR, 0:VR])
            for k in range(CT):
                last = tr(bank(6, 256 + W * k, 256 + W * (k + 1)), cwrow[0:W, k * P:(k + 1) * P], ident[0:W, 0:W])
            last.then_inc(s["vecT_ps"], 1)
            pe.wait_ge(s["ld_cache"], 32)
            for j in range(KC):
                for t in range(2):
                    tr(bank(5, j * CTX + t * P, j * CTX + (t + 1) * P), cachek[:, t, j * P:(j + 1) * P], ident)
            for t in range(2):
                last = tr(bank(4, t * P, (t + 1) * P, DR), cacher[:, t, :], ident)
            last.then_inc(s["tr_ctx"], 1)

            def mod_bank(j):
                return j if j < 4 else 7

            def mod(j):
                if j == 0:
                    pe.wait_ge(s["cact_ok"], 1)
                if j == 4:
                    pe.wait_ge(s["vecT_sb"], 2)
                if j > 4:
                    pe.wait_ge(s["mraw_sb"], j)
                pe.wait_ge(wmod_ld[wm_sem[j]], wm_cnt[j])
                for k in range(KD):
                    q = k % 4
                    last = mm(bank(mod_bank(j), 0, 512, 32 * q + 32, 32 * q), cact[:, k, :], wm_buf[j][:, k, :],
                              start=(k < 4), stop=(k >= 4))
                last.then_inc(s["mod_ps"], 1)

            def mod_turn(j):
                pe.wait_ge(s["mraw_sb"], j + 1)
                if j == 0:
                    pe.wait_ge(s["vecT_sb"], 2)
                if j >= 1:
                    pe.wait_ge(s["mT_sb"], j)
                for m in range(4):
                    last = tr(bank(6, m * P, (m + 1) * P), modr[:, j % 2, m * P:(m + 1) * P], ident)
                last.then_inc(s["mT_ps"], 1)

            def x_turn(k):
                b = hT_bank[k]
                for t in range(TT):
                    o = bank(b, t * P, (t + 1) * P) if t < 4 else bank(b + 1, 0, P)
                    last = tr(o, x[:, t, k * P:(k + 1) * P], ident)
                last.then_inc(s["hT_ps"], 1)

            for j in range(3):
                mod(j)
                if j >= 1:
                    mod_turn(j - 1)
            mod_turn(2)
            pe.wait_ge(s["xn_ok"], TT)
            pe.wait_ge(s["ctx_sb"], 2)
            x_turn(0)
            x_turn(1)
            mod(3)
            mod_turn(3)
            pe.wait_ge(s["mT_sb"], 4)
            for k in range(2, KD):
                if k >= 4:
                    before = max(i for i in range(k) if hT_bank[i] == hT_bank[k])
                    pe.wait_ge(s["hTd"], before + 1)
                x_turn(k)

            def q_stat(i):
                pe.wait_ge(s["sq_ok"], i + 1)
                if i == 0:
                    pe.wait_ge(s["ctx_sb"], 2)
                q = i % 4
                for n in range(2):
                    last = mm(bank(4 + n, 0, HN, 32 * q + 32, 32 * q), ones[:, 0:32], sq[:, i % 2, n * HN:(n + 1) * HN],
                              start=(i < 4), stop=(i + 4 >= QC))
                last.then_inc(s["qst"], 1)

            for i in range(len(tiles_in)):
                if i >= 2:
                    pe.wait_ge(s["ev"], i - 1)
                kind, j = tiles_in[i]
                w_view, M, _, (w_hi, w_lo) = tile_in(i)
                for n, (w, h) in enumerate(((w_hi, h_hi), (w_lo, h_hi), (w_hi, h_lo))):
                    if n < 2:
                        pe.wait_ge(s[["whi_ok", "wlo_ok"][n]], i + 1)
                    for lo, hi, b in ((0, HN, 2 * (i % 2)), (HN, NT, 2 * (i % 2) + 1)):
                        for k in range(KD):
                            if i == 0 and n == 0 and lo == 0:
                                pe.wait_ge(s["hTa"], k + 1)
                                if k == 2:
                                    pe.wait_ge(s["hTd"], 2)
                            if i == 0 and n == 2 and lo == 0 and k % 4 == 0:
                                pe.wait_ge(s[["hlo_p", "hlo_d"][k // 4]], 4)
                            last = mm(bank(b, 0, hi - lo, M), w[:, k, :], h[:, k, lo:hi],
                                      start=(n == 0 and k == 0), stop=(n == 2 and k == KD - 1), skip_group_check=True)
                last.then_inc(s["pj"], 1)
                if i % 2 == 1:
                    mod(4 + i // 2)
                elif i >= 2:
                    mod_turn(3 + i // 2)
                if kind == "q" and j >= 2:
                    q_stat(j - 2)
            q_stat(QC - 2)
            q_stat(QC - 1)
            pe.wait_ge(s["kv_sq"], 3)
            pe.wait_ge(s["mT_sb"], HALF)
            pe.wait_ge(s["mraw_sb"], HALF)
            for n in range(2):
                last = mm(bank(6 + n, 0, HN), ones, sq[:, 2, n * HN:(n + 1) * HN], start=True, stop=True)
            last.then_inc(s["kvs"], 1)
            pe.wait_ge(s["qrow_ok"], 2)
            for t in range(TT):
                last = mm(bank(4, t, t + 1), q_rows[:, t * P:(t + 1) * P], ones[:, 0:1], start=True, stop=True)
            last.then_inc(s["qcol"], 1)

            pe.wait_ge(s["wq_ok"], QC)
            for i in range(6):
                n = 17 + i
                pe.wait_ge(s["ev"], n - 1)
                for lo, hi, b in ((0, HN, 2 * (n % 2)), (HN, NT, 2 * (n % 2) + 1)):
                    for k in range(QC):
                        w = wq[:, k, i * P:(i + 1) * P]
                        last = mm(bank(b, 0, hi - lo), w, qlat[:, k, lo:hi], start=(k == 0), stop=(k == QC - 1))
                last.then_inc(s["pj"], 1)
                if i >= 2:
                    g = i - 2
                    if g == 0:
                        pe.wait_ge(s["qrow_ok"], 2)
                        pe.wait_ge(s["kvs_r"], 2)
                        pe.wait_ge(s["qs_s"], 1)
                    pe.wait_ge(s["diag_ok"], g + 1)
                    mm(bank(4 + g), ones, diag[:, g % 2, :, :].rearrange("p k n -> p (k n)"),
                       start=True, stop=True).then_inc(s["g1_ps"], 1)
            pe.wait_ge(s["g1_sb"], 4)
            mm(bank(5, 0, NS, DR), rotm[0:DR, 0:DR], kr[0:DR, CTX:KS], start=True, stop=True).then_inc(s["rot"], 1)
            pe.wait_ge(s["ev"], 22)
            mm(bank(6), rotm, qr[:, 0, 0:NS], start=True, stop=True).then_inc(s["rot"], 1)
            pe.wait_ge(s["rk_step"], 2)
            pe.wait_ge(s["ev"], 23)
            mm(bank(5), rotm, qr[:, 1, 0:NS], start=True, stop=True).then_inc(s["rot"], 1)
            pe.wait_ge(s["conv_done"], CT)
            for k in range(CT):
                mm(bank(4, 0, CH), ones, mixC[:, k, 0:CH], start=(k == 0), stop=(k == CT - 1))
                last = mm(bank(7, 0, CW - CH), ones, mixC[:, k, CH:CW], start=(k == 0), stop=(k == CT - 1))
            last.then_inc(s["ln_mean"], 1)
            pe.wait_ge(s["ckv_ok"], KC)
            pe.wait_ge(s["ld_wkv"], 32 * KC)
            for i in range(4):
                n = 23 + i
                pe.wait_ge(s["ev"], n - 1)
                for lo, hi, b in ((0, HK, 2 * (n % 2)), (HK, NK, 2 * (n % 2) + 1)):
                    for k in range(KC):
                        last = mm(bank(b, 0, hi - lo), wkv[:, k, i * P:(i + 1) * P], ckvT[:, k, lo:hi],
                                  start=(k == 0), stop=(k == KC - 1))
                last.then_inc(s["pj"], 1)
            pe.wait_ge(s["rq_step"], 6)
            pe.wait_ge(s["ln_sq"], CT)
            for k in range(CT):
                mm(bank(5, 0, CH), ones, dsq[:, k, 0:CH], start=(k == 0), stop=(k == CT - 1))
                last = mm(bank(6, 0, CW - CH), ones, dsq[:, k, CH:CW], start=(k == 0), stop=(k == CT - 1))
            last.then_inc(s["ln_var"], 1)
            for t in range(7):
                n = 27 + t
                pe.wait_ge(s["ev"], n - 1)
                for k in range(KC):
                    last = mm(bank(2 * (n % 2)), ckvT[:, k, t * P:(t + 1) * P], wkv[:, k, H * DN:],
                              start=(k == 0), stop=(k == KC - 1))
                last.then_inc(s["pj"], 1)
            pe.wait_ge(s["ln_d"], CT)
            for j in range(KC):
                tr(bank(4, j * P, (j + 1) * P), ckvT[:, j, KS:NK], ident)
            tr(bank(4, KR, KR + DR), kr[0:DR, KS:NK], ident[0:DR, 0:DR]).then_inc(s["nk_ps"], 1)
            def scores(u):
                h, t, _ = steps[u]
                if u >= 2:
                    pe.wait_ge(s["exp_ok"], u - 1)
                b = 2 * (u % 2)
                q = QT[0:DQK, h, t * P:(t + 1) * P]
                if t < 4:
                    mm(bank(b, 0, KS // 2), q, kT[0:DQK, h, 0:KS // 2], start=True, stop=True)
                    mm(bank(b + 1, 0, KS // 2), q, kT[0:DQK, h, KS // 2:KS], start=True, stop=True).then_inc(s["s_ps"], 1)
                else:
                    mm(bank(b, 0, NP), q, kT[0:DQK, h, KS:NK], start=True, stop=True).then_inc(s["s_ps"], 1)

            def weighted_values(n, part, parts):
                hp, ts = groups[n]
                w = P * len(ts)
                kts = range(6) if ts[0] < 4 else [6]
                each = (len(kts) + parts - 1) // parts
                mine = kts[part * each:(part + 1) * each]
                if part == 0:
                    pe.wait_ge(s["pta"], steps_before(n + 1))
                    pe.wait_ge(s["ptd"], sample_steps(steps_before(n + 1)))
                    if n >= 2:
                        pe.wait_ge(s["ata"], n - 1)
                for kt in mine:
                    for a in range(2):
                        h = 2 * hp + a
                        last = mm(bank(6 + n % 2, 0, w, 64 * a + 64, 64 * a), V[:, kt, h * DV:(h + 1) * DV],
                                  PT[n % 2][:, kt % 6, a, 0:w], start=(kt == kts[0]), stop=(kt == kts[-1]),
                                  skip_group_check=True)
                if mine and mine[-1] == kts[-1]:
                    last.then_inc(s["pv_ps"], 1)

            pe.wait_ge(s["ev"], 34)
            pe.wait_ge(s["rope_a"], 8)
            pe.wait_ge(s["kT_rope"], 1)
            pe.wait_ge(s["ln_s"], 2)
            pe.wait_ge(s["nk_sb"], 1)
            scores(0)
            scores(1)
            for u in range(U):
                h, t, n = steps[u]
                if u + 2 < U:
                    scores(u + 2)
                pe.wait_ge(s["pn_ok"], u + 1)
                if u >= 1:
                    pe.wait_ge(s["pta"], u)
                    pe.wait_ge(s["ptd"], sample_steps(u))
                for kt in range(6) if t < 4 else range(1):
                    last = tr(bank(4 + kt // 3, kt % 3 * P, (kt % 3 + 1) * P), Pb[:, u % 2, kt * P:(kt + 1) * P], ident)
                last.then_inc(s["t_ps"], 1)
                if n >= 1:
                    first = steps_before(n)
                    weighted_values(n - 1, u - first, steps_before(n + 1) - first)
            weighted_values(len(groups) - 1, 0, 1)

            order = [4, 0, 1, 2, 3]

            def out_proj(i, n):
                t = order[i]
                if i >= 2:
                    pe.wait_ge(s["g1m"], 2 * (i - 2) + n + 1)
                for k in range(KD):
                    if n == 0 and k == 4 and i < 2:
                        pe.wait_ge(s["ln_out"], CT * (i + 1))
                    o = CP0 if t == 4 else t * P
                    m = mixA[:, k, t * P:(t + 1) * P] if k < 4 else mixC[:, k - 4, o:o + P]
                    last = mm(bank(2 * (i % 2) + n), m, wout[:, k, n * 512:(n + 1) * 512],
                              start=(k == 0), stop=(k == KD - 1))
                    if n == 0 and k == 1 and i >= 2:
                        aff_transpose(i - 2)
                last.then_inc(s["op_ps"], 1)

            def x_to_features(i):
                pe.wait_ge(s["x1n"], i + 1)
                if i >= 1:
                    pe.wait_ge(s["h2a"], 4 * i)
                    pe.wait_ge(s["h2d"], 4 * i)
                for k in range(KD):
                    last = tr(bank(4 + k // 4, (k % 4) * P, (k % 4 + 1) * P), xn2[:, i % 2, k * P:(k + 1) * P], ident)
                last.then_inc(s["xt_ps"], 1)

            def router(i):
                pe.wait_ge(s["h2a"], 4 * (i + 1))
                pe.wait_ge(s["h2d"], 4 * (i + 1))
                if i >= 1:
                    pe.wait_ge(s["lexp"], i)
                for k in range(KD):
                    last = mm(bank(6, 0, E), h2T[:, i % 2, k, :], wr[:, k, :], start=(k == 0), stop=(k == KD - 1))
                last.then_inc(s["lg_ps"], 1)

            def aff_transpose(i):
                pe.wait_ge(s["affn_ok"], i + 1)
                if i >= 1:
                    pe.wait_ge(s["affT_ok"], i)
                tr(bank(7, 0, P, E), affn[:, i % 2, :], ident).then_inc(s["aff_ps"], 1)

            pe.wait_ge(s["ata"], len(groups))
            pe.wait_ge(s["ld_wout"], 16)
            pe.wait_ge(s["ld_router"], 16)
            for i in range(TT):
                out_proj(i, 0)
                if i >= 1:
                    x_to_features(i - 1)
                out_proj(i, 1)
                if i >= 1:
                    router(i - 1)
            aff_transpose(3)
            x_to_features(4)
            router(4)
            aff_transpose(4)
            pe.wait_ge(s["g1m"], 2 * TT)
            for n in range(4):
                pe.wait_ge(s["diag_ok"], 5 + n)
                d = diag[:, n % 2, :, :].rearrange("p k n -> p (k n)")
                if n < 2:
                    last = mm(bank(0, 0, SW, CS * (n + 1), CS * n), ones[:, 0:CS], d, start=True, stop=True)
                else:
                    for q in range(2):
                        o = CPT * (2 * (n - 2) + q)
                        last = mm(bank(1, 0, PW, o + CPT, o), ones[:, 0:CPT], d[:, q * PW:(q + 1) * PW],
                                  start=True, stop=True)
                last.then_inc(s["g2_ps"], 1)
            pe.wait_ge(s["sel"], 5)
            for g in range(2):
                tr(bank(5, g * E, (g + 1) * E), rows[:, g, :], ident[0:E, 0:E])
            tr(bank(5, 2 * E, 3 * E), gs_row, ident[0:E, 0:E])
            tr(bank(5, 3 * E, 4 * E), gp_row, ident[0:E, 0:E]).then_inc(s["sel_ps"], 1)
            pe.wait_ge(s["sel_sb"], 2)
            pe.wait_ge(s["g2_sb"], 2)

            def turn(b, g, src):
                cols, tiles, M, width = cuts[g]
                for j in range(width // P):
                    last = tr(bank(b + g, j * P, (j + 1) * P), src[:, cols][:, j * P:(j + 1) * P], ident)
                return last

            def product(m, g, half, src):
                cols, tiles, M, width = cuts[g]
                chunks = width // P
                for k in range(4 * half, 4 * half + 4):
                    piece, j = k // chunks, k % chunks
                    rows_k = src[:, cols][:, j * P + piece * M:j * P + piece * M + M]
                    for q in range(tiles):
                        o = 2 * m * SLOT + k * F + q * width
                        last = mm(bank([0, 2, 6][m] + g, 0, width, M * (q + 1), M * q), rows_k, ring[:, o:o + width],
                                  start=(k == 0), stop=(k == KD - 1), skip_group_check=True)
                return last

            def expert(e, last_one):
                pe.wait_ge(slot_ld[0], e * 16 + 16)
                pe.wait_ge(s["xs_s"], e + 1)
                product(0, 0, 0, xsT)
                pe.wait_ge(s["xs_p"], e + 1)
                product(0, 1, 0, xsT).then_inc(s["a_ps"], 1)
                pe.wait_ge(slot_ld[1], e * 16 + 16)
                product(0, 0, 1, xsT).then_inc(s["a_s"], 1)
                product(0, 1, 1, xsT).then_inc(s["a_ps"], 1)
                pe.wait_ge(slot_ld[2], e * 16 + 16)
                product(1, 0, 0, xsT)
                product(1, 1, 0, xsT).then_inc(s["u_ps"], 1)
                pe.wait_ge(slot_ld[3], e * 16 + 16)
                product(1, 0, 1, xsT).then_inc(s["u_s"], 1)
                product(1, 1, 1, xsT).then_inc(s["u_ps"], 1)
                pe.wait_ge(s["h_s"], e + 1)
                turn(0, 0, eh).then_inc(s["hTs_tr"], 1)
                if not last_one:
                    pe.wait_ge(s["gath"], e * 32 + 64)
                    turn(4, 0, xg)
                    turn(4, 1, xg).then_inc(s["xt2_ps"], 1)
                pe.wait_ge(s["h_p"], e + 1)
                turn(0, 1, eh).then_inc(s["hTp_tr"], 1)
                pe.wait_ge(s["yw_ok"], e + 1)
                pe.wait_ge(slot_ld[4], e * 16 + 16)
                pe.wait_ge(s["hTs"], e + 1)
                product(2, 0, 0, ehT)
                pe.wait_ge(s["hTp"], e + 1)
                product(2, 1, 0, ehT).then_inc(s["y_ps"], 1)
                pe.wait_ge(slot_ld[5], e * 16 + 16)
                product(2, 0, 1, ehT)
                product(2, 1, 1, ehT).then_inc(s["y_ps"], 1)

            pe.wait_ge(s["gath"], 32)
            turn(4, 0, xg)
            turn(4, 1, xg).then_inc(s["xt2_ps"], 1)
            with pe.Fori(0, E - 1) as e:
                expert(e, False)
            expert(E - 1, True)

        @block.scalar
        def _(act):
            A = nc.scalar.activation
            act.dma_start(tab[:, 0:384], tables[:, 0:384]).then_inc(s["ld_small"], 16)
            rows = [(V_C, c[0], 8), (V_CCTX, c_ctx, 8), (V_AG, attn_norm_g[0], 8), (V_FG, ffn_norm_g[0], 8),
                    (V_QG, q_norm_g[0], 6), (V_KG, kv_norm_g[0], 2), (V_CB, conv_b[0], 4), (V_LG, conv_ln_g[0], 4),
                    (V_LB, conv_ln_b[0], 4), (V_BM, b_mod[0], 48)]
            for r, v, n in rows:
                act.dma_start(vrow[r:r + n, :], v.rearrange("(r n) -> r n", n=P)).then_inc(s["ld_small"], 16)
            act.dma_start(cwrow[0:W, :], conv_w[0]).then_inc(s["ld_small"], 16)
            act.dma_start(cachek, cache_ckv[0, 0].rearrange("(t p) n -> p t n", p=P)).then_inc(s["ld_cache"], 16)
            act.dma_start(cacher, cache_krope[0, 0].rearrange("(t p) n -> p t n", p=P)).then_inc(s["ld_cache"], 16)
            act.dma_start(tab[:, 384:1408], tables[:, 384:1408]).then_inc(s["ld_angles"], 16)
            act.dma_start(wr, w_router[0].rearrange("(k p) n -> p k n", p=P)).then_inc(s["ld_router"], 16)
            act.wait_ge(s["vecT_sb"], 1)
            act.wait_ge(s["cact_z"], 1)
            A(cact[:, :, 0:2], vec[:, V_C:V_C + 16].rearrange("p (g k) -> p k g", g=2), ACT.Silu).then_inc(s["cact_ok"], 1)

            def mod_out(j):
                act.wait_ge(s["mod_ps"], j + 1)
                if j >= 2:
                    act.wait_ge(s["mT_ps"], j - 1)
                A(modr[:, j % 2, :], bank(j if j < 4 else 7), ACT.Copy).then_inc(s["mraw_sb"], 1)

            def mod_cols(j):
                act.wait_ge(s["mT_ps"], j + 1)
                A(modt[:, 4 * j:4 * j + 4, :].rearrange("p m (q g) -> p m q g", q=4),
                  bank(6).rearrange("p (m q r) -> p m q r", m=4, q=4)[:, :, :, 0:2], ACT.Copy).then_inc(s["mT_sb"], 1)

            for t in range(TT):
                act.wait_ge(s[f"ld_x{t}"], 16)
                A(mixC[:, 0:2, 0:512], x[:, t, :].rearrange("p (a n) -> p a n", a=2), ACT.Square,
                  accum_out=ss[:, t:t + 1]).then_inc(s["sqx"], 1)
                act.wait_ge(s["sqx"], t + 1)
            act.wait_ge(s["gcol_ok"], 1)
            A(rs[:, 0:TT], ss[:, 0:TT], ACT.Sqrt, scale=1.0 / D, bias=ss[:, 5:6]).then_inc(s["rstdx_s"], 1)
            for j in range(4):
                mod_out(j)
                if j >= 1:
                    mod_cols(j - 1)
            mod_cols(3)
            def w_high(i):
                src, M, done, (w_hi, w_lo) = tile_in(i)
                act.wait_ge(s[done], 16)
                if i >= 2:
                    act.wait_ge(s["pj"], i - 1)
                A(w_hi, src, ACT.Copy).then_inc(s["whi_ok"], 1)

            w_high(0)
            for k in range(KD):
                act.wait_ge(s["hTd"], k + 1)
                A(h_hi[:, k, :], h_full[k], ACT.Copy).then_inc(s["hTa"], 1)
            w_high(1)
            for i, (kind, j) in enumerate(tiles_in):
                b = 2 * (i % 2)
                act.wait_ge(s["pj"], i + 1)
                if kind == "gate":
                    if j >= 2:
                        act.wait_ge(s["glu_mul"], j - 1)
                    A(sq[:, j % 2, 0:HN], bank(b, 0, HN), ACT.Sigmoid)
                    A(sq[:, j % 2, HN:NT], bank(b + 1, 0, HN), ACT.Sigmoid).then_inc(s["ev"], 1)
                elif kind == "value":
                    if j == 0:
                        act.wait_ge(s["glu_pad"], 1)
                    A(gluv[:, j, PAD:PAD + HN], bank(b, 0, HN), ACT.Copy)
                    A(gluv[:, j, PAD + HN:PAD + NS], bank(b + 1, 0, NS - HN), ACT.Copy)
                    A(gluv[:, j, 2 * PAD + NS:2 * PAD + NT], bank(b + 1, NS - HN, HN), ACT.Copy).then_inc(s["ev"], 1)
                else:
                    M = DR if kind == "kr" else P
                    dst = {"q": qlat[:, j, :], "kv": ckvT[:, j % KC, CTX:NK], "kr": kr[0:DR, CTX:NK]}[kind]
                    A(dst[:, 0:HN], bank(b, 0, HN, M), ACT.Copy)
                    A(dst[:, HN:NT], bank(b + 1, 0, HN, M), ACT.Copy).then_inc(s["ev"], 1)
                if i + 2 < len(tiles_in):
                    w_high(i + 2)
                if i % 2 == 1:
                    mod_out(4 + i // 2)
                elif i >= 2:
                    mod_cols(3 + i // 2)
                if kind == "q" and j >= QC // 2:
                    act.wait_ge(s["ld_wq"], 32 * QC)
                    for k in (2 * j - QC, 2 * j - QC + 1):
                        A(wq[:, k, :], wq[:, k, :], ACT.Identity, scale=vec[:, V_QG + k:V_QG + k + 1]).then_inc(s["wq_ok"], 1)
            act.wait_ge(s["qst"], QC)
            act.wait_ge(s["mT_ps"], HALF)
            for n in range(2):
                A(q_rows[:, n * HN:(n + 1) * HN], bank(4 + n, 0, HN), ACT.Copy).then_inc(s["qrow_ok"], 1)
            act.wait_ge(s["kvs"], 1)
            for n in range(2):
                A(sq[:, 2, n * HN:(n + 1) * HN], bank(6 + n, 0, HN), ACT.Sqrt, scale=1.0 / KR,
                  bias=ss[:, 5:6]).then_inc(s["kvs_r"], 1)
            act.wait_ge(s["qcol"], 1)
            A(rq[:, 0:TT], bank(4, 0, TT), ACT.Sqrt, scale=1.0 / (32 * QR), bias=ss[:, 5:6]).then_inc(s["qs_s"], 1)
            for i in range(6):
                b = 2 * ((17 + i) % 2)
                act.wait_ge(s["pj"], 18 + i)
                for n in range(2):
                    cols = slice(n * HN, (n + 1) * HN)
                    if i < 4:
                        for a in range(2):
                            last = A(QT[0:DN, 2 * i + a, cols], bank(b + n, 0, HN, DN * (a + 1), DN * a), ACT.Copy)
                    else:
                        last = A(qr[:, i - 4, cols], bank(b + n, 0, HN), ACT.Copy)
                last.then_inc(s["ev"], 1)
                if i >= 2:
                    g = i - 2
                    if g == 0:
                        act.wait_ge(s["conv_done"], CT)
                    act.wait_ge(s["g1_ps"], g + 1)
                    A(g1b[:, g // 2, (g % 2) * 512:(g % 2 + 1) * 512], bank(4 + g), ACT.Copy).then_inc(s["g1_sb"], 1)
            act.wait_ge(s["kvr"], 1)
            act.wait_ge(s["ckv_ok"], KC)
            for i in range(4):
                b = 2 * ((23 + i) % 2)
                act.wait_ge(s["pj"], 24 + i)
                for a in range(2):
                    A(kT[0:DN, 2 * i + a, 0:HK], bank(b, 0, HK, DN * (a + 1), DN * a), ACT.Copy)
                    last = A(kT[0:DN, 2 * i + a, HK:NK], bank(b + 1, 0, HK, DN * (a + 1), DN * a), ACT.Copy)
                last.then_inc(s["ev"], 1)
            act.wait_ge(s["ln_var"], 1)
            A(rv[:, 0:CH], bank(5, 0, CH), ACT.Sqrt, scale=1.0 / CC, bias=ss[:, 5:6]).then_inc(s["ln_s"], 1)
            A(rv[:, CH:CW], bank(6, 0, CW - CH), ACT.Sqrt, scale=1.0 / CC, bias=ss[:, 5:6]).then_inc(s["ln_s"], 1)
            for t in range(8):
                if t < 7:
                    act.wait_ge(s["pj"], 28 + t)
                    A(V[:, t, :], bank(2 * ((27 + t) % 2)), ACT.Copy).then_inc(s["ev"], 1)
                r, j = t // 4, t % 4
                act.wait_ge(s["rq_step"], 3 * (r + 1))
                A(QT[DN:DQK, t, :], qr[DR * j:DR * (j + 1), r, :], ACT.Copy).then_inc(s["rope_a"], 1)
            def exps(u):
                h, t, _ = steps[u]
                act.wait_ge(s["nb_ok"], u + 1)
                if u >= 2:
                    act.wait_ge(s["t_ps"], u - 1)
                b = 2 * (u % 2)
                if t < 4:
                    out, src = Pb[:, u % 2, :].rearrange("p (a n) -> p a n", a=2), two_banks(b, KS // 2)
                else:
                    out, src = Pb[:, u % 2, 0:NP], bank(b, 0, NP)
                A(out, src, ACT.Exp, scale=rq[:, t:t + 1], bias=nb[:, u % 2:u % 2 + 1],
                  accum_out=psm[:, u % 2:u % 2 + 1]).then_inc(s["exp_ok"], 1)

            def attn_out(n):
                hp, ts = groups[n]
                act.wait_ge(s["pv_ps"], n + 1)
                w = P * len(ts)
                A(mixA[:, hp, ts[0] * P:ts[0] * P + w], bank(6 + n % 2, 0, w), ACT.Copy).then_inc(s["ata"], 1)

            exps(0)
            for u in range(U):
                h, t, n = steps[u]
                if u + 1 < U:
                    exps(u + 1)
                act.wait_ge(s["t_ps"], u + 1)
                if n >= 2:
                    act.wait_ge(s["pv_ps"], n - 1)
                w = 3 if t < 4 else 1
                A(PT[n % 2][:, 0:w, h % 2, t % 2 * P:(t % 2 + 1) * P], bank(4, 0, w * P).rearrange("p (k n) -> p k n", k=w),
                  ACT.Copy).then_inc(s["pta"], 1)
                if n >= 2 and u == steps_before(n):
                    attn_out(n - 2)
            attn_out(len(groups) - 2)
            attn_out(len(groups) - 1)
            for lo, hi in ((CP0, CW), (0, NS)):
                for k in range(CT):
                    act.wait_ge(s["ln_n"], k + 1)
                    A(mixC[:, k, lo:hi], mixC[:, k, lo:hi], ACT.Silu, scale=vec[:, V_LG + k:V_LG + k + 1],
                      bias=vec[:, V_LB + k:V_LB + k + 1]).then_inc(s["ln_out"], 1)

            order = [4, 0, 1, 2, 3]

            def squares(i, n):
                t = order[i]
                act.wait_ge(s["x1_ok"], 2 * i + n + 1)
                if i == 0 and n == 0:
                    act.wait_ge(s["t_ps"], U)
                c = slice(n * 512, (n + 1) * 512)
                A(g1b_junk[:, c], x[:, t, c], ACT.Square, accum_out=ss2[:, n, t:t + 1]).then_inc(s["x1sq"], 1)

            def root(i):
                t = order[i]
                act.wait_ge(s["x1sq"], 2 * i + 2)
                act.wait_ge(s["x1h"], i + 1)
                A(rs[:, t:t + 1], ss2[:, 1, t:t + 1], ACT.Sqrt, scale=1.0 / D, bias=sse[:, t:t + 1]).then_inc(s["x1s"], 1)

            def out(i):
                t = order[i]
                act.dma_start(acc_d[t * P:(t + 1) * P, :], x[:, t, :]).then_inc(s["out_x1"], 16)
                act.wait_ge(s["x1n"], i + 1)
                act.dma_start(hn_d[t * P:(t + 1) * P, :], xn2[:, i % 2, :]).then_inc(s[f"out_hn{i}"], 16)

            def h2(i):
                g = 1 if order[i] == 4 else 0
                act.wait_ge(s["xt_ps"], i + 1)
                if i >= 2:
                    act.wait_ge(s["lg_ps"], i - 1)
                for k in range(4):
                    A(h2T[:, i % 2, k, :], bank(4, k * P, (k + 1) * P), ACT.Identity, scale=A2[:, k, g:g + 1],
                      bias=modc[:, 24 + k, g:g + 1]).then_inc(s["h2a"], 1)

            def rexp(i):
                act.wait_ge(s["lmax"], i + 1)
                if i >= 2:
                    act.wait_ge(s["affn_ok"], i - 1)
                A(aff[:, i % 2, :], bank(6, 0, E), ACT.Exp, bias=sm[:, i % 2:i % 2 + 1],
                  accum_out=sm[:, 2 + i % 2:3 + i % 2]).then_inc(s["lexp"], 1)

            g1b_junk = wikr[:, 0:D]
            for i in range(TT):
                squares(i, 0)
                if i >= 1:
                    h2(i - 1)
                squares(i, 1)
                root(i)
                if i >= 1:
                    rexp(i - 1)
                out(i)
            h2(4)
            rexp(4)
            act.wait_ge(s["g2_ps"], 4)
            for g in range(2):
                cols, width = cuts[g][0], cuts[g][3]
                A(G2r[:, cols], bank(g, 0, width), ACT.Copy).then_inc(s["g2_sb"], 1)

            def expert(e):
                for g, ready, n, done in ((0, "a_s", 1, "sil_s"), (1, "a_ps", 2, "sil_p")):
                    act.wait_ge(s[ready], n * e + n)
                    A(esil[:, cuts[g][0]], bank(g, 0, cuts[g][3]), ACT.Silu).then_inc(s[done], 1)
                for g, ready, done in ((0, "hTs_tr", "hTs"), (1, "hTp_tr", "hTp")):
                    act.wait_ge(s[ready], e + 1)
                    A(ehT[:, cuts[g][0]], bank(g, 0, cuts[g][3]), ACT.Copy).then_inc(s[done], 1)

            with act.Fori(0, E) as e:
                expert(e)
            for t in range(TT):
                act.wait_ge(s[f"ld_x{t}"], 48)
                A(g1b_junk, x[:, t, :], ACT.Square, accum_out=ss[:, t:t + 1]).then_inc(s["x1sq"], 1)
                act.wait_ge(s["x1sq"], 2 * TT + t + 1)
                A(rs[:, t:t + 1], ss[:, t:t + 1], ACT.Sqrt, scale=1.0 / D, bias=ss[:, 5:6]).then_inc(s["x1s"], 1)

        @block.vector
        def _(dve):
            v = nc.vector
            v.memset(ss[:, 5:6], EPS).then_inc(s["gcol_ok"], 1)
            dve.wait_ge(s["vecT_ps"], 1)
            v.tensor_copy(vec[:, :], bank(7, 128, 128 + VR)).then_inc(s["vecT_sb"], 1)
            v.tensor_copy(cw, bank(6, 256, 256 + CT * W).rearrange("p (c w) -> p c w", c=CT)).then_inc(s["vecT_sb"], 1)
            dve.wait_ge(s["tr_ctx"], 1)
            v.tensor_copy(kr[0:DR, 0:CTX], bank(4, 0, CTX, DR)).then_inc(s["ctx_sb"], 1)
            v.tensor_copy(ckvT[:, :, 0:CTX], bank(5).rearrange("p (k n) -> p k n", k=KC)).then_inc(s["ctx_sb"], 1)
            dve.wait_ge(s["rstdx_s"], 1)
            v.reciprocal(rs[:, 0:TT], rs[:, 0:TT]).then_inc(s["rstdx"], 1)
            dve.wait_ge(s["rstdx"], 1)
            for t in range(TT):
                v.tensor_scalar(x[:, t, :], x[:, t, :], rs[:, t:t + 1], None, ALU.mult).then_inc(s["xn_ok"], 1)
            dve.wait_ge(s["mT_sb"], 4)
            v.tensor_reduce(modc[:, 0:16, :], modt[:, 0:16, :].rearrange("p m (q g) -> p m g q", q=4), AX,
                            ALU.add).then_inc(s["red"], 1)
            dve.wait_ge(s["red"], 1)
            v.tensor_tensor(modc[:, 0:16, :], modc[:, 0:16, :],
                            vec[:, V_BM:V_BM + 16].unsqueeze(2).broadcast_to([P, 16, 2]), ALU.add).then_inc(s["mod_sum"], 1)
            dve.wait_ge(s["mod_sum"], 1)
            v.scalar_tensor_tensor(out=A1, in0=modc[:, 8:16, :], scalar=1.0,
                                   in1=vec[:, V_AG:V_AG + 8].unsqueeze(2).broadcast_to([P, 8, 2]),
                                   op0=ALU.add, op1=ALU.mult).then_inc(s["a1_ok"], 1)
            dve.wait_ge(s["a1_ok"], 1)
            for k in range(KD):
                dve.wait_ge(s["hT_ps"], k + 1)
                v.tensor_scalar(h_full[k][:, 0:NS], bank(hT_bank[k]), A1[:, k, 0:1], modc[:, k, 0:1], ALU.mult, ALU.add)
                v.tensor_scalar(h_full[k][:, NS:NT], bank(hT_bank[k] + 1, 0, NP), A1[:, k, 1:2], modc[:, k, 1:2],
                                ALU.mult, ALU.add).then_inc(s["hTd"], 1)
            dve.wait_ge(s["hT_ps"], KD)
            dve.wait_ge(s["hTd"], KD)
            for k in range(4, KD):
                dve.wait_ge(s["hTa"], k + 1)
                v.tensor_tensor(h_lo[:, k, :], h_full[k], h_hi[:, k, :].bitcast(F32), ALU.subtract).then_inc(s["hlo_d"], 1)
            n = 0
            for cc in range(CT):
                dve.wait_ge(s["glu_mul"], cc + 1)
                if cc == 0:
                    dve.wait_ge(s["sqx"], TT)
                for w in range(W):
                    src = gluv[:, cc, w:w + CW]
                    if w == 0:
                        o = v.tensor_scalar(mixC[:, cc, :], src, cw[:, cc, 0:1], vec[:, V_CB + cc:V_CB + cc + 1],
                                            ALU.mult, ALU.add)
                    else:
                        dve.wait_ge(s["conv_ops"], n)
                        o = v.scalar_tensor_tensor(out=mixC[:, cc, :], in0=src, scalar=cw[:, cc, w:w + 1],
                                                   in1=mixC[:, cc, :], op0=ALU.mult, op1=ALU.add)
                    if w < W - 1:
                        o.then_inc(s["conv_ops"], 1)
                        n += 1
                    else:
                        o.then_inc(s["conv_done"], 1)
            dve.wait_ge(s["qs_s"], 1)
            v.reciprocal(rq[:, 0:TT], rq[:, 0:TT]).then_inc(s["qs_r"], 1)
            dve.wait_ge(s["qs_r"], 1)
            v.tensor_scalar(rq[:, 0:TT], rq[:, 0:TT], float(DQK) ** -0.5, None, ALU.mult).then_inc(s["qs_r"], 1)
            dve.wait_ge(s["kvs_r"], 2)
            v.reciprocal(sq[:, 2, :], sq[:, 2, :]).then_inc(s["kvr"], 1)
            dve.wait_ge(s["kvr"], 1)
            for j in range(KC):
                v.scalar_tensor_tensor(out=ckvT[:, j, CTX:NK], in0=ckvT[:, j, CTX:NK], scalar=vec[:, V_KG + j:V_KG + j + 1],
                                       in1=sq[:, 2, :], op0=ALU.mult, op1=ALU.mult).then_inc(s["ckv_ok"], 1)
            dve.wait_ge(s["mT_sb"], HALF)
            v.tensor_reduce(modc[:, 16:48, :], modt[:, 16:48, :].rearrange("p m (q g) -> p m g q", q=4), AX,
                            ALU.add).then_inc(s["red"], 1)
            dve.wait_ge(s["red"], 2)
            v.tensor_tensor(modc[:, 16:48, :], modc[:, 16:48, :],
                            vec[:, V_BM + 16:V_BM + 48].unsqueeze(2).broadcast_to([P, 32, 2]), ALU.add).then_inc(s["mod_sum"], 1)
            dve.wait_ge(s["mod_sum"], 2)
            v.scalar_tensor_tensor(out=A2, in0=modc[:, 32:40, :], scalar=1.0,
                                   in1=vec[:, V_FG:V_FG + 8].unsqueeze(2).broadcast_to([P, 8, 2]),
                                   op0=ALU.add, op1=ALU.mult).then_inc(s["a2_ok"], 1)
            dve.wait_ge(s["ld_angles"], 16)
            dve.wait_ge(s["rot"], 1)
            v.tensor_tensor(kr[0:DR, CTX:KS], kr[0:DR, CTX:KS], cos[0:DR, :], ALU.mult).then_inc(s["rk_step"], 1)
            v.tensor_tensor(rt[0:DR, :], bank(5, 0, NS, DR), sin[0:DR, :], ALU.mult).then_inc(s["rk_step"], 1)
            dve.wait_ge(s["rk_step"], 2)
            v.tensor_tensor(kr[0:DR, CTX:KS], kr[0:DR, CTX:KS], rt[0:DR, :], ALU.add).then_inc(s["rk_step"], 1)
            dve.wait_ge(s["rk_step"], 3)
            dve.wait_ge(s["ckv_ok"], KC)
            v.tensor_copy(kT[DN:DQK, :, :], kr[0:DR, :].unsqueeze(1).broadcast_to([DR, H, NK])).then_inc(s["kT_rope"], 1)
            for r in range(2):
                dve.wait_ge(s["rot"], r + 2)
                v.tensor_tensor(qr[:, r, 0:NS], qr[:, r, 0:NS], cos, ALU.mult).then_inc(s["rq_step"], 1)
                v.tensor_tensor(rt, bank(6 - r), sin, ALU.mult).then_inc(s["rq_step"], 1)
                dve.wait_ge(s["rq_step"], 3 * r + 2)
                v.tensor_tensor(qr[:, r, 0:NS], qr[:, r, 0:NS], rt, ALU.add).then_inc(s["rq_step"], 1)
                dve.wait_ge(s["rq_step"], 3 * r + 3)
            dve.wait_ge(s["ln_mean"], 1)
            for k in range(CT):
                v.scalar_tensor_tensor(out=mixC[:, k, 0:CH], in0=bank(4, 0, CH), scalar=-1.0 / CC,
                                       in1=mixC[:, k, 0:CH], op0=ALU.mult, op1=ALU.add)
                v.scalar_tensor_tensor(out=mixC[:, k, CH:CW], in0=bank(7, 0, CW - CH), scalar=-1.0 / CC,
                                       in1=mixC[:, k, CH:CW], op0=ALU.mult, op1=ALU.add).then_inc(s["ln_d"], 1)
            dve.wait_ge(s["ln_s"], 2)
            v.reciprocal(rv, rv).then_inc(s["ln_r"], 1)
            dve.wait_ge(s["ln_r"], 1)
            dve.wait_ge(s["ln_sq"], CT)
            for k in range(CT):
                v.tensor_tensor(mixC[:, k, :], mixC[:, k, :], rv, ALU.mult).then_inc(s["ln_n"], 1)
            dve.wait_ge(s["nk_ps"], 1)
            v.tensor_copy(ost, bank(4, 0, 288)).then_inc(s["nk_sb"], 1)

            def maxima(u):
                h, t, _ = steps[u]
                dve.wait_ge(s["s_ps"], u + 1)
                if u >= 2:
                    dve.wait_ge(s["exp_ok"], u - 1)
                b = 2 * (u % 2)
                if t < 4:
                    m = v.tensor_reduce(mx[:, u % 2:u % 2 + 1], two_banks(b, KS // 2), mybir.AxisListType.XY, ALU.max)
                else:
                    m = v.reduce_max(mx[:, u % 2:u % 2 + 1], bank(b, 0, NP), AX)
                m.then_inc(s["smax"], 1)
                dve.wait_ge(s["smax"], u + 1)
                v.tensor_scalar(nb[:, u % 2:u % 2 + 1], mx[:, u % 2:u % 2 + 1], rq[:, t:t + 1], -1.0,
                                ALU.mult, ALU.mult).then_inc(s["nb_ok"], 1)

            dve.wait_ge(s["qs_r"], 2)
            maxima(0)
            maxima(1)
            for u in range(U):
                h, t, n = steps[u]
                dve.wait_ge(s["exp_ok"], u + 1)
                v.reciprocal(rin[:, u % 2:u % 2 + 1], psm[:, u % 2:u % 2 + 1]).then_inc(s["rin_ok"], 1)
                dve.wait_ge(s["rin_ok"], u + 1)
                w = KS if t < 4 else NP
                v.tensor_scalar(Pb[:, u % 2, 0:w], Pb[:, u % 2, 0:w], rin[:, u % 2:u % 2 + 1], None,
                                ALU.mult).then_inc(s["pn_ok"], 1)
                if u + 2 < U:
                    maxima(u + 2)
                if t < 4:
                    dve.wait_ge(s["t_ps"], u + 1)
                    if n >= 2:
                        dve.wait_ge(s["pv_ps"], n - 1)
                    v.tensor_copy(PT[n % 2][:, 3:6, h % 2, t % 2 * P:(t % 2 + 1) * P],
                                  bank(5, 0, 3 * P).rearrange("p (k n) -> p k n", k=3)).then_inc(s["ptd"], 1)

            order = [4, 0, 1, 2, 3]
            dve.wait_ge(s["g1_sb"], 4)

            def residual(i, n):
                t = order[i]
                g = 1 if t == 4 else 0
                c = slice(n * 512, (n + 1) * 512)
                dve.wait_ge(s["op_ps"], 2 * i + n + 1)
                if n == 0:
                    dve.wait_ge(s[f"ld_x{t}"], 32)
                if i >= 1:
                    dve.wait_ge(s["x1_ok"], 2 * (i - 1) + n + 1)
                v.tensor_tensor(gtmp[:, n, :], bank(2 * (i % 2) + n), g1b[:, g, c], ALU.mult).then_inc(s["g1m"], 1)
                dve.wait_ge(s["g1m"], 2 * i + n + 1)
                v.tensor_tensor(x[:, t, c], x[:, t, c], gtmp[:, n, :], ALU.add).then_inc(s["x1_ok"], 1)

            def half_mean(i):
                t = order[i]
                dve.wait_ge(s["x1sq"], 2 * i + 1)
                v.tensor_scalar(sse[:, t:t + 1], ss2[:, 0, t:t + 1], 1.0 / D, EPS, ALU.mult, ALU.add).then_inc(s["x1h"], 1)

            def normalise(i):
                t = order[i]
                dve.wait_ge(s["x1s"], i + 1)
                v.reciprocal(rs[:, t:t + 1], rs[:, t:t + 1]).then_inc(s["x1r"], 1)
                dve.wait_ge(s["x1r"], i + 1)
                if i >= 2:
                    dve.wait_ge(s["xt_ps"], i - 1)
                    dve.wait_ge(s[f"out_hn{i - 2}"], 16)
                dve.wait_ge(s["x1_ok"], 2 * (i + 1))
                v.tensor_scalar(xn2[:, i % 2, :], x[:, t, :], rs[:, t:t + 1], None, ALU.mult).then_inc(s["x1n"], 1)

            def h2(i):
                g = 1 if order[i] == 4 else 0
                dve.wait_ge(s["xt_ps"], i + 1)
                if i >= 2:
                    dve.wait_ge(s["lg_ps"], i - 1)
                for k in range(4, KD):
                    v.tensor_scalar(h2T[:, i % 2, k, :], bank(5, (k - 4) * P, (k - 3) * P), A2[:, k, g:g + 1],
                                    modc[:, 24 + k, g:g + 1], ALU.mult, ALU.add).then_inc(s["h2d"], 1)

            def softmax_in(i):
                dve.wait_ge(s["lg_ps"], i + 1)
                if i >= 2:
                    dve.wait_ge(s["lexp"], i - 1)
                v.tensor_reduce(sm[:, i % 2:i % 2 + 1], bank(6, 0, E), AX, ALU.max, negate=True).then_inc(s["lmax"], 1)

            def softmax_out(i):
                dve.wait_ge(s["lexp"], i + 1)
                v.reciprocal(sm[:, 4 + i % 2:5 + i % 2], sm[:, 2 + i % 2:3 + i % 2]).then_inc(s["lrec"], 1)
                dve.wait_ge(s["lrec"], i + 1)
                if i >= 2:
                    dve.wait_ge(s["aff_ps"], i - 1)
                v.tensor_scalar(affn[:, i % 2, :], aff[:, i % 2, :], sm[:, 4 + i % 2:5 + i % 2], None,
                                ALU.mult).then_inc(s["affn_ok"], 1)

            def aff_out(i):
                t = order[i]
                dve.wait_ge(s["aff_ps"], i + 1)
                v.tensor_copy(affT[:, t * P:(t + 1) * P], bank(7, 0, P, E)).then_inc(s["affT_ok"], 1)

            top = [0]

            def choose(src, values, places, lo, hi):
                for r in range(lo, hi):
                    best = values[:, 8 * r:8 * r + 8]
                    v.max(best, src).then_inc(s["topk"], 1)
                    dve.wait_ge(s["topk"], top[0] + 1)
                    v.max_index(places[:, 8 * r:8 * r + 8], best, src).then_inc(s["topk"], 1)
                    dve.wait_ge(s["topk"], top[0] + 2)
                    v.match_replace(src, best, src, -1.0).then_inc(s["topk"], 1)
                    dve.wait_ge(s["topk"], top[0] + 3)
                    top[0] += 3

            dve.wait_ge(s["a2_ok"], 1)
            for i in range(TT):
                if i >= 2:
                    aff_out(i - 2)
                if i == 4:
                    dve.wait_ge(s["affT_ok"], 3)
                    choose(affT[:, 0:NS // 2], topv, topi, 0, 4)
                residual(i, 0)
                half_mean(i)
                if i >= 1:
                    h2(i - 1)
                if i == 2:
                    dve.wait_ge(s["affT_ok"], 1)
                    choose(affT[:, NS:NT], topv[:, CS:], topi[:, CS:], 0, CP // 8)
                    dve.wait_ge(s["ld_rows"], 16)
                    v.memset(gp_row, 0.0).then_inc(s["sel"], 1)
                    r = rows[:, 1, :].rearrange("p (q n) -> p q n", q=PQ)[:, :, 0:CP]
                    v.scalar_tensor_tensor(out=r, in0=topi[:, CS:CS + CP].unsqueeze(1).broadcast_to([E, PQ, CP]),
                                           scalar=float(PQ), in1=r, op0=ALU.mult, op1=ALU.add).then_inc(s["sel"], 1)
                    dve.wait_ge(s["sel"], 2)
                    v.tensor_copy(gp_row.rearrange("p (q n) -> p q n", q=PQ)[:, :, 0:CP],
                                  topv[:, CS:CS + CP].unsqueeze(1).broadcast_to([E, PQ, CP])).then_inc(s["sel"], 1)
                if i == 4:
                    choose(affT[:, 0:NS // 2], topv, topi, 4, 6)
                residual(i, 1)
                if i >= 1:
                    softmax_in(i - 1)
                normalise(i)
                if i >= 1:
                    softmax_out(i - 1)
            choose(affT[:, 0:NS // 2], topv, topi, 6, 8)
            aff_out(3)
            h2(4)
            softmax_in(4)
            softmax_out(4)
            aff_out(4)
            dve.wait_ge(s["affT_ok"], TT)
            choose(affT[:, NS // 2:NS], topv2, topi2, 0, CS // 8)
            bv, bi = topv2[:, ::-1], topi2[:, ::-1]
            two = lambda a: a.unsqueeze(1).broadcast_to([E, SH, CS])
            v.tensor_tensor(from_a, topv[:, 0:CS], bv, ALU.is_ge).then_inc(s["merge"], 1)
            v.tensor_tensor(gs_row.rearrange("p (h n) -> p h n", h=SH), two(topv[:, 0:CS]), two(bv), ALU.max).then_inc(s["sel"], 1)
            v.tensor_scalar(b_place, bi, float(NS // 2), None, ALU.add).then_inc(s["merge"], 1)
            dve.wait_ge(s["merge"], 2)
            v.scalar_tensor_tensor(out=change, in0=topi[:, 0:CS], scalar=1.0, in1=b_place, op0=ALU.mult,
                                   op1=ALU.subtract).then_inc(s["merge"], 1)
            r = rows[:, 0, :].rearrange("p (h n) -> p h n", h=SH)
            v.scalar_tensor_tensor(out=r, in0=two(b_place), scalar=float(SH), in1=r, op0=ALU.mult,
                                   op1=ALU.add).then_inc(s["merge"], 1)
            dve.wait_ge(s["merge"], 3)
            v.tensor_tensor(change, change, from_a, ALU.mult).then_inc(s["merge"], 1)
            dve.wait_ge(s["merge"], 5)
            v.scalar_tensor_tensor(out=r, in0=two(change), scalar=float(SH), in1=r, op0=ALU.mult,
                                   op1=ALU.add).then_inc(s["sel"], 1)
            dve.wait_ge(s["sel_ps"], 1)
            v.tensor_copy(idxc, bank(5, 0, 2 * E).rearrange("p (g n) -> p g n", g=2)).then_inc(s["sel_sb"], 1)
            v.tensor_copy(gates, bank(5, 2 * E, 4 * E).rearrange("p (g n) -> p g n", g=2)).then_inc(s["sel_sb"], 1)

            def modulate(e):
                dve.wait_ge(s["xt2_ps"], e + 1)
                for g in range(2):
                    cols, width = cuts[g][0], cuts[g][3]
                    v.tensor_tensor(xmod[:, cols], bank(4 + g, 0, width), A2f[:, cols], ALU.mult).then_inc(s["xm1"], 1)
                    dve.wait_ge(s["xm1"], 2 * e + 1 + g)
                    v.tensor_tensor(xsT[:, cols], xmod[:, cols], S2f[:, cols], ALU.add).then_inc(s[["xs_s", "xs_p"][g]], 1)

            def expert(e, last_one):
                for g in range(2):
                    cols, width = cuts[g][0], cuts[g][3]
                    dve.wait_ge(s[["u_s", "u_ps"][g]], (g + 1) * e + g + 1)
                    dve.wait_ge(s[["sil_s", "sil_p"][g]], e + 1)
                    v.tensor_tensor(eh[:, cols], bank(2 + g, 0, width), esil[:, cols], ALU.mult).then_inc(s[["h_s", "h_p"][g]], 1)
                if not last_one:
                    modulate(e + 1)
                dve.wait_ge(s["y_ps"], 2 * e + 2)
                dve.wait_ge(s["yw_free"], e + 1)
                for g in range(2):
                    cols, width = cuts[g][0], cuts[g][3]
                    last = v.scalar_tensor_tensor(out=yw[:, cols], in0=bank(6 + g, 0, width), scalar=gates[:, g, bass.ds(e, 1)],
                                                  in1=G2r[:, cols], op0=ALU.mult, op1=ALU.mult)
                last.then_inc(s["yw_ok"], 1)

            dve.wait_ge(s["g2_sb"], 2)
            v.memset(ss[:, 6:7], 0.0).then_inc(s["yw_ok"], 1)
            dve.wait_ge(s["full_ok"], 4)
            dve.wait_ge(s["out_x1"], 16 * TT)
            modulate(0)
            with dve.Fori(0, E - 1) as e:
                expert(e, False)
            expert(E - 1, True)
            dve.wait_ge(s["ld_fg"], 16)
            for t in range(TT):
                dve.wait_ge(s["x1s"], TT + t + 1)
                v.reciprocal(rs[:, t:t + 1], rs[:, t:t + 1]).then_inc(s["x1r"], 1)
                dve.wait_ge(s["x1r"], TT + t + 1)
                v.scalar_tensor_tensor(out=x[:, t, :], in0=x[:, t, :], scalar=rs[:, t:t + 1], in1=fgb, op0=ALU.mult,
                                       op1=ALU.mult).then_inc(s["fin_ok"], 1)

        @block.gpsimd
        def _(pool):
            g_ = nc.gpsimd
            g_.memset(cact[:, :, :], 0.0).then_inc(s["cact_z"], 1)

            def w_low(i):
                src, M, done, (w_hi, w_lo) = tile_in(i)
                pool.wait_ge(s[done], 16)
                pool.wait_ge(s["whi_ok"], i + 1)
                g_.tensor_tensor(w_lo, src, w_hi.bitcast(F32), ALU.subtract).then_inc(s["wlo_ok"], 1)

            w_low(0)
            pool.wait_ge(s["hT_ps"], KD)
            for k in range(4):
                pool.wait_ge(s["hTa"], k + 1)
                pool.wait_ge(s["hTd"], k + 1)
                g_.tensor_tensor(h_lo[:, k, :], h_full[k], h_hi[:, k, :].bitcast(F32), ALU.subtract).then_inc(s["hlo_p"], 1)
            w_low(1)
            pool.wait_ge(s["hlo_d"], 4)
            pool.wait_ge(s["hlo_p"], 4)
            for o, n in ((0, PAD), (PAD + NS, PAD), (2 * PAD + NT, PAD)):
                last = g_.memset(gluv[:, :, o:o + n], 0.0)
            last.then_inc(s["glu_pad"], 1)
            for i, (kind, j) in enumerate(tiles_in):
                if i + 2 < len(tiles_in):
                    w_low(i + 2)
                if (kind, j) == ("kv", KC - 1):
                    pool.wait_ge(s["ev"], i + 1)
                    kv2 = mixC[:, 1, 0:NT]
                    g_.tensor_tensor(sq[:, 2, :], ckvT[:, 0, CTX:NK], ckvT[:, 0, CTX:NK], ALU.mult).then_inc(s["kv_sq"], 1)
                    g_.tensor_tensor(kv2, ckvT[:, 1, CTX:NK], ckvT[:, 1, CTX:NK], ALU.mult).then_inc(s["kv_sq"], 1)
                    pool.wait_ge(s["kv_sq"], 2)
                    g_.tensor_tensor(sq[:, 2, :], sq[:, 2, :], kv2, ALU.add).then_inc(s["kv_sq"], 1)
                if kind == "value":
                    pool.wait_ge(s["ev"], i + 1)
                    g_.tensor_tensor(gluv[:, j, PAD:PAD + NS], gluv[:, j, PAD:PAD + NS], sq[:, j % 2, 0:NS], ALU.mult)
                    o = 2 * PAD + NS
                    g_.tensor_tensor(gluv[:, j, o:o + NP], gluv[:, j, o:o + NP], sq[:, j % 2, NS:NT],
                                     ALU.mult).then_inc(s["glu_mul"], 1)
                if kind == "q":
                    pool.wait_ge(s["ev"], i + 1)
                    if j == 0:
                        pool.wait_ge(s["glu_mul"], CT)
                    if j >= 2:
                        pool.wait_ge(s["qst"], j - 1)
                    g_.tensor_tensor(sq[:, j % 2, :], qlat[:, j, :], qlat[:, j, :], ALU.mult).then_inc(s["sq_ok"], 1)
            pool.wait_ge(s["a2_ok"], 1)

            def diagonals(n, chunk, g):
                for k in range(4):
                    last = g_.tensor_scalar(diag[:, n % 2, k, :], ident, modc[:, chunk + k, g:g + 1], None, ALU.mult)
                last.then_inc(s["diag_ok"], 1)

            for n in range(4):
                if n >= 2:
                    pool.wait_ge(s["g1_ps"], n - 1)
                diagonals(n, 16 + 4 * (n % 2), n // 2)
            for k in range(CT):
                pool.wait_ge(s["ln_d"], k + 1)
                g_.tensor_tensor(dsq[:, k, :], mixC[:, k, :], mixC[:, k, :], ALU.mult).then_inc(s["ln_sq"], 1)
            pool.wait_ge(s["nk_sb"], 1)
            pool.dma_start(new_ckv[0, 0], ost[:, 0:KR]).then_inc(s["out_kv"], 16)
            pool.dma_start(new_krope[0, 0], ost[:, KR:KR + DR]).then_inc(s["out_kv"], 16)
            pool.wait_ge(s["nk_ps"], 1)
            for g in range(2):
                cols, tiles, M, width = cuts[g]
                for dst, src in ((A2f, A2[:, :, g]), (S2f, modc[:, 24:32, g])):
                    d = dst[:, cols].rearrange("p (j q n) -> p q j n", q=tiles, n=M)
                    f = src.rearrange("p (q j) -> p q j", q=tiles)
                    for q in range(tiles):
                        last = g_.tensor_copy(d[:, q], f[:, q].unsqueeze(2).broadcast_to([P, width // P, M]))
                    last.then_inc(s["full_ok"], 1)
            pool.wait_ge(s["t_ps"], U)
            pool.wait_ge(s["pv_ps"], len(groups))
            pool.wait_ge(s["out_kv"], 32)
            pool.dma_start(fgb, final_norm_g.rearrange("(o n) -> o n", o=1).broadcast_to([P, D])).then_inc(s["ld_fg"], 16)
            pool.wait_ge(s["op_ps"], 2 * TT)
            for n in range(4):
                if n >= 2:
                    pool.wait_ge(s["g2_ps"], n - 1)
                diagonals(n, 40 + 4 * (n % 2), n // 2)

            def gather(e):
                for g in range(2):
                    g_.indirect_dma_start(xg[:, cuts[g][0]], None, hn_cut[g],
                                          bass.IndirectOffsetOnAxis(ap=idxc[:, g, e:e + 1], axis=0)).then_inc(s["gath"], 16)

            def scatter(e):
                pool.wait_ge(s["yw_ok"], e + 2)
                for g in range(2):
                    g_.indirect_dma_start(acc_cut[g], bass.IndirectOffsetOnAxis(ap=idxc[:, g, e:e + 1], axis=0),
                                          yw[:, cuts[g][0]], None, compute_op=ALU.add).then_inc(s["scat"], 16)
                pool.wait_ge(s["scat"], 32 * (e + 1))
                g_.memset(flag[:, :], 0.0).then_inc(s["yw_free"], 1)

            pool.wait_ge(s["sel_sb"], 2)
            for i in range(TT):
                pool.wait_ge(s[f"out_hn{i}"], 16)
            pool.wait_ge(s["out_x1"], 16 * TT)
            pool.wait_ge(s["spare_ok"], 32)
            g_.memset(flag[:, :], 0.0).then_inc(s["yw_free"], 1)
            gather(0)
            for e in range(E):
                if e + 1 < E:
                    pool.wait_ge(s["xt2_ps"], e + 1)
                    gather(e + 1)
                if e >= 1:
                    scatter(e - 1)
            scatter(E - 1)


_INS = ["x_prompt", "x_sample", "cache_ckv", "cache_krope", "c", "c_ctx", "w_mod", "b_mod", "attn_norm_g", "w_in",
        "q_norm_g", "w_q_up", "kv_norm_g", "w_kv_up", "conv_w", "conv_b", "conv_ln_g", "conv_ln_b", "w_out",
        "ffn_norm_g", "w_router", "w_gate", "w_up", "w_down", "final_norm_g"]
_OUTS = [(1, 128, 1024), (1, 512, 1024), (1, 1, 128, 256), (1, 1, 128, 32)]


def _tables():
    import numpy as _np
    t = _np.zeros((128, 1664), _np.float32)
    t[:, 0:128] = _np.eye(128)
    t[:, 128:256] = 1.0
    for m in range(128):
        if m % 16 < 8:
            t[m + 8, 256 + m] = -1.0
        else:
            t[m - 8, 256 + m] = 1.0
    inv = (1.0 / (_np.float32(10000.0) ** (_np.arange(0, 16, 2, dtype=_np.float32) / _np.float32(16)))).astype(_np.float32)
    pos = _np.arange(512)
    f = _np.arange(128) % 32
    where = _np.where(f[:, None] < 16, pos[None, :] // 64, pos[None, :] % 64).astype(_np.float32)
    ang = (where * inv[f % 8][:, None]).astype(_np.float32)
    t[:, 384:896] = _np.cos(ang)
    t[:, 896:1408] = _np.sin(ang)
    t[:, 1408 + 64:1408 + 128] = 1.0
    for q in range(4):
        t[:, 1536 + 32 * q:1536 + 32 * q + 16] = 4 * 512 + q
        t[:, 1536 + 32 * q + 16:1536 + 32 * (q + 1)] = 4 * 640 + 16 * q + _np.arange(16)
    return t


def kernel(**inputs):
    import numpy as _np
    import concourse.bacc as _bacc
    from concourse import mybir as _mybir
    from concourse.bass_utils import run_bass_kernel_spmd as _run

    nc = _bacc.Bacc("TRN2", target_bir_lowering=False, num_devices=1, dynamic_dma_scratch_size=2048)
    arrays, args = {}, []
    for name in _INS:
        a = _np.ascontiguousarray(inputs[name])
        arrays[f"in_{name}_dram"] = a
        args.append(nc.dram_tensor(f"in_{name}_dram", a.shape, _mybir.dt.from_np(a.dtype), kind="ExternalInput").ap())
    arrays["in_tables_dram"] = _tables()
    args.append(nc.dram_tensor("in_tables_dram", (128, 1664), _mybir.dt.float32, kind="ExternalInput").ap())
    for i, shape in enumerate(_OUTS):
        args.append(nc.dram_tensor(f"out_{i}_dram", shape, _mybir.dt.float32, kind="ExternalOutput").ap())
    layer(nc, *args)
    r = _run(nc, [arrays], core_ids=[0])
    return tuple(r.results[0][f"out_{i}_dram"] for i in range(len(_OUTS)))
```
